# Optimizing a Trainium2 kernel written in Bass

```python
import jax
import jax.numpy as jnp
from jax import lax
import numpy as np

D_MODEL = 2048
BATCH = 1
SEQ = 512
DEPTH = 1
DEC_BATCH = 8
DEC_SEQ = 4
PAST_LEN = 4096
PAGE_SIZE = 128

D_MIX = D_MODEL
D_A = D_MIX // 2
D_B = D_MIX - D_A
HEAD_A = 64
H_A = D_A // HEAD_A
R_W = D_A // 16
R_A = D_A // 16
R_G = D_A // 8
C_A = 3 * D_A + R_W + R_A + R_G
C_TOT = C_A + 2 * D_B
RWKV_SPLITS = (D_A, 2 * D_A, 3 * D_A, 3 * D_A + R_W, 3 * D_A + R_W + R_A)
N_LRU_BLOCKS = 16
LRU_BW = D_B // N_LRU_BLOCKS
CONV_W = 4
C_LRU = 8.0
P_HEADS = 8
N_KEYS = 128
N_EXPERTS = N_KEYS * N_KEYS
TOPK = 16
D_Q = 256
D_QH = D_Q // 2
PEER_BLOCK = 128
LN_EPS = 1e-5
GN_EPS = 64e-5
ALPHA = (2 * DEPTH) ** 0.25
BETA = (8 * DEPTH) ** -0.25

kernel_name = 'hymba_rwkv7_rglru_peer_decoder_step'

def _layernorm(x, w, b):
    xf = x.astype(jnp.float32)
    mean = jnp.mean(xf, axis=-1, keepdims=True)
    var = jnp.mean(jnp.square(xf - mean), axis=-1, keepdims=True)
    return ((xf - mean) * lax.rsqrt(var + LN_EPS)).astype(x.dtype) * w + b

def _wkv_step(S, inp):
    r, w, k, v, kk, kka = inp
    sa = jnp.einsum('bhij,bhj->bhi', S, -kk)
    S = S * w[:, :, None, :] + sa[..., None] * kka[:, :, None, :] + v[..., None] * k[:, :, None, :]
    y = jnp.einsum('bhij,bhj->bhi', S, r)
    return S, y

def _lru_step(h, inp):
    a_t, b_t = inp
    h = a_t * h + b_t
    return h, h

def _rwkv_time_mix(p, p_prev, S0, lp):
    B, T, _ = p.shape
    f32 = jnp.float32
    shifted = jnp.concatenate([p_prev[:, None, :], p[:, :-1]], axis=1)
    p = p + (shifted - p) * lp['mu_shift']
    r, k, v, xw, xa, xg = jnp.split(p, RWKV_SPLITS, axis=-1)
    w_log = -jax.nn.softplus(-(lp['w0'] + jnp.tanh(xw) @ lp['w_w2']).astype(f32)) - 0.5
    decay = jnp.exp(-jnp.exp(w_log))
    a = jax.nn.sigmoid(lp['a0'] + xa @ lp['w_a2'])
    g = jax.nn.sigmoid(xg) @ lp['w_g2']

    def heads(t):
        return t.reshape(B, T, H_A, HEAD_A)

    kk = heads(k * lp['k_k']).astype(f32)
    kk = kk / jnp.maximum(jnp.sqrt(jnp.sum(kk * kk, axis=-1, keepdims=True)), 1e-12)
    k = k * (1 + (a - 1) * lp['k_a'])
    r_h, k_h, v_h, a_h = heads(r), heads(k), heads(v), heads(a)
    seq = tuple(jnp.moveaxis(t.astype(f32), 1, 0)
                for t in (r_h, heads(decay), k_h, v_h, kk, kk * a_h.astype(f32)))
    S, y = lax.scan(_wkv_step, S0.astype(f32), seq)
    y = jnp.moveaxis(y, 0, 1)
    mean = jnp.mean(y, axis=-1, keepdims=True)
    var = jnp.mean(jnp.square(y - mean), axis=-1, keepdims=True)
    yn = ((y - mean) * lax.rsqrt(var + GN_EPS)).reshape(B, T, D_A).astype(p.dtype)
    yn = yn * lp['lnx_w'] + lp['lnx_b']
    bonus = (jnp.sum(r_h * k_h * lp['r_k'], axis=-1, keepdims=True) * v_h).reshape(B, T, D_A)
    return (yn + bonus) * g, S.astype(S0.dtype)

def _rglru_mix(xb, gb, conv_buf, h0, lp):
    B, T, _ = xb.shape
    f32 = jnp.float32
    xpad = jnp.concatenate([conv_buf.astype(xb.dtype), xb], axis=1)
    xc = lp['conv_b']
    for j in range(CONV_W):
        xc = xc + xpad[:, j:j + T] * lp['conv_w'][j]
    xh = xc.reshape(B, T, N_LRU_BLOCKS, LRU_BW)
    r = jax.nn.sigmoid(jnp.einsum('btni,nij->btnj', xh, lp['w_gate_a']).reshape(B, T, D_B) + lp['b_gate_a'])
    i = jax.nn.sigmoid(jnp.einsum('btni,nij->btnj', xh, lp['w_gate_i']).reshape(B, T, D_B) + lp['b_gate_i'])
    log_a = (-C_LRU * r * jax.nn.softplus(-lp['lru_lambda'])).astype(f32)
    a = jnp.exp(log_a)
    gated = jnp.sqrt(-jnp.expm1(2.0 * log_a)) * (i * xc).astype(f32)
    hN, hs = lax.scan(_lru_step, h0.astype(f32), (jnp.moveaxis(a, 1, 0), jnp.moveaxis(gated, 1, 0)))
    y = jnp.moveaxis(hs, 0, 1).astype(xb.dtype) * jax.nn.gelu(gb)
    return y, hN.astype(h0.dtype), xpad[:, -(CONV_W - 1):]

def _peer(h, w_q, sub_keys, peer_u, peer_v):
    B, T, D = h.shape
    n = B * T
    nb = -(-n // PEER_BLOCK)
    xt = jnp.pad(h.reshape(n, D), ((0, nb * PEER_BLOCK - n), (0, 0))).reshape(nb, PEER_BLOCK, D)

    def block(xb):
        q = (xb @ w_q).reshape(PEER_BLOCK, P_HEADS, 2, D_QH)
        s1 = jnp.einsum('thd,kd->thk', q[:, :, 0], sub_keys[0]).astype(jnp.float32)
        s2 = jnp.einsum('thd,kd->thk', q[:, :, 1], sub_keys[1]).astype(jnp.float32)
        v1, i1 = lax.top_k(s1, TOPK)
        v2, i2 = lax.top_k(s2, TOPK)
        cand = (v1[..., :, None] + v2[..., None, :]).reshape(PEER_BLOCK, P_HEADS, TOPK * TOPK)
        sv, si = lax.top_k(cand, TOPK)
        e = (jnp.take_along_axis(i1, si // TOPK, axis=-1) * N_KEYS
             + jnp.take_along_axis(i2, si % TOPK, axis=-1))
        gate = jax.nn.softmax(sv, axis=-1).astype(xb.dtype)
        act = jax.nn.gelu(jnp.einsum('thkd,td->thk', peer_u[e], xb))
        return jnp.einsum('thk,thkd->td', gate * act, peer_v[e])

    out = lax.map(block, xt).reshape(nb * PEER_BLOCK, D)[:n]
    return out.reshape(B, T, D)

def _layer(x, c, shift_prev, wkv0, lru0, conv0, lp):
    mod = jax.nn.silu(c) @ lp['w_ada'] + lp['b_ada']
    sh1, sc1, g1, sh2, sc2, g2 = [m[:, None, :] for m in jnp.split(mod, 6, axis=-1)]
    h = x * (1 + sc1) + sh1
    proj = h @ lp['w_in']
    p_prev = shift_prev @ lp['w_in'][:, :C_A]
    ya, wkv = _rwkv_time_mix(proj[..., :C_A], p_prev, wkv0, lp)
    yb, lru, conv = _rglru_mix(proj[..., C_A:C_A + D_B], proj[..., C_A + D_B:], conv0, lru0, lp)
    mix = jnp.concatenate([ya, yb], axis=-1) @ lp['w_out']
    x = _layernorm(ALPHA * x + (1 + g1) * mix, lp['ln1_w'], lp['ln1_b'])
    h2 = x * (1 + sc2) + sh2
    ff = _peer(h2, lp['w_q'], lp['sub_keys'], lp['peer_u'], lp['peer_v'])
    x = _layernorm(ALPHA * x + (1 + g2) * ff, lp['ln2_w'], lp['ln2_b'])
    return x, h[:, -1], wkv, lru, conv

def setup_inputs(seed: int = 0) -> dict:
    key = jax.random.key(seed)
    kit = iter(list(jax.random.split(key, 48)))
    f32 = jnp.float32
    L = DEPTH

    def nrm(shape, scale):
        return jax.random.normal(next(kit), shape, f32) * scale

    def unif(shape, lo, hi):
        return jax.random.uniform(next(kit), shape, f32, lo, hi)

    sig = unif((L, D_B), 0.9, 0.999) ** (1.0 / C_LRU)
    return {
        'x_prompt': nrm((BATCH, SEQ, D_MODEL), 1.0),
        'x_sample': nrm((DEC_BATCH, DEC_SEQ, D_MODEL), 1.0),
        'c_prompt': nrm((BATCH, D_MODEL), 1.0),
        'c_sample': nrm((DEC_BATCH, D_MODEL), 1.0),
        'state_shift': nrm((L, DEC_BATCH, D_MODEL), 1.0),
        'state_wkv': nrm((L, DEC_BATCH, H_A, HEAD_A, HEAD_A), 0.3),
        'state_lru': nrm((L, DEC_BATCH, D_B), 0.5),
        'state_conv': nrm((L, DEC_BATCH, CONV_W - 1, D_B), 1.0),
        'w_ada': nrm((L, D_MODEL, 6 * D_MODEL), 0.3 * D_MODEL ** -0.5),
        'b_ada': nrm((L, 6 * D_MODEL), 0.01),
        'w_in': nrm((L, D_MODEL, C_TOT), D_MODEL ** -0.5),
        'mu_shift': unif((L, C_A), 0.0, 1.0),
        'w0': unif((L, D_A), -5.0, 1.0),
        'w_w2': nrm((L, R_W, D_A), 0.5 * R_W ** -0.5),
        'a0': nrm((L, D_A), 0.1),
        'w_a2': nrm((L, R_A, D_A), 0.5 * R_A ** -0.5),
        'w_g2': nrm((L, R_G, D_A), R_G ** -0.5),
        'k_k': 0.85 + nrm((L, D_A), 0.1),
        'k_a': 1.0 + nrm((L, D_A), 0.1),
        'r_k': nrm((L, H_A, HEAD_A), 0.1),
        'lnx_w': 1.0 + nrm((L, D_A), 0.1),
        'lnx_b': nrm((L, D_A), 0.01),
        'conv_w': nrm((L, CONV_W, D_B), CONV_W ** -0.5),
        'conv_b': nrm((L, D_B), 0.01),
        'w_gate_a': nrm((L, N_LRU_BLOCKS, LRU_BW, LRU_BW), LRU_BW ** -0.5),
        'b_gate_a': nrm((L, D_B), 0.01),
        'w_gate_i': nrm((L, N_LRU_BLOCKS, LRU_BW, LRU_BW), LRU_BW ** -0.5),
        'b_gate_i': nrm((L, D_B), 0.01),
        'lru_lambda': jnp.log(sig) - jnp.log1p(-sig),
        'w_out': nrm((L, D_MIX, D_MODEL), BETA * D_MIX ** -0.5),
        'ln1_w': 1.0 + nrm((L, D_MODEL), 0.1),
        'ln1_b': nrm((L, D_MODEL), 0.01),
        'w_q': nrm((L, D_MODEL, P_HEADS * D_Q), D_MODEL ** -0.5),
        'sub_keys': nrm((L, 2, N_KEYS, D_QH), D_QH ** -0.5),
        'peer_u': nrm((L, N_EXPERTS, D_MODEL), D_MODEL ** -0.5),
        'peer_v': nrm((L, N_EXPERTS, D_MODEL), BETA * P_HEADS ** -0.5),
        'ln2_w': 1.0 + nrm((L, D_MODEL), 0.1),
        'ln2_b': nrm((L, D_MODEL), 0.01),
    }

def reference(x_prompt, x_sample, c_prompt, c_sample, state_shift, state_wkv, state_lru, state_conv,
              w_ada, b_ada, w_in, mu_shift, w0, w_w2, a0, w_a2, w_g2, k_k, k_a, r_k, lnx_w, lnx_b,
              conv_w, conv_b, w_gate_a, b_gate_a, w_gate_i, b_gate_i, lru_lambda, w_out,
              ln1_w, ln1_b, w_q, sub_keys, peer_u, peer_v, ln2_w, ln2_b):
    yp, ys = x_prompt, x_sample
    bp = x_prompt.shape[0]
    p_shift, p_wkv, p_lru, p_conv = [], [], [], []
    s_shift, s_wkv, s_lru, s_conv = [], [], [], []
    for l in range(DEPTH):
        lp = {
            'w_ada': w_ada[l], 'b_ada': b_ada[l], 'w_in': w_in[l], 'mu_shift': mu_shift[l],
            'w0': w0[l], 'w_w2': w_w2[l], 'a0': a0[l], 'w_a2': w_a2[l], 'w_g2': w_g2[l],
            'k_k': k_k[l], 'k_a': k_a[l], 'r_k': r_k[l], 'lnx_w': lnx_w[l], 'lnx_b': lnx_b[l],
            'conv_w': conv_w[l], 'conv_b': conv_b[l], 'w_gate_a': w_gate_a[l], 'b_gate_a': b_gate_a[l],
            'w_gate_i': w_gate_i[l], 'b_gate_i': b_gate_i[l], 'lru_lambda': lru_lambda[l],
            'w_out': w_out[l], 'ln1_w': ln1_w[l], 'ln1_b': ln1_b[l], 'w_q': w_q[l],
            'sub_keys': sub_keys[l], 'peer_u': peer_u[l], 'peer_v': peer_v[l],
            'ln2_w': ln2_w[l], 'ln2_b': ln2_b[l],
        }
        yp, ps, pw, pl, pc = _layer(
            yp, c_prompt,
            jnp.zeros((bp, D_MODEL), yp.dtype),
            jnp.zeros((bp, H_A, HEAD_A, HEAD_A), state_wkv.dtype),
            jnp.zeros((bp, D_B), state_lru.dtype),
            jnp.zeros((bp, CONV_W - 1, D_B), state_conv.dtype),
            lp)
        p_shift.append(ps)
        p_wkv.append(pw)
        p_lru.append(pl)
        p_conv.append(pc)
        ys, ss, sw, sl, sc = _layer(ys, c_sample, state_shift[l], state_wkv[l], state_lru[l], state_conv[l], lp)
        s_shift.append(ss)
        s_wkv.append(sw)
        s_lru.append(sl)
        s_conv.append(sc)
    return (yp, ys, jnp.stack(p_shift), jnp.stack(p_wkv), jnp.stack(p_lru), jnp.stack(p_conv),
            jnp.stack(s_shift), jnp.stack(s_wkv), jnp.stack(s_lru), jnp.stack(s_conv))


_drawn_inputs = setup_inputs


def setup_inputs(seed=0):
    import zlib

    import numpy as np

    out = dict(_drawn_inputs(seed))
    spreads = {}
    factors = {'lnx_b': 23.47, 'b_gate_a': 27.405, 'b_gate_i': 8.0, 'ln1_b': 4.079, 'ln2_b': 5.718}
    for name, (base, spread) in spreads.items():
        noise = np.random.default_rng([zlib.crc32(name.encode()), seed]).standard_normal(out[name].shape)
        drawn = base * np.exp(spread * noise) if base else spread * noise
        out[name] = jnp.asarray(drawn.astype(out[name].dtype))
    for name, factor in factors.items():
        out[name] = (out[name] * factor).astype(out[name].dtype)
    return out
```

```python
import concourse.bass as bass
from concourse import mybir
from concourse.alu_op_type import AluOpType as ALU
from contextlib import ExitStack

F32 = mybir.dt.float32
U32 = mybir.dt.uint32
I32 = mybir.dt.int32
ACT = mybir.ActivationFunctionType
AX = mybir.AxisListType

P = 128
D = 2048
KT = D // P
SEQ = 512
NB, NS = 8, 4
T = SEQ + NB * NS
TH = T // 2
TP = SEQ + NB * (NS + 1)
SP5 = NB * (NS + 1)
W1 = TP + 1
DA = 1024
NPAIR = DA // P
ADA = 6 * KT
CH_CHUNK = 32
NK = 128
HEADS, TOPK = 8, 16
JG = 8
NG = NK // JG
ALPHA = 2.0 ** 0.25
LN_EPS, GN_EPS = 1e-5, 64e-5
EXP_HALF = 0.6065306597126334
C_LRU = 8.0
NEG = -3.0e38

PAR_SIZES = [("mu", 26), ("w0", 8), ("a0", 8), ("k_k", 8), ("k_a", 8), ("r_k", 8), ("lnx_w", 8), ("lnx_b", 8),
             ("conv_w", 32), ("conv_b", 8), ("b_ga", 8), ("b_gi", 8), ("lam", 8),
             ("ln1_w", 16), ("ln1_b", 16), ("ln2_w", 16), ("ln2_b", 16)]
PAR = {}
_at = 0
for _n, _s in PAR_SIZES:
    PAR[_n] = _at
    _at += _s
NPAR = _at


def samples5(ap, lo=1):
    return ap.rearrange("p (b s) -> p b s", s=NS + 1)[:, :, lo:NS + 1]


def samples4(ap):
    return ap.rearrange("p (b s) -> p b s", s=NS)


def bcast(ap, axis, n):
    v = ap.unsqueeze(axis)
    shape = list(v.shape)
    shape[axis] = n
    return v.broadcast_to(shape)


class Mem:

    used = []

    def __init__(self, nc, stack, tag):
        self.nc, self.stack, self.tag = nc, stack, tag

    def sb(self, name, shape, dt=F32):
        return self.stack.enter_context(self.nc.sbuf_tensor(f"{self.tag}_{name}", shape, dt))

    def sem(self, name):
        s = self.stack.enter_context(self.nc.semaphore(f"{self.tag}_{name}"))
        Mem.used.append(s)
        return s

    def sems(self, name, n):
        return [self.sem(f"{name}{i}") for i in range(n)]


def run(phase, nc, io, g):
    with ExitStack() as stack:
        Mem.used = []
        phase(nc, io, g, stack)
        with nc.Block() as block:
            @block.sync
            def _(sp):
                for s in Mem.used:
                    sp.sem_clear(s)


def phase_ada(nc, io, g, stack):
    m = Mem(nc, stack, "ada")
    PS, RING, HT, MOD, PARAM = g["PS"], g["RING"], g["HT"], g["MOD"], g["PARAM"]
    XT = m.sb("XT", [P, KT, T])
    CT = m.sb("CT", [P, KT, 9])
    CS = m.sb("CS", [P, KT, 9])
    BADA = m.sb("BADA", [P, ADA])
    SHT = m.sb("SHT", [P, KT, NB])
    SHO = m.sb("SHO", [P, KT, 9])
    c_in, x_in, b_in, out_sem = m.sem("c_in"), m.sem("x_in"), m.sem("b_in"), m.sem("out")
    w_in = m.sems("w_in", 4)
    tile_done, sig_ready, cs_ready, bank_free, h_ready = (
        m.sem(x) for x in ("tile_done", "sig_ready", "cs_ready", "bank_free", "h_ready"))

    with nc.Block() as block:
        @block.sync
        def _(sp):
            sp.dma_start(CT[:], io["cT"]).then_inc(c_in, 16)
            for k in range(4):
                sp.dma_start(RING[:, k, :], io["w_ada"][k]).then_inc(w_in[k], 16)
            sp.dma_start(BADA[:], io["b_ada"]).then_inc(b_in, 16)
            sp.dma_start(XT[:], io["xT"]).then_inc(x_in, 16)
            sp.dma_start(SHT[:], io["shiftT"]).then_inc(x_in, 16)
            sp.dma_start(PARAM[:], io["par"]).then_inc(x_in, 16)
            with sp.Fori(0, ADA // 4 - 1) as i:
                for k in range(4):
                    sp.wait_ge(tile_done, 4 * i + k + 1)
                    sp.dma_start(RING[:, k, :], io["w_ada"][4 * i + (4 + k)]).then_inc(w_in[k], 16)
            sp.wait_ge(h_ready, 1)
            sp.dma_start(io["shift_out"], SHO[:]).then_inc(out_sem, 16)
            sp.wait_ge(out_sem, 16)

        @block.scalar
        def _(act):
            act.wait_ge(c_in, 16)
            nc.scalar.activation(CS[:], CT[:], ACT.Sigmoid).then_inc(sig_ready, 1)

        @block.tensor
        def _(pe):
            pe.wait_ge(cs_ready, 1)
            with pe.Fori(0, ADA // 16) as i:
                for half in range(2):
                    pe.wait_ge(bank_free, 2 * i + half + 1)
                    for c in range(8):
                        slot = c % 4
                        pe.wait_ge(w_in[slot], 64 * i + (32 * half + 16 * (c // 4) + 16))
                        for k in range(KT):
                            mm = nc.tensor.matmul(PS[:, half, 9 * c:9 * c + 9], RING[:, slot, P * k:P * k + P],
                                                  CS[:, k, :], start=(k == 0), stop=(k == KT - 1))
                        mm.then_inc(tile_done, 1)

        @block.vector
        def _(dve):
            dve.sem_inc(bank_free, 2)
            dve.wait_ge(sig_ready, 1)
            nc.vector.tensor_tensor(CS[:], CS[:], CT[:], ALU.mult).then_inc(cs_ready, 1)
            dve.wait_ge(b_in, 16)
            dve.wait_ge(x_in, 48)
            nc.vector.tensor_copy(HT[:, :, SEQ:TP].rearrange("p k (b s) -> p k b s", s=NS + 1)[:, :, :, 0], SHT[:])
            with dve.Fori(0, ADA // 16) as i:
                for half in range(2):
                    dve.wait_ge(tile_done, 16 * i + 8 * half + 8)
                    nc.vector.tensor_tensor(
                        MOD[:, bass.ds(16 * i + 8 * half, 8), :],
                        PS[:, half, 0:72].rearrange("p (c b) -> p c b", b=9),
                        bcast(BADA[:, bass.ds(16 * i + 8 * half, 8)], 2, 9), ALU.add).then_inc(bank_free, 1)
            dve.drain()
            for a in (1, 4):
                nc.vector.tensor_scalar(MOD[:, KT * a:KT * (a + 2), :], MOD[:, KT * a:KT * (a + 2), :], 1.0, None, ALU.add)
            dve.drain()
            for k in range(KT):
                nc.vector.tensor_scalar(HT[:, k, 0:SEQ], XT[:, k, 0:SEQ], MOD[:, KT + k, 0:1], MOD[:, k, 0:1],
                                        ALU.mult, ALU.add)
            hs = HT[:, :, SEQ:TP].rearrange("p k (b s) -> p k b s", s=NS + 1)[:, :, :, 1:NS + 1]
            xs = XT[:, :, SEQ:T].rearrange("p k (b s) -> p k b s", s=NS)
            nc.vector.tensor_tensor(hs, xs, bcast(MOD[:, KT:2 * KT, 1:9], 3, NS), ALU.mult)
            dve.drain()
            nc.vector.tensor_tensor(hs, hs, bcast(MOD[:, 0:KT, 1:9], 3, NS), ALU.add)
            dve.drain()
            nc.vector.tensor_copy(SHO[:, :, 0:1], HT[:, :, SEQ - 1:SEQ])
            nc.vector.tensor_copy(SHO[:, :, 1:9],
                                  HT[:, :, SEQ:TP].rearrange("p k (b s) -> p k b s", s=NS + 1)[:, :, :, NS]).then_inc(h_ready, 1)


def phase_lru(nc, io, g, stack):
    m = Mem(nc, stack, "lru")
    PS, RING, HT, PARAM, LR = g["PS"], g["RING"], g["HT"], g["PARAM"], g["LR"]
    IDENT, BD, MASK, LM, SM, EPSG = (g[x] for x in ("IDENT", "BD", "MASK", "LM", "SM", "EPSG"))
    WG = m.sb("WG", [P, 2, 2, P])
    XP = m.sb("XP", [P, 3 + SEQ + NB * 7])
    XC = m.sb("XC", [P, T])
    RG, IG, AA, TT, QQ, HS, GE = (m.sb(x, [P, T]) for x in ("RG", "IG", "AA", "TT", "QQ", "HS", "GE"))
    YB = m.sb("YB", [P, T])
    LRU0 = m.sb("LRU0", [P, 8, 8])
    CONV0 = m.sb("CONV0", [P, 8, 24])
    LRUO = m.sb("LRUO", [P, 8, 9])
    CVO = m.sb("CVO", [P, 8, 27])
    SPL = m.sb("SPL", [P, 4, 8])
    PT = m.sb("PT", [P, 2, W1])
    DT = m.sb("DT", [P, W1])
    IA = m.sb("IA", [P, 2, P], I32)
    IB = m.sb("IB", [P, 2, P], I32)
    BK = m.sb("BK", [P, 6, P])
    TMPS = m.sb("TMPS", [P, NB])
    st_in, out_sem, y_out = m.sem("st_in"), m.sem("out"), m.sem("y_out")
    w_in = m.sems("w_in", 4)
    wg_in = m.sems("wg_in", 2)
    names = ("slot_used", "wg_used", "lr_mm", "lr_ev", "lr_shift", "px_done", "pg_done", "px_free", "pg_free",
             "xp_ready", "xp_free", "xc_ready", "gates_done", "gates_free", "sig_ready", "a_ready", "q_ready", "s_ready",
             "ge_ready", "tile_done", "y_ready", "iota_ready", "sp_a", "sp_b", "sp_c")
    (slot_used, wg_used, lr_mm, lr_ev, lr_shift, px_done, pg_done, px_free, pg_free, xp_ready, xp_free, xc_ready,
     gates_done, gates_free, sig_ready, a_ready, q_ready, s_ready, ge_ready, tile_done, y_ready, iota_ready,
     sp_a, sp_b, sp_c) = (m.sem(x) for x in names)
    y_free, cleared = m.sem("y_free"), m.sem("cleared")
    N0 = 24

    with nc.Block() as block:
        def load_gates(sp, i, slot):
            for blk in range(2):
                rows = slice(64 * blk, 64 * blk + 64)
                sp.dma_start(WG[rows, slot, :, rows], io["w_gate"][i][rows]).then_inc(wg_in[slot], 16)

        @block.sync
        def _(sp):
            for k in range(2):
                sp.dma_start(RING[:, k, :], io["w_in"][N0 + k]).then_inc(w_in[k], 16)
            sp.dma_start(LRU0[:], io["lru0"]).then_inc(st_in, 16)
            sp.dma_start(CONV0[:], io["conv0"]).then_inc(st_in, 16)
            for k in range(2):
                sp.dma_start(RING[:, 2 + k, :], io["w_in"][26 + 8 * k]).then_inc(w_in[2 + k], 16)
            sp.wait_ge(cleared, 1)
            load_gates(sp, 0, 0)
            for k in range(2):
                sp.wait_ge(slot_used, k + 1)
                sp.dma_start(RING[:, k, :], io["w_in"][27 + 8 * k]).then_inc(w_in[k], 16)
            load_gates(sp, 1, 1)
            with sp.Fori(0, 3) as j:
                for odd in range(2):
                    for k in range(2):
                        slot = 2 * (1 - odd) + k
                        sp.wait_ge(slot_used, 4 * j + (2 * odd + k + 3))
                        sp.dma_start(RING[:, slot, :], io["w_in"][2 * j + (28 + odd + 8 * k)]).then_inc(w_in[slot], 16)
                    sp.wait_ge(wg_used, 2 * j + odd + 1)
                    load_gates(sp, 2 * j + 2 + odd, odd)
            sp.wait_ge(tile_done, 9)
            sp.dma_start(io["lru_out"], LRUO[:]).then_inc(out_sem, 16)
            sp.dma_start(io["conv_out"], CVO[:]).then_inc(out_sem, 16)
            sp.wait_ge(out_sem, 32)

        def lr_project(pe, k):
            pe.wait_ge(w_in[k], 16)
            for part, (lo, n) in enumerate(((0, SEQ), (SEQ, SP5))):
                for kt in range(KT):
                    mm = nc.tensor.matmul(PS[:, 2 * k + part, 0:n], RING[:, k, P * kt:P * kt + P], HT[:, kt, lo:lo + n],
                                          start=(kt == 0), stop=(kt == KT - 1))
            mm.then_inc(slot_used, 1)
            pe.drain().then_inc(lr_mm, 1)

        @block.tensor
        def _(pe):
            for k in range(2):
                lr_project(pe, k)

            def project(j, odd):
                for k, free, done in ((0, px_free, px_done), (1, pg_free, pg_done)):
                    slot = 2 * (1 - odd) + k
                    pe.wait_ge(free, 2 * j + odd + 1)
                    pe.wait_ge(w_in[slot], 16 * j + (32 if odd else 16))
                    for part, (lo, n) in enumerate(((0, SEQ), (SEQ, SP5))):
                        for kt in range(KT):
                            mm = nc.tensor.matmul(PS[:, 2 * k + part, 0:n], RING[:, slot, P * kt:P * kt + P],
                                                  HT[:, kt, lo:lo + n], start=(kt == 0), stop=(kt == KT - 1))
                    mm.then_inc(slot_used, 1)
                    pe.drain().then_inc(done, 1)

            def gates(j, odd):
                pe.wait_ge(xc_ready, 2 * j + odd + 1)
                pe.wait_ge(wg_in[odd], 32 * j + 32)
                pe.wait_ge(gates_free, 2 * j + odd + 1)
                for gate in range(2):
                    for half in range(2):
                        mm = nc.tensor.matmul(PS[:, 4 + 2 * gate + half, 0:TH], WG[:, odd, gate, :],
                                              XC[:, TH * half:TH * half + TH], start=True, stop=True)
                mm.then_inc(wg_used, 1)
                pe.drain().then_inc(gates_done, 1)

            project(0, 0)
            with pe.Fori(0, 3) as j:
                project(j, 1)
                gates(j, 0)
                project(j + 1, 0)
                gates(j, 1)
            project(3, 1)
            gates(3, 0)
            gates(3, 1)

        @block.scalar
        def _(act):
            act.wait_ge(cleared, 1)
            for k in range(2):
                act.wait_ge(lr_mm, k + 1)
                nc.scalar.activation(PT[:, k, 1:1 + SEQ], PS[:, 2 * k, 0:SEQ], ACT.Copy)
                nc.scalar.activation(PT[:, k, 1 + SEQ:W1], PS[:, 2 * k + 1, 0:SP5], ACT.Copy).then_inc(lr_ev, 1)
            act.drain().then_inc(px_free, 1)
            act.sem_inc(pg_free, 1)
            act.sem_inc(gates_free, 1)
            act.sem_inc(xp_free, 1)
            act.wait_ge(lr_shift, 2)
            nc.scalar.activation(LR[0:64, 0, 1:W1], LR[0:64, 0, 1:W1], ACT.Tanh)
            nc.scalar.activation(LR[:, 1, 1:W1], LR[:, 1, 1:W1], ACT.Sigmoid)
            act.wait_ge(sp_a, 1)
            nc.scalar.activation(SPL[:, 1], SPL[:, 0], ACT.Exp, scale=-1.0).then_inc(sp_b, 1)
            act.wait_ge(sp_a, 2)
            nc.scalar.activation(SPL[:, 3], SPL[:, 2], ACT.Ln).then_inc(sp_b, 1)
            with act.Fori(0, 8) as i:
                act.wait_ge(px_done, i + 1)
                act.wait_ge(tile_done, i + 1)
                nc.scalar.activation(XP[:, 3:3 + SEQ], PS[:, 0, 0:SEQ], ACT.Copy)
                nc.scalar.activation(XP[:, 3 + SEQ:].rearrange("p (b s) -> p b s", s=7)[:, :, 3:7],
                                     samples5(PS[:, 1, 0:SP5]), ACT.Copy).then_inc(xp_ready, 1)
                act.drain().then_inc(px_free, 1)
                act.wait_ge(pg_done, i + 1)
                nc.scalar.activation(GE[:, 0:SEQ], PS[:, 2, 0:SEQ], ACT.Gelu_apprx_tanh)
                nc.scalar.activation(samples4(GE[:, SEQ:T]), samples5(PS[:, 3, 0:SP5]),
                                     ACT.Gelu_apprx_tanh).then_inc(ge_ready, 1)
                act.drain().then_inc(pg_free, 1)
                act.wait_ge(gates_done, i + 1)
                nc.scalar.activation(RG[:].rearrange("p (h n) -> p h n", h=2), PS[:, 4:6, 0:TH], ACT.Sigmoid,
                                     bias=PARAM[:, bass.ds(i + PAR["b_ga"], 1)])
                nc.scalar.activation(IG[:].rearrange("p (h n) -> p h n", h=2), PS[:, 6:8, 0:TH], ACT.Sigmoid,
                                     bias=PARAM[:, bass.ds(i + PAR["b_gi"], 1)]).then_inc(sig_ready, 1)
                act.drain().then_inc(gates_free, 1)
                act.wait_ge(sp_c, 1)
                nc.scalar.activation(TT[:], RG[:], ACT.Tanh, scale=g["SP8"][:, 0, bass.ds(i, 1)]).then_inc(a_ready, 1)
                nc.scalar.activation(AA[:], RG[:], ACT.Exp, scale=g["SP8"][:, 1, bass.ds(i, 1)]).then_inc(a_ready, 1)
                act.wait_ge(q_ready, i + 1)
                nc.scalar.activation(QQ[:], QQ[:], ACT.Sqrt).then_inc(s_ready, 1)

        @block.gpsimd
        def _(pool):
            nc.gpsimd.iota(IA[:, 0, :], [[0, P]], base=0, channel_multiplier=1)
            nc.gpsimd.iota(IA[:, 1, :], [[1, P]], base=0, channel_multiplier=0)
            nc.gpsimd.memset(IDENT[:], 0.0)
            pool.drain()
            nc.gpsimd.affine_select(out=IDENT[:], in_=IDENT[:], compare_op=ALU.not_equal, fill=1.0, base=0,
                                    pattern=[[-1, P]], channel_multiplier=1)
            pool.drain().then_inc(iota_ready, 1)
            pool.sem_inc(y_free, 1)
            with pool.Fori(0, 8) as i:
                pool.wait_ge(y_ready, i + 1)
                pool.dma_start(io["mix"][8 + i], YB[:]).then_inc(y_out, 16)
                pool.wait_ge(y_out, 16 * i + 16)
                pool.sem_inc(y_free, 1)

        @block.vector
        def _(dve):
            V = nc.vector
            V.memset(EPSG[:, 0:1], GN_EPS)
            V.memset(EPSG[:, 1:2], LN_EPS)
            V.memset(BD[:], 0.0)
            V.memset(SM[:], 0.0)
            V.memset(LR[:], 0.0)
            V.memset(PT[:], 0.0)
            V.memset(XP[:], 0.0)
            V.memset(WG[:], 0.0)
            dve.drain().then_inc(cleared, 1)
            V.memset(BD[0:64, 0:64], 1.0)
            V.memset(BD[64:128, 64:128], 1.0)
            V.memset(SM[:, 1:1 + SEQ].rearrange("p (c s) -> p c s", s=CH_CHUNK)[:, :, 0], 1.0)
            V.memset(SM[:, 1 + SEQ:W1].rearrange("p (b s) -> p b s", s=NS + 1)[:, :, 1], 1.0)
            dve.wait_ge(iota_ready, 1)
            for n in range(6):
                V.tensor_scalar(IB[:], IA[:], n, None, ALU.logical_shift_right)
                dve.drain()
                V.tensor_tensor(BK[:, n, :], IB[:, 0, :], IB[:, 1, :], ALU.is_equal)
                dve.drain()
            V.tensor_tensor(MASK[:, 0, :], IA[:, 0, :], IA[:, 1, :], ALU.is_lt)
            V.tensor_tensor(MASK[:, 1, :], IA[:, 0, :], IA[:, 1, :], ALU.is_le)
            dve.drain()
            for lv in range(5):
                V.tensor_tensor(LM[:, lv, :], BK[:, lv + 1, :], BK[:, lv, :], ALU.subtract)
            dve.drain()
            for lv in range(5):
                V.tensor_tensor(LM[:, lv, :], LM[:, lv, :], MASK[:, 0, :], ALU.mult)
            dve.drain()
            for k in range(2):
                V.tensor_tensor(MASK[:, k, :], MASK[:, k, :], BK[:, 5, :], ALU.mult)
            dve.drain()
            V.tensor_copy(MASK[:, 2:4, :], MASK[:, 0:2, :])
            for k in range(2):
                dve.wait_ge(lr_ev, k + 1)
                V.tensor_tensor(DT[:, 1:W1], PT[:, k, 0:W1 - 1], PT[:, k, 1:W1], ALU.subtract)
                dve.drain()
                c = PAR["mu"] + N0 + k
                V.scalar_tensor_tensor(LR[:, k, 1:W1], DT[:, 1:W1], PARAM[:, c:c + 1], PT[:, k, 1:W1], ALU.mult, ALU.add)
                dve.drain().then_inc(lr_shift, 1)
            lam = PARAM[:, PAR["lam"]:PAR["lam"] + 8]
            SP8 = g["SP8"]
            V.tensor_scalar(SPL[:, 0], lam, -1.0, None, ALU.mult)
            dve.drain()
            V.tensor_tensor(SPL[:, 0], SPL[:, 0], lam, ALU.max)
            dve.drain().then_inc(sp_a, 1)
            dve.wait_ge(sp_b, 1)
            V.tensor_scalar(SPL[:, 2], SPL[:, 1], 1.0, None, ALU.add)
            dve.drain().then_inc(sp_a, 1)
            dve.wait_ge(sp_b, 2)
            V.tensor_scalar(SPL[:, 2], SPL[:, 2], -1.0, None, ALU.add)
            dve.drain()
            V.tensor_scalar(SPL[:, 0], SPL[:, 2], 0.0, None, ALU.is_equal)
            dve.drain()
            V.tensor_tensor(SPL[:, 2:4], SPL[:, 2:4], bcast(SPL[:, 0], 1, 2), ALU.add)
            dve.drain()
            V.reciprocal(SPL[:, 2], SPL[:, 2])
            V.tensor_tensor(SPL[:, 1], SPL[:, 1], SPL[:, 3], ALU.mult)
            V.tensor_scalar(SPL[:, 0], lam, -1.0, 0.0, ALU.mult, ALU.max)
            dve.drain()
            V.tensor_tensor(SPL[:, 1], SPL[:, 1], SPL[:, 2], ALU.mult)
            dve.drain()
            V.tensor_tensor(SPL[:, 1], SPL[:, 1], SPL[:, 0], ALU.add)
            dve.drain()
            V.tensor_scalar(SP8[:, 0], SPL[:, 1], C_LRU, None, ALU.mult)
            V.tensor_scalar(SP8[:, 1], SPL[:, 1], -C_LRU, None, ALU.mult)
            dve.drain().then_inc(sp_c, 1)
            dve.wait_ge(st_in, 32)
            dve.sem_inc(tile_done, 1)
            xps = XP[:, 3 + SEQ:].rearrange("p (b s) -> p b s", s=7)
            with dve.Fori(0, 8) as i:
                V.tensor_copy(xps[:, :, 0:3], CONV0[:, bass.ds(i, 1), :].rearrange("p i (b s) -> p (i b) s", s=3))
                dve.drain()
                dve.wait_ge(xp_ready, i + 1)
                cw = [PARAM[:, bass.ds(i + (PAR["conv_w"] + 8 * j), 1)] for j in range(4)]
                cb = PARAM[:, bass.ds(i + PAR["conv_b"], 1)]
                xcs = samples4(XC[:, SEQ:T])
                V.tensor_scalar(XC[:, 0:SEQ], XP[:, 0:SEQ], cw[0], cb, ALU.mult, ALU.add)
                V.tensor_scalar(xcs, xps[:, :, 0:4], cw[0], cb, ALU.mult, ALU.add)
                for j in range(1, 4):
                    dve.drain()
                    V.scalar_tensor_tensor(XC[:, 0:SEQ], XP[:, j:j + SEQ], cw[j], XC[:, 0:SEQ], ALU.mult, ALU.add)
                    V.scalar_tensor_tensor(xcs, xps[:, :, j:j + 4], cw[j], xcs, ALU.mult, ALU.add)
                dve.drain().then_inc(xc_ready, 1)
                cvo = CVO[:, bass.ds(i, 1), :].rearrange("p i (b s) -> p (i b) s", s=3)
                V.tensor_copy(cvo[:, 0:1, :], XP[:, SEQ:SEQ + 3].unsqueeze(1))
                V.tensor_copy(cvo[:, 1:9, :], xps[:, :, 4:7])
                dve.wait_ge(a_ready, 2 * i + 1)
                V.tensor_scalar(HS[:], TT[:], 1.0, None, ALU.add)
                V.tensor_scalar(QQ[:], TT[:], 2.0, 1e-30, ALU.mult, ALU.max)
                dve.drain()
                V.reciprocal(HS[:], HS[:])
                dve.drain()
                V.tensor_tensor(QQ[:], QQ[:], HS[:], ALU.mult)
                dve.drain().then_inc(q_ready, 1)
                V.tensor_tensor(IG[:], IG[:], XC[:], ALU.mult)
                dve.drain()
                dve.wait_ge(s_ready, i + 1)
                V.tensor_tensor(QQ[:], QQ[:], IG[:], ALU.mult)
                dve.wait_ge(a_ready, 2 * i + 2)
                a0 = samples4(AA[:, SEQ:T])[:, :, 0]
                g0 = samples4(QQ[:, SEQ:T])[:, :, 0]
                V.tensor_tensor(TMPS[:], a0, LRU0[:, bass.ds(i, 1), :].rearrange("p i b -> p (i b)"), ALU.mult)
                dve.drain()
                V.tensor_tensor(g0, g0, TMPS[:], ALU.add)
                V.memset(a0, 0.0)
                dve.drain()
                V.tensor_tensor_scan(HS[:], AA[:], QQ[:], 0.0, ALU.mult, ALU.add)
                dve.drain()
                lo = LRUO[:, bass.ds(i, 1), :].rearrange("p i b -> p (i b)")
                V.tensor_copy(lo[:, 0:1], HS[:, SEQ - 1:SEQ])
                V.tensor_copy(lo[:, 1:9], samples4(HS[:, SEQ:T])[:, :, NS - 1])
                dve.wait_ge(ge_ready, i + 1)
                dve.wait_ge(y_free, i + 1)
                V.tensor_tensor(YB[:], HS[:], GE[:], ALU.mult)
                dve.drain().then_inc(y_ready, 1)
                dve.sem_inc(tile_done, 1)


KA_, KR_, KB_, KK_, KBH, KKH, KV_ = range(7)


def phase_rwkv(nc, io, g, stack):
    m = Mem(nc, stack, "rw")
    PS, RING, HT, PARAM, LR = g["PS"], g["RING"], g["HT"], g["PARAM"], g["LR"]
    IDENT, BD, MASK, LM, SM, EPSG = (g[x] for x in ("IDENT", "BD", "MASK", "LM", "SM", "EPSG"))
    WLR = m.sb("WLR", [P, 2, P])
    PP = m.sb("PP", [P, 3, W1])
    RR, KX, WD, AG, GN, G2, DT, PX, PI, RPI, SQ, NR = (m.sb(x, [P, W1]) for x in (
        "RR", "KX", "WD", "AG", "GN", "G2", "DT", "PX", "PI", "RPI", "SQ", "NR"))
    BO, YT, YC = (m.sb(x, [P, T]) for x in ("BO", "YT", "YC"))
    OMK = m.sb("OMK", [P, 8])
    BDM = m.sb("BDM", [P, P])
    CHN = m.sb("CHN", [P, 7, W1])
    SLT = m.sb("SLT", [P, 7, 2 * P])
    MM = m.sb("MM", [P, 4, 4, P])
    LT = m.sb("LT", [P, 2, 4, P])
    TB = m.sb("TB", [P, 2, 4, P])
    ZS = m.sb("ZS", [P, 4, P])
    TK = m.sb("TK", [P, 2, 3, P])
    AXX = m.sb("AXX", [P, 4, 2, 64])
    AW = m.sb("AW", [P, 2, 2, 2, 64])
    R2 = m.sb("R2", [P, 2, P])
    Y0 = m.sb("Y0", [P, 2, P])
    GS = m.sb("GS", [P, 8, P])
    K0 = m.sb("K0", [P, 8, P])
    DG = m.sb("DG", [P, 8, P])
    SB = m.sb("SB", [P, 9, P])
    SI = m.sb("SI", [P, 8, P])
    SO = m.sb("SO", [P, 8, P])
    w_in = m.sems("w_in", 3)
    wlr_in, si_in, so_out, sp_out, y_out = (m.sem(x) for x in ("wlr_in", "si_in", "so_out", "sp_out", "y_out"))
    (cleared, slot_used, proj_done, proj_ev, gk_free, banks_idle, act_rows, rows_used, sq_ready, ss_done, ss_ready,
     nr_ready, rk_ready, bo_done, rows_in, g2_free, prep_ready, tr_done, tr_ready, mm_prod, mm_ready, lt_ready,
     dg_ready, x_done, x_ready, z_done, z_ready, t_done, t_ready, aw_done, aw_ready, ry_done, y0_ready,
     r2_ready, gk_done, gk_read, gk_ready, s_done, s_ready, yy_done, yt_ready, mean_done, yc_ready, ysq_ready, var_done,
     sd_ready, post_done, mix_free, so_ready, so_free, sp_ready, sp_free, si_free) = (m.sem(x) for x in (
        "cleared slot_used proj_done proj_ev gk_free banks_idle act_rows rows_used sq_ready ss_done ss_ready "
        "nr_ready rk_ready bo_done rows_in g2_free prep_ready tr_done tr_ready mm_prod mm_ready lt_ready "
        "dg_ready x_done x_ready z_done z_ready t_done t_ready aw_done aw_ready ry_done y0_ready "
        "r2_ready gk_done gk_read gk_ready s_done s_ready yy_done yt_ready mean_done yc_ready ysq_ready var_done "
        "sd_ready post_done mix_free so_ready so_free sp_ready sp_free si_free").split())
    PC0, PC1 = 1 + SEQ, W1

    def chan_view(kind, x, step):
        if step < 2:
            lo = 1 + 2 * P * step + P * x
            return CHN[:, kind, lo:lo + P]
        return SLT[:, kind, P * x:P * x + P]

    def two_kinds(rows, kind, x, step):
        if step < 2:
            lo = 1 + 2 * P * step + P * x
            return CHN[rows, kind:kind + 2, lo:lo + P]
        return SLT[rows, kind:kind + 2, P * x:P * x + P]

    with nc.Block() as block:
        @block.sync
        def _(sp):
            for k in range(3):
                sp.dma_start(RING[:, k, :], io["w_in"][8 * k]).then_inc(w_in[k], 16)
            sp.dma_start(WLR[:], io["w_lr"][0]).then_inc(wlr_in, 16)
            with sp.Fori(0, NPAIR - 1) as i:
                for k in range(3):
                    sp.wait_ge(slot_used, 4 * i + k + 1)
                    sp.dma_start(RING[:, k, :], io["w_in"][i + (8 * k + 1)]).then_inc(w_in[k], 16)
                sp.wait_ge(slot_used, 4 * i + 4)
                sp.dma_start(WLR[:], io["w_lr"][i + 1]).then_inc(wlr_in, 16)

        BANKS = (6, 2, 4, 6, 2, 4)

        def project(pe, i, which):
            lhs = RING[:, which, :]
            pe.wait_ge(w_in[which], 16 * i + 16)
            for lo, n, out in ((0, SEQ, PS[:, BANKS[which], 0:SEQ]),
                               (SEQ, SP5, PS[:, 7, SP5 * which:SP5 * which + SP5])):
                for kt in range(KT):
                    mm = nc.tensor.matmul(out, lhs[:, P * kt:P * kt + P], HT[:, kt, lo:lo + n],
                                          start=(kt == 0), stop=(kt == KT - 1))
            mm.then_inc(slot_used, 1)
            pe.drain().then_inc(proj_done, 1)

        def project_low(pe, i):
            pe.wait_ge(wlr_in, 16 * i + 16)
            for n, (lhs, rhs) in enumerate(((WLR[0:64, 0, :], LR[0:64, 0, :]), (WLR[64:P, 0, :], LR[64:P, 0, :]),
                                            (WLR[:, 1, :], LR[:, 1, :]))):
                pe.wait_ge(proj_ev, 6 * i + (n + 1))
                bank = BANKS[3 + n]
                nc.tensor.matmul(PS[:, bank, 0:SEQ], lhs, rhs[:, 1:1 + SEQ], start=True, stop=True)
                mm = nc.tensor.matmul(PS[:, 7, SP5 * (3 + n):SP5 * (4 + n)], lhs, rhs[:, PC0:PC1], start=True, stop=True)
                if n == 2:
                    mm.then_inc(slot_used, 1)
                pe.drain().then_inc(proj_done, 1)

        def head_sum(pe, ready, value, done, bank, bank2):
            pe.wait_ge(ready, value)
            nc.tensor.matmul(PS[:, bank, 0:SEQ], BD[:], SQ[:, 1:1 + SEQ], start=True, stop=True)
            nc.tensor.matmul(PS[:, bank2, 0:SP5], BD[:], SQ[:, PC0:PC1],
                             start=True, stop=True).then_inc(done, 1)

        def evacuate(act, i):
            A = nc.scalar.activation
            w0, a0 = (PARAM[:, bass.ds(i + PAR[n], 1)] for n in ("w0", "a0"))
            for sample in range(2):
                cols = slice(PC0, PC1) if sample else slice(1, 1 + SEQ)
                for which in range(6):
                    if sample:
                        src = PS[:, 7, SP5 * which:SP5 * which + SP5]
                        if which == 0:
                            act.wait_ge(proj_done, 6 * i + 6)
                    else:
                        src = PS[:, BANKS[which], 0:SEQ]
                        act.wait_ge(proj_done, 6 * i + (which + 1))
                    if which == 3:
                        last = A(WD[:, cols], src, ACT.Sigmoid, bias=w0)
                    elif which == 4:
                        last = A(AG[:, cols], src, ACT.Sigmoid, bias=a0)
                    else:
                        last = A(GN[:, cols] if which == 5 else PP[:, which, cols], src, ACT.Copy)
                    if not sample:
                        last.then_inc(proj_ev, 1)
            act.drain()
            A(WD[:, 1:W1], WD[:, 1:W1], ACT.Exp, scale=-EXP_HALF).then_inc(rows_in, 1)

        def pe_scan(pe, i, step, n):
            pe.wait_ge(s_ready, 18 * i + 9 * step + n + 1)
            nc.tensor.matmul(PS[:, 7, CH_CHUNK * n:CH_CHUNK * n + CH_CHUNK], SB[:, n, :],
                             R2[:, n // 4, 32 * (n % 4):32 * (n % 4) + 32], start=True, stop=True)
            nc.tensor.matmul(PS[:, 7, 256 + P * (n % 2):256 + P * (n % 2) + P], GS[:, n, :], SB[:, n, :],
                             start=True, stop=True).then_inc(s_done, 1)

        def pe_step(pe, i, step):
            u = 3 * i + step
            if step:
                pe.wait_ge(y0_ready, 2 * u)
            for x in range(2):
                for c, kind in enumerate((KA_, KBH, KKH, KV_)):
                    mm = nc.tensor.transpose(PS[:, 4 + x, P * c:P * c + P], chan_view(kind, x, step), IDENT[:])
                mm.then_inc(tr_done, 1)
            if step:
                pe.wait_ge(gk_read, u)
            for q in range(4):
                x, h = q // 2, q % 2
                rows = slice(64 * h, 64 * h + 64)
                for c, kind in enumerate((KB_, KK_)):
                    mm = nc.tensor.matmul(PS[:, q, 256 * c:256 * c + 256], chan_view(kind, x, step)[rows],
                                          two_kinds(rows, KA_, x, step), start=True, stop=True)
                mm.then_inc(mm_prod, 1)
            for x in range(2):
                pe.wait_ge(mm_ready, 4 * u + (2 * x + 2))
                pe.wait_ge(tr_ready, 2 * u + (x + 1))
                for h in range(2):
                    mm = nc.tensor.matmul(PS[:, 4 + x, 64 * h:64 * h + 64], MM[:, 2, 2 * x + h, :],
                                          TK[:, x, 2, 64 * h:64 * h + 64], start=True, stop=True)
                mm.then_inc(x_done, 1)
            if step:
                pe.wait_ge(gk_ready, u)
            for lv in range(5):
                for x in range(2):
                    pe.wait_ge(lt_ready, 10 * u + (2 * lv + x + 1))
                    if lv:
                        pe.wait_ge(t_ready, 10 * u + (2 * lv + x - 1))
                    for h in range(2):
                        q = 2 * x + h
                        if lv == 0:
                            mm = nc.tensor.transpose(PS[:, 2 * x, P * h:P * h + P], LT[:, 0, q, :], IDENT[:])
                        else:
                            mm = nc.tensor.matmul(PS[:, 2 * x, P * h:P * h + P], LT[:, lv % 2, q, :], TB[:, 0, q, :],
                                                  start=True, stop=True)
                    mm.then_inc(z_done, 1)
                if lv == 0:
                    continue
                if step:
                    pe_scan(pe, i, step - 1, 2 * lv - 2)
                for x in range(2):
                    pe.wait_ge(z_ready, 8 * u + (2 * lv + x - 1))
                    for h in range(2):
                        q = 2 * x + h
                        if lv < 4:
                            nc.tensor.matmul(PS[:, 2 * x + 1, P * h:P * h + P], TB[:, 1, q, :], ZS[:, q, :],
                                             start=True, stop=True)
                        mm = nc.tensor.matmul(PS[:, 2 * x + 1, 256 + P * h:256 + P * h + P], ZS[:, q, :], TB[:, 1, q, :],
                                              start=True, stop=True)
                    mm.then_inc(t_done, 1)
                if step:
                    pe_scan(pe, i, step - 1, 2 * lv - 1)
            for x in range(2):
                pe.wait_ge(x_ready, 2 * u + (x + 1))
                pe.wait_ge(t_ready, 10 * u + (9 + x))
                for h in range(2):
                    mm = nc.tensor.matmul(PS[:, 4 + x, P * h:P * h + P], TB[:, 1, 2 * x + h, :], AXX[:, 2 * x + h, :, :],
                                          start=True, stop=True)
                mm.then_inc(aw_done, 1)
            for x in range(2):
                pe.wait_ge(aw_ready, 2 * u + (x + 1))
                for h in range(2):
                    q = 2 * x + h
                    rows = slice(64 * h, 64 * h + 64)
                    nc.tensor.matmul(PS[rows, 4 + x, 256:384], AW[:, x, 0, h, :], MM[:, 1, q, :], start=True, stop=True)
                    y0 = PS[rows, 4 + x, 384:512]
                    nc.tensor.matmul(y0, AW[:, x, 1, h, :], MM[:, 1, q, :], start=True, stop=False)
                    mm = nc.tensor.matmul(y0, TK[:, x, 2, 64 * h:64 * h + 64], MM[:, 3, q, :], start=False, stop=True)
                mm.then_inc(ry_done, 1)
            for x in range(2):
                for c in range(4):
                    rows = slice(32 * c, 32 * c + 32)
                    at = 256 * x
                    nc.tensor.matmul(PS[:, c, at:at + P], AW[rows, x, 0, :, :], TK[rows, x, 0, :], start=True, stop=True)
                    nc.tensor.matmul(PS[:, c, at + P:at + 2 * P], TK[rows, x, 0, :], AW[rows, x, 1, :, :],
                                     start=True, stop=False)
                    mm = nc.tensor.matmul(PS[:, c, at + P:at + 2 * P], TK[rows, x, 1, :], TK[rows, x, 2, :],
                                          start=False, stop=True)
            mm.then_inc(gk_done, 1)

        def pe_samples(pe, i):
            u = 3 * i + 2
            pe.wait_ge(gk_ready, u + 1)
            pe.wait_ge(y0_ready, 2 * u + 2)
            pe.wait_ge(si_in, 32 * i + 32)
            for n in range(8):
                nc.tensor.matmul(PS[:, 4 + n // 4, P * (n % 4):P * (n % 4) + P], GS[:, n, :], SI[:, n, :],
                                 start=True, stop=True)
                mm = nc.tensor.matmul(PS[:, 7, CH_CHUNK * n:CH_CHUNK * n + CH_CHUNK], SI[:, n, :],
                                      R2[:, n // 4, 32 * (n % 4):32 * (n % 4) + 32], start=True, stop=True)
            mm.then_inc(yy_done, 1)

        def pe_post(pe, i, ahead2):
            pe.wait_ge(yt_ready, 3 * i + 3)
            for half in range(2):
                mm = nc.tensor.matmul(PS[:, 0 + half, 0:TH], BDM[:], YT[:, TH * half:TH * half + TH], start=True, stop=True)
            mm.then_inc(mean_done, 1)
            if ahead2:
                project(pe, i + 2, 0)
            pe.wait_ge(ysq_ready, i + 1)
            for half in range(2):
                mm = nc.tensor.matmul(PS[:, 2 + half, 0:TH], BDM[:], SQ[:, TH * half:TH * half + TH], start=True, stop=True)
            mm.then_inc(var_done, 1)

        @block.tensor
        def _(pe):
            pe.wait_ge(cleared, 1)
            for which in range(3):
                project(pe, 0, which)
            project_low(pe, 0)
            pe.wait_ge(rows_in, 1)
            project(pe, 1, 0)

            def pair(i, ahead, ahead2):
                pe.wait_ge(banks_idle, i + 1)
                head_sum(pe, sq_ready, i + 1, ss_done, 3, 5)
                if ahead:
                    project(pe, i + 1, 1)
                head_sum(pe, rk_ready, i + 1, bo_done, 0, 1)
                if ahead:
                    project(pe, i + 1, 2)
                    project_low(pe, i + 1)
                    pe.wait_ge(rows_in, i + 2)
                pe.wait_ge(prep_ready, i + 1)
                for step in range(3):
                    pe_step(pe, i, step)
                pe_samples(pe, i)
                pe_post(pe, i, ahead2)

            with pe.Fori(0, NPAIR - 2) as i:
                pair(i, True, True)
            pair(NPAIR - 2, True, False)
            pair(NPAIR - 1, False, False)

        def act_step(act, i, step):
            u = 3 * i + step
            A = nc.scalar.activation
            for x in range(2):
                act.wait_ge(tr_done, 2 * u + (x + 1))
                A(AXX[:, 2 * x:2 * x + 2, 0, :], PS[:, 4 + x, 0:P].rearrange("p (h c) -> p h c", h=2), ACT.Copy)
                A(TK[:, x].rearrange("p k c -> p (k c)"), PS[:, 4 + x, P:4 * P], ACT.Copy)
                act.drain().then_inc(tr_ready, 1)
            for x in range(2):
                act.wait_ge(x_done, 2 * u + (x + 1))
                A(AXX[:, 2 * x:2 * x + 2, 1, :], PS[:, 4 + x, 0:P].rearrange("p (h c) -> p h c", h=2),
                  ACT.Copy).then_inc(x_ready, 1)
            for lv in range(1, 5):
                for x in range(2):
                    act.wait_ge(z_done, 10 * u + (2 * lv + x + 1))
                    A(ZS[:, 2 * x:2 * x + 2], PS[:, 2 * x, 0:256].rearrange("p (h c) -> p h c", h=2),
                      ACT.Copy).then_inc(z_ready, 1)
            for x in range(2):
                act.wait_ge(aw_done, 2 * u + (x + 1))
                A(AW[:, x].rearrange("p k h c -> p h k c"),
                  PS[:, 4 + x, 0:256].rearrange("p (h k c) -> p h k c", h=2, k=2), ACT.Copy).then_inc(aw_ready, 1)
            if step:
                act.wait_ge(yt_ready, u)
            for x in range(2):
                act.wait_ge(r2_ready, 2 * u + (x + 1))
                A(Y0[:, x], PS[:, 4 + x, 384:512], ACT.Copy).then_inc(y0_ready, 1)

        @block.scalar
        def _(act):
            A = nc.scalar.activation
            act.wait_ge(cleared, 1)
            evacuate(act, 0)

            def pair(i, ahead):
                act.wait_ge(act_rows, i + 1)
                A(SQ[:, 1:W1], KX[:, 1:W1], ACT.Square, scale=PARAM[:, bass.ds(i + PAR["k_k"], 1)]).then_inc(sq_ready, 1)
                act.wait_ge(ss_ready, i + 1)
                A(NR[:, 1:W1], NR[:, 1:W1], ACT.Sqrt).then_inc(nr_ready, 1)
                act.wait_ge(g2_free, i + 1)
                A(G2[:, 1:W1], GN[:, 1:W1], ACT.Copy)
                if ahead:
                    act.wait_ge(rows_used, i + 1)
                    evacuate(act, i + 1)
                for step in range(3):
                    act_step(act, i, step)
                act.wait_ge(yc_ready, i + 1)
                A(SQ[:, 0:T], YC[:], ACT.Square).then_inc(ysq_ready, 1)
                act.wait_ge(var_done, i + 1)
                A(NR[:, 0:T].rearrange("p (h n) -> p h n", h=2), PS[:, 2:4, 0:TH], ACT.Sqrt,
                  bias=EPSG[:, 0:1]).then_inc(sd_ready, 1)

            with act.Fori(0, NPAIR - 1) as i:
                pair(i, True)
            pair(NPAIR - 1, False)

        @block.gpsimd
        def _(pool):
            G = nc.gpsimd
            pool.wait_ge(cleared, 1)

            def load_states(i):
                for h in range(2):
                    rows = slice(64 * h, 64 * h + 64)
                    pool.dma_start(SI[rows, :, rows], io["wkv0"][i][rows]).then_inc(si_in, 16)

            load_states(0)

            def pair(i, ahead):
                for step in range(3):
                    u = 3 * i + step
                    pool.wait_ge(prep_ready, i + 1)
                    ident = bcast(IDENT[:], 1, 4)
                    pool.wait_ge(gk_free, u + 1)
                    for x in range(2):
                        if step < 2:
                            lo = 1 + 2 * P * step + P * x + CH_CHUNK - 1
                            pc = PI[:, lo:lo + 3 * CH_CHUNK + 1:CH_CHUNK]
                        else:
                            lo = PC0 + 4 * (NS + 1) * x + NS
                            pc = PI[:, lo:lo + 3 * (NS + 1) + 1:NS + 1]
                        G.tensor_tensor(DG[:, 4 * x:4 * x + 4, :], ident, bcast(pc, 2, P), ALU.mult)
                    pool.drain().then_inc(dg_ready, 1)
                    pool.wait_ge(mm_ready, 4 * u + 4)
                    for lv in range(5):
                        for x in range(2):
                            if lv >= 2:
                                pool.wait_ge(t_ready, 10 * u + (2 * lv + x - 3))
                            G.tensor_tensor(LT[:, lv % 2, 2 * x:2 * x + 2], MM[:, 0, 2 * x:2 * x + 2, :],
                                            bcast(LM[:, lv, :], 1, 2), ALU.mult)
                            pool.drain().then_inc(lt_ready, 1)
                    if step == 2:
                        pool.wait_ge(sp_ready, i + 1)
                        for h in range(2):
                            rows = slice(64 * h, 64 * h + 64)
                            pool.dma_start(io["wkv_p"][i][rows], SB[rows, 8, rows]).then_inc(sp_out, 16)
                        pool.wait_ge(sp_out, 32 * i + 32)
                        pool.sem_inc(sp_free, 1)
                pool.wait_ge(so_ready, i + 1)
                for h in range(2):
                    rows = slice(64 * h, 64 * h + 64)
                    pool.dma_start(io["wkv_s"][i][rows], SO[rows, :, rows]).then_inc(so_out, 16)
                if ahead:
                    load_states(i + 1)
                pool.wait_ge(so_out, 32 * i + 32)
                pool.sem_inc(so_free, 1)
                pool.wait_ge(post_done, i + 1)
                pool.dma_start(io["mix"][i], YT[:]).then_inc(y_out, 16)
                pool.wait_ge(y_out, 16 * i + 16)
                pool.sem_inc(mix_free, 1)

            with pool.Fori(0, NPAIR - 1) as i:
                pair(i, True)
            pair(NPAIR - 1, False)

        def prep(dve, i):
            V = nc.vector
            body = slice(1, W1)
            dve.wait_ge(rows_in, i + 1)
            for which, (kt, dst) in enumerate(((0, RR[:, body]), (8, KX[:, body]), (16, CHN[:, KV_, body]))):
                V.tensor_tensor(DT[:, body], PP[:, which, 0:W1 - 1], PP[:, which, 1:W1], ALU.subtract)
                dve.drain()
                V.scalar_tensor_tensor(dst, DT[:, body], PARAM[:, bass.ds(i + (PAR["mu"] + kt), 1)], PP[:, which, 1:W1],
                                       ALU.mult, ALU.add)
                dve.drain()
                if which == 1:
                    dve.sem_inc(act_rows, 1)
            V.tensor_tensor_scan(PX[:, body], WD[:, 0:W1 - 1], SM[:, body], 1.0, ALU.mult, ALU.max)
            V.tensor_scalar(DT[:, body], AG[:, body], PARAM[:, bass.ds(i + PAR["k_a"], 1)], OMK[:, bass.ds(i, 1)],
                            ALU.mult, ALU.add)
            dve.drain()
            V.tensor_tensor(PI[:, body], PX[:, body], WD[:, body], ALU.mult)
            V.tensor_tensor(DT[:, body], DT[:, body], KX[:, body], ALU.mult)
            dve.wait_ge(ss_done, i + 1)
            V.tensor_scalar(NR[:, 1:1 + SEQ], PS[:, 3, 0:SEQ], 1e-24, None, ALU.max)
            V.tensor_scalar(NR[:, PC0:PC1], PS[:, 5, 0:SP5], 1e-24, None, ALU.max)
            dve.drain().then_inc(ss_ready, 1)
            V.scalar_tensor_tensor(SQ[:, body], RR[:, body], PARAM[:, bass.ds(i + PAR["r_k"], 1)], DT[:, body],
                                   ALU.mult, ALU.mult)
            dve.drain().then_inc(rk_ready, 1)
            V.reciprocal(RPI[:, body], PI[:, body])
            V.tensor_tensor(CHN[:, KR_, body], RR[:, body], PI[:, body], ALU.mult)
            dve.drain()
            V.tensor_tensor(CHN[:, KK_, body], DT[:, body], RPI[:, body], ALU.mult)
            dve.wait_ge(nr_ready, i + 1)
            V.reciprocal(NR[:, body], NR[:, body])
            dve.drain()
            V.scalar_tensor_tensor(NR[:, body], KX[:, body], PARAM[:, bass.ds(i + PAR["k_k"], 1)], NR[:, body],
                                   ALU.mult, ALU.mult)
            dve.drain()
            V.scalar_tensor_tensor(CHN[:, KA_, body], NR[:, body], -1.0, PX[:, body], ALU.mult, ALU.mult)
            V.tensor_tensor(DT[:, body], NR[:, body], AG[:, body], ALU.mult)
            dve.drain()
            V.tensor_tensor(CHN[:, KB_, body], DT[:, body], RPI[:, body], ALU.mult)
            dve.drain()
            V.tensor_tensor(CHN[:, KBH:KKH + 1, 1:1 + SEQ].rearrange("p k (c s) -> p k c s", s=CH_CHUNK),
                            CHN[:, KB_:KK_ + 1, 1:1 + SEQ].rearrange("p k (c s) -> p k c s", s=CH_CHUNK),
                            bcast(bcast(PI[:, CH_CHUNK:1 + SEQ:CH_CHUNK], 2, CH_CHUNK), 1, 2), ALU.mult)
            s5 = lambda lo, hi: CHN[:, lo:hi, PC0:PC1].rearrange("p k (b s) -> p k b s", s=NS + 1)[:, :, :, 1:]
            s32 = lambda lo, hi: SLT[:, lo:hi, :].rearrange("p k (b s) -> p k b s", s=CH_CHUNK)[:, :, :, 0:NS]
            V.tensor_copy(s32(KA_, KK_ + 1), s5(KA_, KK_ + 1))
            V.tensor_copy(s32(KV_, KV_ + 1), s5(KV_, KV_ + 1))
            V.tensor_tensor(s32(KBH, KKH + 1), s5(KB_, KK_ + 1),
                            bcast(bcast(PI[:, PC0 + NS:PC1:NS + 1], 2, NS), 1, 2), ALU.mult)
            dve.wait_ge(bo_done, i + 1)
            V.tensor_tensor(BO[:, 0:SEQ], CHN[:, KV_, 1:1 + SEQ], PS[:, 0, 0:SEQ], ALU.mult)
            V.tensor_tensor(samples4(BO[:, SEQ:T]), samples5(CHN[:, KV_, PC0:PC1]), samples5(PS[:, 1, 0:SP5]),
                            ALU.mult)
            dve.drain().then_inc(rows_used, 1)
            dve.sem_inc(prep_ready, 1)

        def dve_step(dve, i, step):
            V = nc.vector
            u = 3 * i + step
            y0 = Y0[:].rearrange("p x t -> p (x t)")
            for q in range(4):
                dve.wait_ge(mm_prod, 4 * u + (q + 1))
                V.tensor_tensor(MM[:, :, q, :], PS[:, q, :].rearrange("p (k t) -> p k t", k=4), MASK[:],
                                ALU.mult).then_inc(mm_ready, 1)
            if step:
                if step == 1:
                    dve.wait_ge(sp_free, i + 1)
                    V.memset(SB[:, 0, :], 0.0).then_inc(s_ready, 1)
                else:
                    V.tensor_copy(SB[:, 0, :], SB[:, 8, :])
                    dve.drain().then_inc(s_ready, 1)
            for lv in range(5):
                if lv and step:
                    dve_scan(dve, i, step - 1, 2 * lv - 2)
                for x in range(2):
                    tb, tbk = TB[:, :, 2 * x:2 * x + 2, :], slice(2 * x, 2 * x + 2)
                    if lv == 0:
                        dve.wait_ge(lt_ready, 10 * u + (x + 1))
                        V.tensor_tensor(TB[:, 1, tbk], LT[:, 0, tbk], bcast(IDENT[:], 1, 2), ALU.add)
                        dve.wait_ge(z_done, 10 * u + (x + 1))
                        V.tensor_tensor(TB[:, 0, tbk], PS[:, 2 * x, 0:256].rearrange("p (h t) -> p h t", h=2),
                                        bcast(IDENT[:], 1, 2), ALU.add)
                        dve.drain().then_inc(t_ready, 1)
                        continue
                    dve.wait_ge(t_done, 8 * u + (2 * lv + x - 1))
                    if lv < 4:
                        V.tensor_tensor(tb, tb, PS[:, 2 * x + 1, :].rearrange("p (k h t) -> p k h t", k=2, h=2), ALU.add)
                    else:
                        V.tensor_tensor(TB[:, 1, tbk], TB[:, 1, tbk],
                                        PS[:, 2 * x + 1, 256:512].rearrange("p (h t) -> p h t", h=2), ALU.add)
                    dve.drain().then_inc(t_ready, 1)
                if lv and step:
                    dve_scan(dve, i, step - 1, 2 * lv - 1)
            if step:
                if step == 2:
                    dve.drain().then_inc(sp_ready, 1)
                if step == 1:
                    dve.wait_ge(mix_free, i + 1)
                V.tensor_tensor(YT[:, 256 * step - 256:256 * step], y0, PS[:, 7, 0:256], ALU.add)
                dve.drain().then_inc(yt_ready, 1)
            for x in range(2):
                dve.wait_ge(ry_done, 2 * u + (x + 1))
                V.tensor_tensor(R2[:, x, :], chan_view(KR_, x, step), PS[:, 4 + x, 256:384], ALU.add)
                dve.drain().then_inc(r2_ready, 1)
            dve.wait_ge(gk_done, u + 1)
            bd = bcast(bcast(BD[:], 1, 4), 1, 2)
            by_chunk = lambda ap: ap.rearrange("p (x c) t -> p x c t", x=2)
            prod = PS[:, 0:4, :].rearrange("p c (x k t) -> p k x c t", x=2, k=2)
            V.tensor_tensor(by_chunk(GS[:]), prod[:, 0], bd, ALU.mult)
            V.tensor_tensor(by_chunk(K0[:]), prod[:, 1], bd, ALU.mult)
            dve.drain().then_inc(gk_read, 1)
            dve.wait_ge(dg_ready, u + 1)
            V.tensor_tensor(GS[:], GS[:], DG[:], ALU.add)
            dve.drain().then_inc(gk_ready, 1)
            dve.sem_inc(gk_free, 1)

        def dve_scan(dve, i, step, n):
            dve.wait_ge(s_done, 16 * i + 8 * step + (n + 1))
            nc.vector.tensor_tensor(SB[:, n + 1, :], K0[:, n, :], PS[:, 7, 256 + P * (n % 2):256 + P * (n % 2) + P],
                                    ALU.add).then_inc(s_ready, 1)

        def dve_samples(dve, i):
            V = nc.vector
            u = 3 * i + 2
            dve.wait_ge(yy_done, i + 1)
            dve.wait_ge(y0_ready, 2 * u + 2)
            sl = lambda ap: ap.rearrange("p (b s) -> p b s", s=CH_CHUNK)[:, :, 0:NS]
            V.tensor_tensor(samples4(YT[:, SEQ:T]), sl(Y0[:].rearrange("p x t -> p (x t)")), sl(PS[:, 7, 0:256]), ALU.add)
            dve.drain().then_inc(yt_ready, 1)
            dve.wait_ge(so_free, i + 1)
            V.tensor_tensor(SO[:].rearrange("p (x c) t -> p x c t", x=2), K0[:].rearrange("p (x c) t -> p x c t", x=2),
                            PS[:, 4:6, :].rearrange("p x (c t) -> p x c t", c=4), ALU.add)
            dve.drain().then_inc(so_ready, 1)

        def post(dve, i):
            V = nc.vector
            dve.wait_ge(mean_done, i + 1)
            halves = lambda ap: ap.rearrange("p (h n) -> p h n", h=2)
            V.tensor_tensor(halves(YC[:]), halves(YT[:]), PS[:, 0:2, 0:TH], ALU.subtract)
            dve.drain().then_inc(yc_ready, 1)
            dve.wait_ge(sd_ready, i + 1)
            V.reciprocal(NR[:, 0:T], NR[:, 0:T])
            dve.drain().then_inc(banks_idle, 1)
            V.tensor_tensor(YC[:], YC[:], NR[:, 0:T], ALU.mult)
            dve.drain()
            V.tensor_scalar(YC[:], YC[:], PARAM[:, bass.ds(i + PAR["lnx_w"], 1)], PARAM[:, bass.ds(i + PAR["lnx_b"], 1)],
                            ALU.mult, ALU.add)
            dve.drain()
            V.tensor_tensor(YC[:], YC[:], BO[:], ALU.add)
            dve.drain()
            V.tensor_tensor(YT[:, 0:SEQ], YC[:, 0:SEQ], G2[:, 1:1 + SEQ], ALU.mult)
            V.tensor_tensor(samples4(YT[:, SEQ:T]), samples4(YC[:, SEQ:T]), samples5(G2[:, PC0:PC1]), ALU.mult)
            dve.drain().then_inc(post_done, 1)
            dve.sem_inc(g2_free, 1)

        @block.vector
        def _(dve):
            V = nc.vector
            for buf in (PP, WD, SLT, SI, SB, CHN, NR):
                V.memset(buf[:], 0.0)
            V.tensor_scalar(OMK[:], PARAM[:, PAR["k_a"]:PAR["k_a"] + 8], -1.0, 1.0, ALU.mult, ALU.add)
            V.tensor_scalar(BDM[:], BD[:], 1.0 / 64, None, ALU.mult)
            dve.drain().then_inc(cleared, 1)
            dve.sem_inc(mix_free, 1)
            dve.sem_inc(so_free, 1)
            dve.sem_inc(sp_free, 1)
            dve.sem_inc(gk_free, 1)
            dve.sem_inc(g2_free, 1)
            dve.sem_inc(banks_idle, 1)
            with dve.Fori(0, NPAIR) as i:
                prep(dve, i)
                for step in range(3):
                    dve_step(dve, i, step)
                dve_samples(dve, i)
                post(dve, i)


class Norm:

    def __init__(self, nc, m, g, X, wname, bname):
        self.nc, self.g, self.X, self.wname, self.bname = nc, g, X, wname, bname
        self.SQ = m.sb("nSQ", [P, 2, T])
        self.MN = m.sb("nMN", [P, 2, T])
        self.ONES = m.sb("nONES", [P, P])
        self.ones_ready, self.mean_done, self.xc_ready, self.sq_ready, self.sq_used, self.sd_ready = (
            m.sem("n_" + x) for x in ("ones_ready", "mean_done", "xc_ready", "sq_ready", "sq_used", "sd_ready"))

    def start(self, dve):
        self.nc.vector.memset(self.ONES[:], 1.0 / D)
        dve.drain().then_inc(self.ones_ready, 1)

    def tensor(self, pe, x_ready, per_tile):
        PS = self.g["PS"]
        pe.wait_ge(self.ones_ready, 1)
        for kt in range(KT):
            pe.wait_ge(x_ready, per_tile * (kt + 1))
            for half in range(2):
                mm = self.nc.tensor.matmul(PS[:, 4 + half, 0:TH], self.ONES[:], self.X[:, kt, TH * half:TH * half + TH],
                                           start=(kt == 0), stop=(kt == KT - 1))
        mm.then_inc(self.mean_done, 1)
        for kt in range(KT):
            pe.wait_ge(self.sq_ready, kt + 1)
            for half in range(2):
                mm = self.nc.tensor.matmul(PS[:, 6 + half, 0:TH], self.ONES[:],
                                           self.SQ[:, kt % 2, TH * half:TH * half + TH],
                                           start=(kt == 0), stop=(kt == KT - 1))
            mm.then_inc(self.sq_used, 1)

    def scalar(self, act):
        for kt in range(KT):
            act.wait_ge(self.xc_ready, kt + 1)
            if kt >= 2:
                act.wait_ge(self.sq_used, kt - 1)
            self.nc.scalar.activation(self.SQ[:, kt % 2, :], self.X[:, kt, :], ACT.Square).then_inc(self.sq_ready, 1)
        act.wait_ge(self.sq_used, KT)
        self.nc.scalar.activation(self.MN[:, 1].rearrange("p (h n) -> p h n", h=2), self.g["PS"][:, 6:8, 0:TH], ACT.Sqrt,
                                  bias=self.g["EPSG"][:, 1:2]).then_inc(self.sd_ready, 1)

    def vector(self, dve, per_tile):
        V, PARAM = self.nc.vector, self.g["PARAM"]
        dve.wait_ge(self.mean_done, 1)
        V.tensor_copy(self.MN[:, 0].rearrange("p (h n) -> p h n", h=2), self.g["PS"][:, 4:6, 0:TH])
        dve.drain()
        for kt in range(KT):
            V.tensor_tensor(self.X[:, kt, :], self.X[:, kt, :], self.MN[:, 0], ALU.subtract).then_inc(self.xc_ready, 1)
        dve.wait_ge(self.sd_ready, 1)
        V.reciprocal(self.MN[:, 1], self.MN[:, 1])
        dve.drain()
        for kt in range(KT):
            V.tensor_tensor(self.X[:, kt, :], self.X[:, kt, :], self.MN[:, 1], ALU.mult)
        dve.drain()
        for kt in range(KT):
            w, b = (PARAM[:, PAR[n] + kt:PAR[n] + kt + 1] for n in (self.wname, self.bname))
            V.tensor_scalar(self.X[:, kt, :], self.X[:, kt, :], w, b, ALU.mult, ALU.add)
            if per_tile:
                per_tile(kt)


def phase_out(nc, io, g, stack):
    m = Mem(nc, stack, "out")
    PS, RING, MOD, XT, H2 = g["PS"], g["RING"], g["MOD"], g["XT"], g["HT"]
    MIX = m.sb("MIX", [P, KT, T])
    TMP = m.sb("TMP", [P, 2, T])
    norm = Norm(nc, m, g, XT, "ln1_w", "ln1_b")
    w_in = m.sems("w_in", 4)
    mix_in, x_in, tile_done, x_ready, bank_free = (
        m.sem(x) for x in ("mix_in", "x_in", "tile_done", "x_ready", "bank_free"))

    with nc.Block() as block:
        @block.sync
        def _(sp):
            sp.dma_start(MIX[:], io["mix"].rearrange("k p t -> p k t")).then_inc(mix_in, 16)
            for k in range(4):
                sp.dma_start(RING[:, k, :], io["w_out"][k]).then_inc(w_in[k], 16)
            sp.dma_start(XT[:], io["xT"]).then_inc(x_in, 16)
            with sp.Fori(0, 3) as i:
                for k in range(4):
                    sp.wait_ge(tile_done, 4 * i + k + 1)
                    sp.dma_start(RING[:, k, :], io["w_out"][4 * i + (k + 4)]).then_inc(w_in[k], 16)

        @block.tensor
        def _(pe):
            pe.wait_ge(mix_in, 16)
            with pe.Fori(0, 4) as i:
                for k in range(4):
                    pe.wait_ge(bank_free, 4 * i + k + 1)
                    pe.wait_ge(w_in[k], 16 * i + 16)
                    for half in range(2):
                        for kt in range(KT):
                            mm = nc.tensor.matmul(PS[:, 2 * (k % 2) + half, 0:TH], RING[:, k, P * kt:P * kt + P],
                                                  MIX[:, kt, TH * half:TH * half + TH], start=(kt == 0), stop=(kt == KT - 1))
                    mm.then_inc(tile_done, 1)
            norm.tensor(pe, x_ready, 1)

        @block.scalar
        def _(act):
            norm.scalar(act)

        @block.vector
        def _(dve):
            V = nc.vector
            dve.sem_inc(bank_free, 2)
            norm.start(dve)
            dve.wait_ge(x_in, 16)
            with dve.Fori(0, 4) as i:
                for k in range(4):
                    ct = 4 * i + k
                    tmp = TMP[:, k % 2]
                    ps = PS[:, 2 * (k % 2):2 * (k % 2) + 2, 0:TH]
                    dve.wait_ge(tile_done, 4 * i + k + 1)
                    V.tensor_scalar(tmp[:, 0:TH], ps[:, 0], MOD[:, bass.ds(ct + 2 * KT, 1), 0:1].rearrange("p c b -> p (c b)"),
                                    None, ALU.mult)
                    V.tensor_scalar(tmp[:, TH:SEQ], ps[:, 1, 0:SEQ - TH],
                                    MOD[:, bass.ds(ct + 2 * KT, 1), 0:1].rearrange("p c b -> p (c b)"), None, ALU.mult)
                    V.tensor_tensor(samples4(tmp[:, SEQ:T]), samples4(ps[:, 1, SEQ - TH:TH]),
                                    bcast(MOD[:, bass.ds(ct + 2 * KT, 1), 1:9].rearrange("p c b -> p (c b)"), 2, NS), ALU.mult)
                    dve.drain().then_inc(bank_free, 1)
                    x = XT[:, bass.ds(ct, 1), :].rearrange("p c t -> p (c t)")
                    V.scalar_tensor_tensor(x, x, ALPHA, tmp, ALU.mult, ALU.add).then_inc(x_ready, 1)
            dve.drain()
            norm.vector(dve, None)
            dve.drain()
            for kt in range(KT):
                V.tensor_scalar(H2[:, kt, 0:SEQ], XT[:, kt, 0:SEQ], MOD[:, 4 * KT + kt, 0:1], MOD[:, 3 * KT + kt, 0:1],
                                ALU.mult, ALU.add)
            xs = XT[:, :, SEQ:T].rearrange("p k (b s) -> p k b s", s=NS)
            hs = H2[:, :, SEQ:T].rearrange("p k (b s) -> p k b s", s=NS)
            V.tensor_tensor(hs, xs, bcast(MOD[:, 4 * KT:5 * KT, 1:9], 3, NS), ALU.mult)
            dve.drain()
            V.tensor_tensor(hs, hs, bcast(MOD[:, 3 * KT:4 * KT, 1:9], 3, NS), ALU.add)


NT = 5


def phase_route(nc, io, g, stack):
    m = Mem(nc, stack, "rt")
    PS, RING, H2, IDENT = g["PS"], g["RING"], g["HT"], g["IDENT"]
    RT = m.sb("RT", [P, 3, NT * P])
    g["RT"] = RT
    run(route_scores, nc, io, g)
    run(gate_tables, nc, io, g)


def route_scores(nc, io, g, stack):
    m = Mem(nc, stack, "sc")
    PS, RING, H2, IDENT, RT = g["PS"], g["RING"], g["HT"], g["IDENT"], g["RT"]
    KEYS = m.sb("KEYS", [P, 2, NK])
    QT = m.sb("QT", [P, 2, NT * P])
    SC = m.sb("SC", [P, NT, 16, NK])
    ST = m.sb("ST", [P, 16, NK])
    VV = m.sb("VV", [P, 16, TOPK])
    II = m.sb("II", [P, 16, TOPK], U32)
    IF = m.sb("IF", [P, 16, TOPK])
    CA = m.sb("CA", [P, HEADS, TOPK, TOPK])
    EQ = m.sb("EQ", [P, HEADS, TOPK, TOPK])
    SV = m.sb("SV", [P, HEADS, TOPK])
    SI = m.sb("SI", [P, HEADS, TOPK], U32)
    HL = m.sb("HL", [P, 2, HEADS, TOPK], U32)
    HF = m.sb("HF", [P, 2, HEADS, TOPK])
    EG = m.sb("EG", [P, 3, P])
    SM1 = m.sb("SM1", [P, HEADS])
    IO16 = m.sb("IO16", [P, TOPK])
    w_in = m.sems("w_in", 4)
    (keys_in, tile_done, bank_free, q_ready, q_free, sc_done, sc_free, sc_ready, iota_ready,
     ex_in, ex_ready, eg_ready, eg_done, rt_ready, cleared) = (m.sem(x) for x in (
        "keys_in tile_done bank_free q_ready q_free sc_done sc_free sc_ready iota_ready "
        "ex_in ex_ready eg_ready eg_done rt_ready cleared").split())

    with nc.Block() as block:
        @block.sync
        def _(sp):
            for k in range(4):
                sp.dma_start(RING[:, k, :], io["w_q"][k]).then_inc(w_in[k], 16)
            sp.dma_start(KEYS[:], io["keys"]).then_inc(keys_in, 16)
            with sp.Fori(0, 3) as i:
                for k in range(4):
                    sp.wait_ge(tile_done, 4 * i + k + 1)
                    sp.dma_start(RING[:, k, :], io["w_q"][4 * i + (k + 4)]).then_inc(w_in[k], 16)

        @block.tensor
        def _(pe):
            pe.wait_ge(keys_in, 16)
            with pe.Fori(0, 4) as i:
                for k in range(4):
                    n = 4 * i + k
                    pe.wait_ge(bank_free, n + 1)
                    pe.wait_ge(w_in[k], 16 * i + 16)
                    for half in range(2):
                        for kt in range(KT):
                            mm = nc.tensor.matmul(PS[:, 2 * (k % 2) + half, 0:TH], RING[:, k, P * kt:P * kt + P],
                                                  H2[:, kt, TH * half:TH * half + TH], start=(kt == 0), stop=(kt == KT - 1))
                    mm.then_inc(tile_done, 1)
                    pe.wait_ge(q_ready, n + 1)
                    pe.wait_ge(sc_free, n + 1)
                    for t in range(NT):
                        mm = nc.tensor.matmul(PS[:, 4 + t // 4, P * (t % 4):P * (t % 4) + P], QT[:, k % 2, P * t:P * t + P],
                                              KEYS[:, k % 2, :], start=True, stop=True)
                    mm.then_inc(sc_done, 1)
            for t in range(NT):
                pe.wait_ge(eg_ready, t + 1)
                pe.wait_ge(eg_done, t + 1)
                for j in range(3):
                    mm = nc.tensor.transpose(PS[:, 6, P * j:P * j + P], EG[:, j, :], IDENT[:])
                mm.then_inc(rt_ready, 1)

        @block.scalar
        def _(act):
            A = nc.scalar.activation
            act.sem_inc(bank_free, 2)
            act.sem_inc(sc_free, 1)
            act.sem_inc(eg_done, 1)
            act.wait_ge(cleared, 1)
            with act.Fori(0, 4) as i:
                for k in range(4):
                    n = 4 * i + k
                    act.wait_ge(tile_done, n + 1)
                    A(QT[:, k % 2, 0:T].rearrange("p (h n) -> p h n", h=2), PS[:, 2 * (k % 2):2 * (k % 2) + 2, 0:TH],
                      ACT.Copy).then_inc(q_ready, 1)
                    act.drain().then_inc(bank_free, 1)
                    act.wait_ge(sc_done, n + 1)
                    A(SC[:, 0:4, bass.ds(n, 1), :].rearrange("p t n k -> p t (n k)"),
                      PS[:, 4, :].rearrange("p (t k) -> p t k", t=4), ACT.Copy)
                    A(SC[:, 4, bass.ds(n, 1), :].rearrange("p n k -> p (n k)"), PS[:, 5, 0:P], ACT.Copy)
                    act.drain().then_inc(sc_free, 1)
            for t in range(NT):
                act.wait_ge(ex_in, t + 1)
                A(SV[:], SV[:], ACT.Exp).then_inc(ex_ready, 1)
                act.wait_ge(rt_ready, t + 1)
                A(RT[:, :, P * t:P * t + P], PS[:, 6, 0:3 * P].rearrange("p (j t) -> p j t", j=3), ACT.Copy)\
                    .then_inc(eg_done, 1)

        @block.gpsimd
        def _(pool):
            nc.gpsimd.iota(IO16[:], [[1, TOPK]], base=0, channel_multiplier=0,
                           allow_small_or_imprecise_dtypes=True).then_inc(iota_ready, 1)

        @block.vector
        def _(dve):
            V = nc.vector
            V.memset(QT[:], 0.0)
            dve.drain().then_inc(cleared, 1)
            dve.wait_ge(iota_ready, 1)
            dve.wait_ge(sc_free, 17)

            def best16(values, indices, data):
                for r in range(2):
                    V.max(values[r], data)
                    dve.drain()
                    V.max_index(indices[r], values[r], data)
                    if r == 0:
                        V.match_replace(data, values[r], data, NEG)
                        dve.drain()

            with dve.Fori(0, NT) as t:
                V.tensor_copy(ST[:], SC[:, bass.ds(t, 1)].rearrange("p t u k -> p (t u) k"))
                dve.drain()
                for u in range(16):
                    best16([VV[:, u, 0:8], VV[:, u, 8:16]], [II[:, u, 0:8], II[:, u, 8:16]], ST[:, u, :])
                dve.drain()
                v1 = VV[:].rearrange("p (h two) k -> p h two k", two=2)
                V.tensor_tensor(CA[:], bcast(v1[:, :, 0, :], 3, TOPK), bcast(v1[:, :, 1, :], 2, TOPK), ALU.add)
                V.tensor_copy(IF[:], II[:])
                dve.drain()
                for h in range(HEADS):
                    best16([SV[:, h, 0:8], SV[:, h, 8:16]], [SI[:, h, 0:8], SI[:, h, 8:16]],
                           CA[:, h].rearrange("p a b -> p (a b)"))
                dve.drain()
                V.tensor_scalar(HL[:, 0], SI[:], 4, None, ALU.logical_shift_right)
                V.tensor_scalar(HL[:, 1], SI[:], 15, None, ALU.bitwise_and)
                V.tensor_copy(SM1[:], SV[:, :, 0])
                dve.drain()
                V.tensor_tensor(SV[:], SV[:], bcast(SM1[:], 2, TOPK), ALU.subtract)
                V.tensor_copy(HF[:], HL[:])
                dve.drain().then_inc(ex_in, 1)
                dve.wait_ge(eg_done, t + 1)
                i1 = IF[:].rearrange("p (h two) k -> p h two k", two=2)
                for j in range(2):
                    V.tensor_tensor(EQ[:], bcast(HF[:, j], 3, TOPK), bcast(bcast(IO16[:], 1, TOPK), 1, HEADS), ALU.is_equal)
                    dve.drain()
                    V.tensor_tensor(EQ[:], EQ[:], bcast(i1[:, :, j, :], 2, TOPK), ALU.mult)
                    dve.drain()
                    V.tensor_reduce(EG[:, j, :].rearrange("p (h k) -> p h k", h=HEADS), EQ[:], AX.X, ALU.add)
                    dve.drain()
                dve.wait_ge(ex_ready, t + 1)
                V.tensor_reduce(SM1[:], SV[:], AX.X, ALU.add)
                dve.drain()
                V.reciprocal(SM1[:], SM1[:])
                dve.drain()
                V.tensor_tensor(EG[:, 2, :].rearrange("p (h k) -> p h k", h=HEADS), SV[:], bcast(SM1[:], 2, TOPK), ALU.mult)
                dve.drain().then_inc(eg_ready, 1)


def gate_tables(nc, io, g, stack):
    m = Mem(nc, stack, "gt")
    PS, RT = g["PS"], g["RT"]
    IOTA = m.sb("IOTA", [P, NK])
    BATCH = 4
    OH = m.sb("OH", [P, 2, 2, BATCH, NK])
    STG = m.sb("STG", [P, 2, NG, 16, JG])
    (iota_ready, oh_ready, oh_free, tab_done, bank_free, stg_ready) = (m.sem(x) for x in (
        "iota_ready oh_ready oh_free tab_done bank_free stg_ready").split())
    stored = m.sems("stored", 2)

    with nc.Block() as block:
        @block.gpsimd
        def _(pool):
            nc.gpsimd.iota(IOTA[:], [[1, NK]], base=0, channel_multiplier=0,
                           allow_small_or_imprecise_dtypes=True).then_inc(iota_ready, 1)

        @block.vector
        def _(dve):
            V = nc.vector
            dve.sem_inc(oh_free, 2)
            dve.wait_ge(iota_ready, 1)
            with dve.Fori(0, T // (2 * BATCH)) as i:
                for b in range(2):
                    dve.wait_ge(oh_free, 2 * i + b + 1)
                    for q in range(BATCH):
                        at = bass.ds(2 * BATCH * i + (BATCH * b + q), 1)
                        V.tensor_scalar(OH[:, b, 0, q, :], IOTA[:], RT[:, 0, at], RT[:, 2, at], ALU.is_equal, ALU.mult)
                        last = V.tensor_scalar(OH[:, b, 1, q, :], IOTA[:], RT[:, 1, at], None, ALU.is_equal)
                    last.then_inc(oh_ready, 1)

        @block.tensor
        def _(pe):
            with pe.Fori(0, T // (2 * BATCH)) as i:
                for b in range(2):
                    pe.wait_ge(bank_free, 2 * i + b + 1)
                    pe.wait_ge(oh_ready, 2 * i + b + 1)
                    for q in range(BATCH):
                        mm = nc.tensor.matmul(PS[:, b, NK * q:NK * q + NK], OH[:, b, 0, q, :], OH[:, b, 1, q, :],
                                              start=True, stop=True)
                    mm.then_inc(tab_done, 1)

        @block.scalar
        def _(act):
            A = nc.scalar.activation
            act.sem_inc(bank_free, 2)

            def sixteen(i, half, first=False):
                if not first:
                    act.wait_ge(stored[half], 16 * i)
                for b in range(4):
                    act.wait_ge(tab_done, 8 * i + (4 * half + b + 1))
                    A(STG[:, half].rearrange("p g t j -> p t g j")[:, BATCH * b:BATCH * b + BATCH],
                      PS[:, b % 2, :].rearrange("p (t g j) -> p t g j", t=BATCH, g=NG), ACT.Copy).then_inc(bank_free, 1)
                    act.sem_inc(oh_free, 1)
                act.drain().then_inc(stg_ready, 1)

            for half in range(2):
                sixteen(0, half, first=True)
            with act.Fori(1, T // 32) as i:
                for half in range(2):
                    sixteen(i, half)

        @block.sync
        def _(sp):
            gd = io["gd"].rearrange("g p t j -> p g t j")
            with sp.Fori(0, T // 32) as i:
                for half in range(2):
                    sp.wait_ge(stg_ready, 2 * i + half + 1)
                    sp.dma_start(gd[:, :, bass.ds(32 * i + 16 * half, 16), :].rearrange("p g t j -> p g (t j)"),
                                 STG[:, half].rearrange("p g t j -> p g (t j)")).then_inc(stored[half], 16)
            for half in range(2):
                sp.wait_ge(stored[half], 16 * (T // 32))


def phase_experts(nc, io, g, stack):
    m = Mem(nc, stack, "ex")
    PS, RING, H2, YA = g["PS"], g["RING"], g["HT"], g["YA"]
    GG = m.sb("GG", [P, 2, T, JG])
    HB = m.sb("HB", [P, JG, T])
    GE = m.sb("GE", [P, 2, T])
    w_in = m.sems("w_in", 4)
    g_in = m.sems("g_in", 2)
    (u_done, ge_ready, ge_free, ge_used, hb_ready, v_done, ya_ready, gg_free, bank_free) = (m.sem(x) for x in (
        "u_done ge_ready ge_free ge_used hb_ready v_done ya_ready gg_free bank_free").split())
    PER = 16

    with nc.Block() as block:
        @block.sync
        def _(sp):
            def load(slot, src):
                sp.dma_start(RING[:, slot, :], src).then_inc(w_in[slot], 16)

            def group(gi, par, last=False):
                for n in range(4, PER + 4):
                    if n < 12:
                        sp.wait_ge(u_done, 8 * gi + (n - 3))
                    else:
                        sp.wait_ge(v_done, 8 * gi + (n - 11))
                    if n < 8:
                        load(n % 4, io["peer_u"][8 * gi + n])
                    elif n < PER:
                        load(n % 4, io["peer_v"][gi, n - 8])
                    elif not last:
                        load(n % 4, io["peer_u"][8 * gi + (8 + n - PER)])
                    if n == 8 and not last:
                        sp.wait_ge(gg_free, gi + 1)
                        sp.dma_start(GG[:, 1 - par], io["gd"][gi + 1]).then_inc(g_in[1 - par], 16)

            for k in range(4):
                load(k, io["peer_u"][k])
            sp.dma_start(GG[:, 0], io["gd"][0]).then_inc(g_in[0], 16)
            with sp.Fori(0, NG // 2 - 1) as i:
                for par in range(2):
                    group(2 * i + par, par)
            group(NG - 2, 0)
            group(NG - 1, 1, last=True)

        @block.tensor
        def _(pe):
            with pe.Fori(0, NG) as gi:
                for j in range(JG):
                    pe.wait_ge(ge_free, 8 * gi + (j + 1))
                    pe.wait_ge(w_in[j % 4], 64 * gi + (16 * (j // 4) + 16))
                    for half in range(2):
                        for kt in range(KT):
                            mm = nc.tensor.matmul(PS[:, 2 * (j % 2) + half, 0:TH], RING[:, j % 4, P * kt:P * kt + P],
                                                  H2[:, kt, TH * half:TH * half + TH], start=(kt == 0), stop=(kt == KT - 1))
                    mm.then_inc(u_done, 1)
                for dp in range(8):
                    pe.wait_ge(w_in[dp % 4], 64 * gi + (16 * (dp // 4) + 48))
                    for dd in range(2):
                        ct = 2 * dp + dd
                        pe.wait_ge(bank_free, 16 * gi + (ct + 1))
                        for half in range(2):
                            for j in range(JG):
                                if ct == 0 and half == 0:
                                    pe.wait_ge(hb_ready, 8 * gi + (j + 1))
                                mm = nc.tensor.matmul(PS[:, 4 + 2 * (ct % 2) + half, 0:TH],
                                                      RING[:, dp % 4, 256 * j + P * dd:256 * j + P * dd + P],
                                                      HB[:, j, TH * half:TH * half + TH], start=(j == 0), stop=(j == JG - 1))
                        if dd == 0:
                            mm.then_inc(ya_ready, 1)
                    mm.then_inc(v_done, 1)

        @block.scalar
        def _(act):
            act.sem_inc(ge_free, 2)
            with act.Fori(0, NG) as gi:
                for j in range(JG):
                    act.wait_ge(u_done, 8 * gi + (j + 1))
                    act.wait_ge(ge_used, 8 * gi + (j + 1))
                    nc.scalar.activation(GE[:, j % 2].rearrange("p (h n) -> p h n", h=2),
                                         PS[:, 2 * (j % 2):2 * (j % 2) + 2, 0:TH], ACT.Gelu_apprx_tanh).then_inc(ge_ready, 1)
                    act.drain().then_inc(ge_free, 1)

        @block.vector
        def _(dve):
            V = nc.vector
            V.memset(YA[:], 0.0)
            dve.sem_inc(bank_free, 2)
            dve.sem_inc(ge_used, 2)
            dve.sem_inc(gg_free, 1)
            dve.drain()
            with dve.Fori(0, NG // 2) as i:
                for par in range(2):
                    dve.wait_ge(g_in[par], 16 * i + 16)
                    for j in range(JG):
                        dve.wait_ge(ge_ready, 16 * i + (8 * par + j + 1))
                        V.tensor_tensor(HB[:, j, :], GE[:, j % 2], GG[:, par, :, j], ALU.mult).then_inc(hb_ready, 1)
                        dve.drain().then_inc(ge_used, 1)
                    dve.sem_inc(gg_free, 1)
                    for ct in range(KT):
                        if ct % 2 == 0:
                            dve.wait_ge(ya_ready, 16 * i + (8 * par + ct // 2 + 1))
                        else:
                            dve.wait_ge(v_done, 16 * i + (8 * par + ct // 2 + 1))
                        V.tensor_tensor(YA[:, ct, :].rearrange("p (h n) -> p h n", h=2),
                                        YA[:, ct, :].rearrange("p (h n) -> p h n", h=2),
                                        PS[:, 4 + 2 * (ct % 2):6 + 2 * (ct % 2), 0:TH], ALU.add).then_inc(bank_free, 1)


def phase_final(nc, io, g, stack):
    m = Mem(nc, stack, "fin")
    MOD, XT, YA = g["MOD"], g["XT"], g["YA"]
    norm = Norm(nc, m, g, XT, "ln2_w", "ln2_b")
    x_ready, y_ready, y_out = m.sem("x_ready"), m.sem("y_ready"), m.sem("y_out")

    with nc.Block() as block:
        @block.tensor
        def _(pe):
            norm.tensor(pe, x_ready, 1)

        @block.scalar
        def _(act):
            norm.scalar(act)

        @block.vector
        def _(dve):
            V = nc.vector
            norm.start(dve)
            for kt in range(KT):
                V.tensor_scalar(YA[:, kt, 0:SEQ], YA[:, kt, 0:SEQ], MOD[:, 5 * KT + kt, 0:1], None, ALU.mult)
            ys = YA[:, :, SEQ:T].rearrange("p k (b s) -> p k b s", s=NS)
            V.tensor_tensor(ys, ys, bcast(MOD[:, 5 * KT:6 * KT, 1:9], 3, NS), ALU.mult)
            dve.drain()
            for kt in range(KT):
                V.scalar_tensor_tensor(XT[:, kt, :], XT[:, kt, :], ALPHA, YA[:, kt, :], ALU.mult, ALU.add)\
                    .then_inc(x_ready, 1)
            dve.drain()
            norm.vector(dve, lambda kt: dve.drain().then_inc(y_ready, 1) if kt % 4 == 3 else None)

        @block.sync
        def _(sp):
            for q in range(4):
                sp.wait_ge(y_ready, q + 1)
                sp.dma_start(io["y"][:, 4 * q:4 * q + 4, :], XT[:, 4 * q:4 * q + 4, :]).then_inc(y_out, 16)
            sp.wait_ge(y_out, 64)


def phase_rest(nc, io, g):
    with ExitStack() as tail:
        m = Mem(nc, tail, "tail")
        g["XT"] = m.sb("XT", [P, KT, T])
        run(phase_out, nc, io, g)
        run(phase_route, nc, io, g)
        g["YA"] = m.sb("YA", [P, KT, T])
        run(phase_experts, nc, io, g)
        run(phase_final, nc, io, g)


def program(nc, io):
    with ExitStack() as top:
        m = Mem(nc, top, "all")
        g = {
            "PS": top.enter_context(nc.psum_tensor("PS", [P, 8, 512], F32)),
            "RING": m.sb("RING", [P, 4, D]),
            "HT": m.sb("HT", [P, KT, TP]),
            "MOD": m.sb("MOD", [P, ADA, 9]),
            "PARAM": m.sb("PARAM", [P, NPAR]),
            "IDENT": m.sb("IDENT", [P, P]),
            "EPSG": m.sb("EPSG", [P, 2]),
        }
        run(phase_ada, nc, io, g)
        with ExitStack() as mixer:
            mx = Mem(nc, mixer, "mix")
            g.update({
                "LR": mx.sb("LR", [P, 2, W1]), "BD": mx.sb("BD", [P, P]), "MASK": mx.sb("MASK", [P, 4, P]),
                "LM": mx.sb("LM", [P, 5, P]), "SM": mx.sb("SM", [P, W1]), "SP8": mx.sb("SP8", [P, 2, 8]),
            })
            run(phase_lru, nc, io, g)
            run(phase_rwkv, nc, io, g)
        phase_rest(nc, io, g)


INPUTS = {
    "xT": (P, KT, T), "cT": (P, KT, 9), "shiftT": (P, KT, NB), "w_ada": (ADA, P, D), "b_ada": (P, ADA),
    "par": (P, NPAR), "w_in": (42, P, D), "w_gate": (8, P, 2, 64), "lru0": (P, 8, 8), "conv0": (P, 8, 24),
    "w_lr": (8, P, 2, P), "wkv0": (8, P, NB, 64), "w_out": (KT, P, D), "w_q": (KT, P, D), "keys": (P, 2, NK),
    "peer_u": (NK, P, D), "peer_v": (NG, 8, P, D),
}
OUTPUTS = {
    "y": (P, KT, T), "shift_out": (P, KT, 9), "wkv_p": (8, P, 64), "wkv_s": (8, P, NB, 64), "lru_out": (P, 8, 9),
    "conv_out": (P, 8, 27),
}
SCRATCH = {"mix": (KT, P, T), "gd": (NG, P, T, JG)}


def laid_out(i):
    import numpy as np

    def cols(v):
        return v.reshape(-1, P).T

    def tiles(w):
        k, c = w.shape
        return w.reshape(k // P, P, c // P, P).transpose(2, 1, 0, 3).reshape(c // P, P, -1)

    def chan(x):
        return x.T.reshape(-1, P, x.shape[0]).transpose(1, 0, 2)

    x = np.concatenate([i["x_prompt"][0], i["x_sample"].reshape(NB * NS, D)])
    c = np.concatenate([i["c_prompt"], i["c_sample"]])
    par = np.concatenate([cols(i[n][0].reshape(-1)) for n in (
        "mu_shift", "w0", "a0", "k_k", "k_a", "r_k", "lnx_w", "lnx_b", "conv_w", "conv_b", "b_gate_a", "b_gate_i",
        "lru_lambda", "ln1_w", "ln1_b", "ln2_w", "ln2_b")], axis=1)
    out = {
        "xT": chan(x), "cT": chan(c), "shiftT": chan(i["state_shift"][0]), "w_ada": tiles(i["w_ada"][0]),
        "b_ada": cols(i["b_ada"][0]), "par": par, "w_in": tiles(i["w_in"][0]),
        "w_gate": np.stack([i["w_gate_a"][0].reshape(8, P, 64), i["w_gate_i"][0].reshape(8, P, 64)], axis=2),
        "lru0": chan(i["state_lru"][0]),
        "conv0": chan(i["state_conv"][0].reshape(NB * 3, DA)),
        "w_lr": np.stack([np.concatenate([i["w_w2"][0], i["w_a2"][0]]).reshape(P, 8, P),
                          i["w_g2"][0].reshape(P, 8, P)], axis=2).transpose(1, 0, 2, 3),
        "wkv0": i["state_wkv"][0].transpose(1, 3, 0, 2).reshape(8, P, NB, 64),
        "w_out": tiles(i["w_out"][0]), "w_q": tiles(i["w_q"][0]),
        "keys": i["sub_keys"][0].transpose(2, 0, 1),
        "peer_u": i["peer_u"][0].reshape(P, NK, KT, P).transpose(1, 3, 2, 0).reshape(NK, P, D),
        "peer_v": i["peer_v"][0].reshape(P, NG, JG, 8, 256).transpose(1, 3, 0, 2, 4).reshape(NG, 8, P, D),
    }
    return {k: np.ascontiguousarray(v) for k, v in out.items()}


def gathered(o):
    def rows(x):
        return x.transpose(2, 1, 0).reshape(x.shape[2], -1)

    y, sh = rows(o["y"]), rows(o["shift_out"])
    lru, conv = rows(o["lru_out"]), rows(o["conv_out"]).reshape(9, 3, DA)
    wp = o["wkv_p"].reshape(16, 64, 64).transpose(0, 2, 1)
    ws = o["wkv_s"].reshape(16, 64, NB, 64).transpose(2, 0, 3, 1)
    return (y[None, :SEQ], y[SEQ:].reshape(NB, NS, D), sh[None, :1], wp[None, None], lru[None, :1], conv[None, :1],
            sh[None, 1:], ws[None], lru[None, 1:], conv[None, 1:])


def kernel(**inputs):
    import numpy as np
    import concourse.bacc as bacc
    from concourse.bass_utils import run_bass_kernel_spmd

    arrays = {f"in_{k}": v for k, v in laid_out({k: np.asarray(v) for k, v in inputs.items()}).items()}
    nc = bacc.Bacc("TRN2", target_bir_lowering=False, num_devices=1)
    io = {k: nc.dram_tensor(f"in_{k}", s, F32, kind="ExternalInput").ap() for k, s in INPUTS.items()}
    io.update({k: nc.dram_tensor(f"out_{k}", s, F32, kind="ExternalOutput").ap() for k, s in OUTPUTS.items()})
    io.update({k: nc.dram_tensor(f"tmp_{k}", s, F32).ap() for k, s in SCRATCH.items()})
    program(nc, io)
    r = run_bass_kernel_spmd(nc, [arrays], core_ids=[0]).results[0]
    return tuple(np.ascontiguousarray(x) for x in gathered({k: np.asarray(r[f"out_{k}"]) for k in OUTPUTS}))
```

```python
import concourse.bass as bass
from concourse import mybir
from concourse.alu_op_type import AluOpType as ALU
from contextlib import ExitStack

F32 = mybir.dt.float32
U32 = mybir.dt.uint32
I32 = mybir.dt.int32
ACT = mybir.ActivationFunctionType
AX = mybir.AxisListType

P = 128
D = 2048
KT = D // P
SEQ = 512
NB, NS = 8, 4
T = SEQ + NB * NS
TH = T // 2
TP = SEQ + NB * (NS + 1)
SP5 = NB * (NS + 1)
TPH = TP // 2
PB = SEQ - TPH
W1 = TP + 1
DA = 1024
NPAIR = DA // P
ADA = 6 * KT
ADA_H = 2 * KT
ADA_PAIR = 8
CH_CHUNK = 32
NK = 128
HEADS, TOPK = 8, 16
JG = 8
NG = NK // JG
ALPHA = 2.0 ** 0.25
LN_EPS, GN_EPS = 1e-5, 64e-5
EXP_HALF = 0.6065306597126334
C_LRU = 8.0
NEG = -3.0e38

PAR_SIZES = [("mu", 26), ("w0", 8), ("a0", 8), ("k_k", 8), ("k_a", 8), ("r_k", 8), ("lnx_w", 8), ("lnx_b", 8),
             ("conv_w", 32), ("conv_b", 8), ("b_ga", 8), ("b_gi", 8), ("lam", 8),
             ("ln1_w", 16), ("ln1_b", 16), ("ln2_w", 16), ("ln2_b", 16)]
PAR = {}
_at = 0
for _n, _s in PAR_SIZES:
    PAR[_n] = _at
    _at += _s
NPAR = _at


def samples5(ap, lo=1):
    return ap.rearrange("p (b s) -> p b s", s=NS + 1)[:, :, lo:NS + 1]


def halves(ap):
    return ap.rearrange("p (h n) -> p h n", h=2)


def samples4(ap):
    return ap.rearrange("p (b s) -> p b s", s=NS)


def bcast(ap, axis, n):
    v = ap.unsqueeze(axis)
    shape = list(v.shape)
    shape[axis] = n
    return v.broadcast_to(shape)


class Mem:

    used = []

    def __init__(self, nc, stack, tag):
        self.nc, self.stack, self.tag = nc, stack, tag

    def sb(self, name, shape, dt=F32):
        return self.stack.enter_context(self.nc.sbuf_tensor(f"{self.tag}_{name}", shape, dt))

    def sem(self, name):
        s = self.stack.enter_context(self.nc.semaphore(f"{self.tag}_{name}"))
        Mem.used.append(s)
        return s

    def sems(self, name, n):
        return [self.sem(f"{name}{i}") for i in range(n)]


def run(phase, nc, io, g):
    with ExitStack() as stack:
        Mem.used = []
        phase(nc, io, g, stack)
        with nc.Block() as block:
            @block.sync
            def _(sp):
                for s in Mem.used:
                    sp.sem_clear(s)


def phase_ada(nc, io, g, stack):
    m = Mem(nc, stack, "ada")
    PS, RING, HT, MOD, PARAM, CS, BADA = (g[x] for x in ("PS", "RING", "HT", "MOD", "PARAM", "CS", "BADA"))
    IDENT = g["IDENT"]
    XT = m.sb("XT", [P, KT, T])
    MR = m.sb("MR", [9, 2, 4 * P])
    CT = m.sb("CT", [P, KT, 9])
    SHT = m.sb("SHT", [P, KT, NB])
    SHO = m.sb("SHO", [P, KT, 9])
    c_in, x_in, b_in, out_sem = m.sem("c_in"), m.sem("x_in"), m.sem("b_in"), m.sem("out")
    w_in = m.sems("w_in", 4)
    (tile_done, sig_ready, cs_ready, bank_free, rows_ready, turned, turned_free, ident_ready, h_ready) = (m.sem(x) for x in (
        "tile_done sig_ready cs_ready bank_free rows_ready turned turned_free ident_ready h_ready").split())

    with nc.Block() as block:
        @block.sync
        def _(sp):
            sp.dma_start(CT[:], io["cT"]).then_inc(c_in, 16)
            for k in range(4):
                sp.dma_start(RING[:, k, :], io["w_ada"][k]).then_inc(w_in[k], 16)
            sp.dma_start(BADA[:], io["b_ada"]).then_inc(b_in, 16)
            sp.dma_start(XT[:], io["xT"]).then_inc(x_in, 16)
            sp.dma_start(SHT[:], io["shiftT"]).then_inc(x_in, 16)
            sp.dma_start(PARAM[:], io["par"]).then_inc(x_in, 16)
            with sp.Fori(0, ADA_H // 4 - 1) as i:
                for k in range(4):
                    sp.wait_ge(tile_done, 4 * i + k + 1)
                    sp.dma_start(RING[:, k, :], io["w_ada"][4 * i + (4 + k)]).then_inc(w_in[k], 16)
            sp.wait_ge(h_ready, 1)
            sp.dma_start(io["shift_out"], SHO[:]).then_inc(out_sem, 16)
            sp.wait_ge(out_sem, 16)

        @block.scalar
        def _(act):
            act.wait_ge(c_in, 16)
            nc.scalar.activation(CS[:], CT[:], ACT.Sigmoid).then_inc(sig_ready, 1)
            act.sem_inc(bank_free, 2)
            with act.Fori(0, ADA_H // 8) as i:
                for b in range(2):
                    act.wait_ge(tile_done, 8 * i + 4 * b + 4)
                    nc.scalar.activation(MR[:, b, :], PS[0:9, b, :], ACT.Copy).then_inc(rows_ready, 1)
                    act.drain().then_inc(bank_free, 1)

        @block.gpsimd
        def _(pool):
            nc.gpsimd.memset(IDENT[:], 0.0)
            pool.drain()
            nc.gpsimd.affine_select(out=IDENT[:], in_=IDENT[:], compare_op=ALU.not_equal, fill=1.0, base=0,
                                    pattern=[[-1, P]], channel_multiplier=1)
            pool.drain().then_inc(ident_ready, 1)

        @block.tensor
        def _(pe):
            def group(i, b):
                pe.wait_ge(bank_free, 2 * i + b + 1)
                for c in range(4):
                    pe.wait_ge(w_in[c], 32 * i + (16 * b + 16))
                    for k in range(KT):
                        mm = nc.tensor.matmul(PS[0:9, b, P * c:P * c + P], CS[:, k, :], RING[:, c, P * k:P * k + P],
                                              start=(k == 0), stop=(k == KT - 1))
                    mm.then_inc(tile_done, 1)

            def turn(i, b):
                pe.wait_ge(rows_ready, 2 * i + b + 1)
                pe.wait_ge(turned_free, 2 * i + b + 1)
                for c in range(4):
                    mm = nc.tensor.matmul(PS[:, 2 + b, 9 * c:9 * c + 9], MR[:, b, P * c:P * c + P], IDENT[0:9, 0:9],
                                          start=True, stop=True)
                mm.then_inc(turned, 1)

            pe.wait_ge(cs_ready, 1)
            pe.wait_ge(ident_ready, 1)
            group(0, 0)
            with pe.Fori(0, ADA_H // 8 - 1) as i:
                group(i, 1)
                turn(i, 0)
                group(i + 1, 0)
                turn(i, 1)
            group(ADA_H // 8 - 1, 1)
            for b in range(2):
                turn(ADA_H // 8 - 1, b)

        @block.vector
        def _(dve):
            dve.sem_inc(turned_free, 2)
            dve.wait_ge(sig_ready, 1)
            nc.vector.tensor_tensor(CS[:], CS[:], CT[:], ALU.mult).then_inc(cs_ready, 1)
            dve.wait_ge(b_in, 16)
            dve.wait_ge(x_in, 48)
            nc.vector.tensor_copy(HT[:, :, SEQ:TP].rearrange("p k (b s) -> p k b s", s=NS + 1)[:, :, :, 0], SHT[:])
            with dve.Fori(0, ADA_H // 8) as i:
                for b in range(2):
                    dve.wait_ge(turned, 2 * i + b + 1)
                    at = bass.ds(8 * i + 4 * b, 4)
                    nc.vector.tensor_tensor(MOD[:, at, :], PS[:, 2 + b, 0:36].rearrange("p (c b) -> p c b", b=9),
                                            bcast(BADA[:, at], 2, 9), ALU.add).then_inc(turned_free, 1)
            dve.drain()
            nc.vector.tensor_scalar(MOD[:, KT:2 * KT, :], MOD[:, KT:2 * KT, :], 1.0, None, ALU.add)
            dve.drain()
            for k in range(KT):
                nc.vector.tensor_scalar(HT[:, k, 0:SEQ], XT[:, k, 0:SEQ], MOD[:, KT + k, 0:1], MOD[:, k, 0:1],
                                        ALU.mult, ALU.add)
            hs = HT[:, :, SEQ:TP].rearrange("p k (b s) -> p k b s", s=NS + 1)[:, :, :, 1:NS + 1]
            xs = XT[:, :, SEQ:T].rearrange("p k (b s) -> p k b s", s=NS)
            nc.vector.tensor_tensor(hs, xs, bcast(MOD[:, KT:2 * KT, 1:9], 3, NS), ALU.mult)
            dve.drain()
            nc.vector.tensor_tensor(hs, hs, bcast(MOD[:, 0:KT, 1:9], 3, NS), ALU.add)
            dve.drain()
            nc.vector.tensor_copy(SHO[:, :, 0:1], HT[:, :, SEQ - 1:SEQ])
            nc.vector.tensor_copy(SHO[:, :, 1:9],
                                  HT[:, :, SEQ:TP].rearrange("p k (b s) -> p k b s", s=NS + 1)[:, :, :, NS]).then_inc(h_ready, 1)


def phase_lru(nc, io, g, stack):
    m = Mem(nc, stack, "lru")
    PS, RING, HT, PARAM, LR = g["PS"], g["RING"], g["HT"], g["PARAM"], g["LR"]
    IDENT, BD, MASK, LM, SM, EPSG = (g[x] for x in ("IDENT", "BD", "MASK", "LM", "SM", "EPSG"))
    WG = m.sb("WG", [P, 2, 2, P])
    XP = m.sb("XP", [P, 2, 3 + SEQ + NB * 7])
    XC = m.sb("XC", [P, T])
    RG, IG, AA, TT, QQ, HS, GE = (m.sb(x, [P, T]) for x in ("RG", "IG", "AA", "TT", "QQ", "HS", "GE"))
    YB = m.sb("YB", [P, T])
    LRU0 = m.sb("LRU0", [P, 8, 8])
    CONV0 = m.sb("CONV0", [P, 8, 24])
    LRUO = m.sb("LRUO", [P, 8, 9])
    CVO = m.sb("CVO", [P, 8, 27])
    SPL = m.sb("SPL", [P, 4, 8])
    PT = m.sb("PT", [P, 2, W1])
    DT = m.sb("DT", [P, W1])
    IA = m.sb("IA", [P, 2, P], I32)
    IB = m.sb("IB", [P, 2, P], I32)
    BK = m.sb("BK", [P, 6, P])
    TMPS = m.sb("TMPS", [P, NB])
    st_in, out_sem, y_out = m.sem("st_in"), m.sem("out"), m.sem("y_out")
    w_in = m.sems("w_in", 4)
    wg_in = m.sems("wg_in", 2)
    names = ("slot_used", "wg_used", "lr_mm", "lr_ev", "lr_shift", "px_done", "pg_done", "px_free", "pg_free",
             "xp_ready", "xc_ready", "gates_done", "gates_free", "sig_ready", "a_ready", "q_ready", "s_ready",
             "ge_ready", "tile_done", "y_ready", "iota_ready", "sp_a", "sp_b", "sp_c")
    (slot_used, wg_used, lr_mm, lr_ev, lr_shift, px_done, pg_done, px_free, pg_free, xp_ready, xc_ready,
     gates_done, gates_free, sig_ready, a_ready, q_ready, s_ready, ge_ready, tile_done, y_ready, iota_ready,
     sp_a, sp_b, sp_c) = (m.sem(x) for x in names)
    y_free, cleared = m.sem("y_free"), m.sem("cleared")
    N0 = 24

    with nc.Block() as block:
        def load_gates(sp, i, slot):
            for blk in range(2):
                rows = slice(64 * blk, 64 * blk + 64)
                sp.dma_start(WG[rows, slot, :, rows], io["w_gate"][i][rows]).then_inc(wg_in[slot], 16)

        @block.sync
        def _(sp):
            for k in range(2):
                sp.dma_start(RING[:, k, :], io["w_in"][N0 + k]).then_inc(w_in[k], 16)
            sp.dma_start(LRU0[:], io["lru0"]).then_inc(st_in, 16)
            sp.dma_start(CONV0[:], io["conv0"]).then_inc(st_in, 16)
            for k in range(2):
                sp.dma_start(RING[:, 2 + k, :], io["w_in"][26 + 8 * k]).then_inc(w_in[2 + k], 16)
            sp.wait_ge(cleared, 1)
            load_gates(sp, 0, 0)
            for k in range(2):
                sp.wait_ge(slot_used, k + 1)
                sp.dma_start(RING[:, k, :], io["w_in"][27 + 8 * k]).then_inc(w_in[k], 16)
            load_gates(sp, 1, 1)
            with sp.Fori(0, 3) as j:
                for odd in range(2):
                    for k in range(2):
                        slot = 2 * (1 - odd) + k
                        sp.wait_ge(slot_used, 4 * j + (2 * odd + k + 3))
                        sp.dma_start(RING[:, slot, :], io["w_in"][2 * j + (28 + odd + 8 * k)]).then_inc(w_in[slot], 16)
                    sp.wait_ge(wg_used, 2 * j + odd + 1)
                    load_gates(sp, 2 * j + 2 + odd, odd)
            sp.wait_ge(tile_done, 9)
            sp.dma_start(io["lru_out"], LRUO[:]).then_inc(out_sem, 16)
            sp.dma_start(io["conv_out"], CVO[:]).then_inc(out_sem, 16)
            sp.wait_ge(out_sem, 32)

        def lr_project(pe, k):
            pe.wait_ge(w_in[k], 16)
            for half in range(2):
                for kt in range(KT):
                    mm = nc.tensor.matmul(PS[:, 2 * k + half, 0:TPH], RING[:, k, P * kt:P * kt + P],
                                          HT[:, kt, TPH * half:TPH * half + TPH], start=(kt == 0), stop=(kt == KT - 1))
            mm.then_inc(slot_used, 1)
            pe.drain().then_inc(lr_mm, 1)

        @block.tensor
        def _(pe):
            for k in range(2):
                lr_project(pe, k)

            def project(j, odd, k):
                free, done = ((px_free, px_done), (pg_free, pg_done))[k]
                slot = 2 * (1 - odd) + k
                pe.wait_ge(free, 2 * j + odd + 1)
                pe.wait_ge(w_in[slot], 16 * j + (32 if odd else 16))
                for half in range(2):
                    for kt in range(KT):
                        mm = nc.tensor.matmul(PS[:, 2 * k + half, 0:TPH], RING[:, slot, P * kt:P * kt + P],
                                              HT[:, kt, TPH * half:TPH * half + TPH], start=(kt == 0), stop=(kt == KT - 1))
                mm.then_inc(slot_used, 1)
                pe.drain().then_inc(done, 1)

            def gates(j, odd):
                pe.wait_ge(xc_ready, 2 * j + odd + 1)
                pe.wait_ge(wg_in[odd], 32 * j + 32)
                pe.wait_ge(gates_free, 2 * j + odd + 1)
                for gate in range(2):
                    for half in range(2):
                        mm = nc.tensor.matmul(PS[:, 4 + 2 * gate + half, 0:TH], WG[:, odd, gate, :],
                                              XC[:, TH * half:TH * half + TH], start=True, stop=True)
                mm.then_inc(wg_used, 1)
                pe.drain().then_inc(gates_done, 1)

            project(0, 0, 0)
            project(0, 0, 1)
            with pe.Fori(0, 3) as j:
                project(j, 1, 0)
                gates(j, 0)
                project(j, 1, 1)
                project(j + 1, 0, 0)
                gates(j, 1)
                project(j + 1, 0, 1)
            project(3, 1, 0)
            gates(3, 0)
            project(3, 1, 1)
            gates(3, 1)

        @block.scalar
        def _(act):
            act.wait_ge(cleared, 1)
            for k in range(2):
                act.wait_ge(lr_mm, k + 1)
                nc.scalar.activation(halves(PT[:, k, 1:W1]), PS[:, 2 * k:2 * k + 2, 0:TPH], ACT.Copy).then_inc(lr_ev, 1)
            act.drain().then_inc(px_free, 1)
            act.sem_inc(pg_free, 1)
            act.sem_inc(gates_free, 1)
            act.wait_ge(lr_shift, 2)
            nc.scalar.activation(LR[0:64, 0, 1:W1], LR[0:64, 0, 1:W1], ACT.Tanh)
            nc.scalar.activation(LR[:, 1, 1:W1], LR[:, 1, 1:W1], ACT.Sigmoid)
            act.wait_ge(sp_a, 1)
            nc.scalar.activation(SPL[:, 1], SPL[:, 0], ACT.Exp, scale=-1.0).then_inc(sp_b, 1)
            act.wait_ge(sp_a, 2)
            nc.scalar.activation(SPL[:, 3], SPL[:, 2], ACT.Ln).then_inc(sp_b, 1)

            def x_branch(i, par):
                act.wait_ge(px_done, i + 1)
                nc.scalar.activation(XP[:, par, 3:3 + TPH], PS[:, 0, 0:TPH], ACT.Copy)
                nc.scalar.activation(XP[:, par, 3 + TPH:3 + SEQ], PS[:, 1, 0:PB], ACT.Copy)
                nc.scalar.activation(XP[:, par, 3 + SEQ:].rearrange("p (b s) -> p b s", s=7)[:, :, 3:7],
                                     samples5(PS[:, 1, PB:TPH]), ACT.Copy).then_inc(xp_ready, 1)
                act.drain().then_inc(px_free, 1)

            def gate_branch(i):
                act.wait_ge(pg_done, i + 1)
                act.wait_ge(tile_done, i + 1)
                nc.scalar.activation(GE[:, 0:TPH], PS[:, 2, 0:TPH], ACT.Gelu_apprx_tanh)
                nc.scalar.activation(GE[:, TPH:SEQ], PS[:, 3, 0:PB], ACT.Gelu_apprx_tanh)
                nc.scalar.activation(samples4(GE[:, SEQ:T]), samples5(PS[:, 3, PB:TPH]),
                                     ACT.Gelu_apprx_tanh).then_inc(ge_ready, 1)
                act.drain().then_inc(pg_free, 1)

            def tile(i, par, last=False):
                act.wait_ge(gates_done, i + 1)
                nc.scalar.activation(RG[:].rearrange("p (h n) -> p h n", h=2), PS[:, 4:6, 0:TH], ACT.Sigmoid,
                                     bias=PARAM[:, bass.ds(i + PAR["b_ga"], 1)])
                nc.scalar.activation(IG[:].rearrange("p (h n) -> p h n", h=2), PS[:, 6:8, 0:TH], ACT.Sigmoid,
                                     bias=PARAM[:, bass.ds(i + PAR["b_gi"], 1)]).then_inc(sig_ready, 1)
                act.drain().then_inc(gates_free, 1)
                act.wait_ge(sp_c, 1)
                nc.scalar.activation(TT[:], RG[:], ACT.Tanh, scale=g["SP8"][:, 0, bass.ds(i, 1)]).then_inc(a_ready, 1)
                nc.scalar.activation(AA[:], RG[:], ACT.Exp, scale=g["SP8"][:, 1, bass.ds(i, 1)]).then_inc(a_ready, 1)
                if not last:
                    x_branch(i + 1, 1 - par)
                act.wait_ge(q_ready, i + 1)
                nc.scalar.activation(QQ[:], QQ[:], ACT.Sqrt).then_inc(s_ready, 1)
                if not last:
                    gate_branch(i + 1)

            x_branch(0, 0)
            gate_branch(0)
            with act.Fori(0, 3) as j:
                for odd in range(2):
                    tile(2 * j + odd, odd)
            tile(6, 0)
            tile(7, 1, last=True)

        @block.gpsimd
        def _(pool):
            nc.gpsimd.iota(IA[:, 0, :], [[0, P]], base=0, channel_multiplier=1)
            nc.gpsimd.iota(IA[:, 1, :], [[1, P]], base=0, channel_multiplier=0)
            pool.drain().then_inc(iota_ready, 1)
            pool.sem_inc(y_free, 1)
            with pool.Fori(0, 8) as i:
                pool.wait_ge(y_ready, i + 1)
                pool.dma_start(io["mix"][8 + i], YB[:]).then_inc(y_out, 16)
                pool.wait_ge(y_out, 16 * i + 16)
                pool.sem_inc(y_free, 1)

        @block.vector
        def _(dve):
            V = nc.vector
            V.memset(EPSG[:, 0:1], GN_EPS)
            V.memset(EPSG[:, 1:2], LN_EPS)
            V.memset(BD[:], 0.0)
            V.memset(SM[:], 0.0)
            V.memset(LR[:], 0.0)
            V.memset(PT[:], 0.0)
            V.memset(XP[:], 0.0)
            V.memset(WG[:], 0.0)
            dve.drain().then_inc(cleared, 1)
            V.memset(BD[0:64, 0:64], 1.0)
            V.memset(BD[64:128, 64:128], 1.0)
            V.memset(SM[:, 1:1 + SEQ].rearrange("p (c s) -> p c s", s=CH_CHUNK)[:, :, 0], 1.0)
            V.memset(SM[:, 1 + SEQ:W1].rearrange("p (b s) -> p b s", s=NS + 1)[:, :, 1], 1.0)
            dve.wait_ge(iota_ready, 1)
            for n in range(6):
                V.tensor_scalar(IB[:], IA[:], n, None, ALU.logical_shift_right)
                dve.drain()
                V.tensor_tensor(BK[:, n, :], IB[:, 0, :], IB[:, 1, :], ALU.is_equal)
                dve.drain()
            V.tensor_tensor(MASK[:, 0, :], IA[:, 0, :], IA[:, 1, :], ALU.is_lt)
            V.tensor_tensor(MASK[:, 1, :], IA[:, 0, :], IA[:, 1, :], ALU.is_le)
            dve.drain()
            for lv in range(5):
                V.tensor_tensor(LM[:, lv, :], BK[:, lv + 1, :], BK[:, lv, :], ALU.subtract)
            dve.drain()
            for lv in range(5):
                V.tensor_tensor(LM[:, lv, :], LM[:, lv, :], MASK[:, 0, :], ALU.mult)
            dve.drain()
            for k in range(2):
                V.tensor_tensor(MASK[:, k, :], MASK[:, k, :], BK[:, 5, :], ALU.mult)
            dve.drain()
            V.tensor_copy(MASK[:, 2:4, :], MASK[:, 0:2, :])
            for k in range(2):
                dve.wait_ge(lr_ev, k + 1)
                V.tensor_tensor(DT[:, 1:W1], PT[:, k, 0:W1 - 1], PT[:, k, 1:W1], ALU.subtract)
                dve.drain()
                c = PAR["mu"] + N0 + k
                V.scalar_tensor_tensor(LR[:, k, 1:W1], DT[:, 1:W1], PARAM[:, c:c + 1], PT[:, k, 1:W1], ALU.mult, ALU.add)
                dve.drain().then_inc(lr_shift, 1)
            lam = PARAM[:, PAR["lam"]:PAR["lam"] + 8]
            SP8 = g["SP8"]
            V.tensor_scalar(SPL[:, 0], lam, -1.0, None, ALU.mult)
            dve.drain()
            V.tensor_tensor(SPL[:, 0], SPL[:, 0], lam, ALU.max)
            dve.drain().then_inc(sp_a, 1)
            dve.wait_ge(sp_b, 1)
            V.tensor_scalar(SPL[:, 2], SPL[:, 1], 1.0, None, ALU.add)
            dve.drain().then_inc(sp_a, 1)
            dve.wait_ge(sp_b, 2)
            V.tensor_scalar(SPL[:, 2], SPL[:, 2], -1.0, None, ALU.add)
            dve.drain()
            V.tensor_scalar(SPL[:, 0], SPL[:, 2], 0.0, None, ALU.is_equal)
            dve.drain()
            V.tensor_tensor(SPL[:, 2:4], SPL[:, 2:4], bcast(SPL[:, 0], 1, 2), ALU.add)
            dve.drain()
            V.reciprocal(SPL[:, 2], SPL[:, 2])
            V.tensor_tensor(SPL[:, 1], SPL[:, 1], SPL[:, 3], ALU.mult)
            V.tensor_scalar(SPL[:, 0], lam, -1.0, 0.0, ALU.mult, ALU.max)
            dve.drain()
            V.tensor_tensor(SPL[:, 1], SPL[:, 1], SPL[:, 2], ALU.mult)
            dve.drain()
            V.tensor_tensor(SPL[:, 1], SPL[:, 1], SPL[:, 0], ALU.add)
            dve.drain()
            V.tensor_scalar(SP8[:, 0], SPL[:, 1], C_LRU, None, ALU.mult)
            V.tensor_scalar(SP8[:, 1], SPL[:, 1], -C_LRU, None, ALU.mult)
            dve.drain().then_inc(sp_c, 1)
            dve.wait_ge(st_in, 32)
            dve.sem_inc(tile_done, 1)

            def tile(i, par):
                xp = XP[:, par]
                xps = xp[:, 3 + SEQ:].rearrange("p (b s) -> p b s", s=7)
                V.tensor_copy(xps[:, :, 0:3], CONV0[:, bass.ds(i, 1), :].rearrange("p i (b s) -> p (i b) s", s=3))
                dve.drain()
                dve.wait_ge(xp_ready, i + 1)
                cw = [PARAM[:, bass.ds(i + (PAR["conv_w"] + 8 * j), 1)] for j in range(4)]
                cb = PARAM[:, bass.ds(i + PAR["conv_b"], 1)]
                xcs = samples4(XC[:, SEQ:T])
                V.tensor_scalar(XC[:, 0:SEQ], xp[:, 0:SEQ], cw[0], cb, ALU.mult, ALU.add)
                V.tensor_scalar(xcs, xps[:, :, 0:4], cw[0], cb, ALU.mult, ALU.add)
                for j in range(1, 4):
                    dve.drain()
                    V.scalar_tensor_tensor(XC[:, 0:SEQ], xp[:, j:j + SEQ], cw[j], XC[:, 0:SEQ], ALU.mult, ALU.add)
                    V.scalar_tensor_tensor(xcs, xps[:, :, j:j + 4], cw[j], xcs, ALU.mult, ALU.add)
                dve.drain().then_inc(xc_ready, 1)
                cvo = CVO[:, bass.ds(i, 1), :].rearrange("p i (b s) -> p (i b) s", s=3)
                V.tensor_copy(cvo[:, 0:1, :], xp[:, SEQ:SEQ + 3].unsqueeze(1))
                V.tensor_copy(cvo[:, 1:9, :], xps[:, :, 4:7])
                dve.wait_ge(a_ready, 2 * i + 1)
                V.tensor_scalar(HS[:], TT[:], 1.0, None, ALU.add)
                V.tensor_scalar(QQ[:], TT[:], 2.0, 1e-30, ALU.mult, ALU.max)
                dve.drain()
                V.reciprocal(HS[:], HS[:])
                dve.drain()
                V.tensor_tensor(QQ[:], QQ[:], HS[:], ALU.mult)
                dve.drain().then_inc(q_ready, 1)
                V.tensor_tensor(IG[:], IG[:], XC[:], ALU.mult)
                dve.drain()
                dve.wait_ge(s_ready, i + 1)
                V.tensor_tensor(QQ[:], QQ[:], IG[:], ALU.mult)
                dve.wait_ge(a_ready, 2 * i + 2)
                a0 = samples4(AA[:, SEQ:T])[:, :, 0]
                g0 = samples4(QQ[:, SEQ:T])[:, :, 0]
                V.tensor_tensor(TMPS[:], a0, LRU0[:, bass.ds(i, 1), :].rearrange("p i b -> p (i b)"), ALU.mult)
                dve.drain()
                V.tensor_tensor(g0, g0, TMPS[:], ALU.add)
                V.memset(a0, 0.0)
                dve.drain()
                V.tensor_tensor_scan(HS[:], AA[:], QQ[:], 0.0, ALU.mult, ALU.add)
                dve.drain()
                lo = LRUO[:, bass.ds(i, 1), :].rearrange("p i b -> p (i b)")
                V.tensor_copy(lo[:, 0:1], HS[:, SEQ - 1:SEQ])
                V.tensor_copy(lo[:, 1:9], samples4(HS[:, SEQ:T])[:, :, NS - 1])
                dve.wait_ge(ge_ready, i + 1)
                dve.wait_ge(y_free, i + 1)
                V.tensor_tensor(YB[:], HS[:], GE[:], ALU.mult)
                dve.drain().then_inc(y_ready, 1)
                dve.sem_inc(tile_done, 1)

            with dve.Fori(0, 4) as j:
                for odd in range(2):
                    tile(2 * j + odd, odd)


KA_, KR_, KB_, KK_, KBH, KKH, KV_ = range(7)


def phase_rwkv(nc, io, g, stack):
    m = Mem(nc, stack, "rw")
    PS, RING, HT, PARAM, LR = g["PS"], g["RING"], g["HT"], g["PARAM"], g["LR"]
    IDENT, BD, MASK, LM, SM, EPSG = (g[x] for x in ("IDENT", "BD", "MASK", "LM", "SM", "EPSG"))
    MOD, CS, BADA = g["MOD"], g["CS"], g["BADA"]
    WLR = m.sb("WLR", [P, 2, P])
    PP = m.sb("PP", [P, 3, W1])
    RR, KX, WD, AG, GN, G2, DT, PX, PI, RPI, SQ, NR = (m.sb(x, [P, W1]) for x in (
        "RR", "KX", "WD", "AG", "GN", "G2", "DT", "PX", "PI", "RPI", "SQ", "NR"))
    BO, YT, YC = (m.sb(x, [P, T]) for x in ("BO", "YT", "YC"))
    OMK = m.sb("OMK", [P, 8])
    BDM = m.sb("BDM", [P, P])
    CHN = m.sb("CHN", [P, 7, W1])
    SLT = m.sb("SLT", [P, 7, 2 * P])
    MM = m.sb("MM", [P, 4, 4, P])
    LT = m.sb("LT", [P, 2, 4, P])
    TB = m.sb("TB", [P, 2, 4, P])
    ZS = m.sb("ZS", [P, 4, P])
    TK = m.sb("TK", [P, 2, 3, P])
    AXX = m.sb("AXX", [P, 4, 2, 64])
    AW = m.sb("AW", [P, 2, 2, 2, 64])
    R2 = m.sb("R2", [P, 2, P])
    Y0 = m.sb("Y0", [P, 2, P])
    GS = m.sb("GS", [P, 8, P])
    K0 = m.sb("K0", [P, 8, P])
    DG = m.sb("DG", [P, 8, P])
    SB = m.sb("SB", [P, 9, P])
    SI = m.sb("SI", [P, 8, P])
    SO = m.sb("SO", [P, 8, P])
    w_in = m.sems("w_in", 3)
    wlr_in, si_in, so_out, sp_out, y_out = (m.sem(x) for x in ("wlr_in", "si_in", "so_out", "sp_out", "y_out"))
    MR = m.sb("MR", [9, 3 * P])
    ada_in, ada_used, mr_ready, turned, mod_read = (m.sem(x) for x in "ada_in ada_used mr_ready turned mod_read".split())
    (cleared, slot_used, proj_done, proj_ev, gk_free, banks_idle, act_rows, rows_used, sq_ready, ss_done, ss_ready,
     nr_ready, rk_ready, bo_done, rows_in, g2_free, prep_ready, tr_done, tr_ready, mm_prod, mm_ready, lt_ready,
     dg_ready, x_done, x_ready, z_done, z_ready, t_done, t_ready, aw_done, aw_ready, ry_done, y0_ready,
     r2_ready, gk_done, gk_read, gk_ready, s_done, s_ready, yy_done, yt_ready, mean_done, yc_ready, ysq_ready, var_done,
     sd_ready, post_done, mix_free, so_ready, so_free, sp_ready, sp_free, si_free) = (m.sem(x) for x in (
        "cleared slot_used proj_done proj_ev gk_free banks_idle act_rows rows_used sq_ready ss_done ss_ready "
        "nr_ready rk_ready bo_done rows_in g2_free prep_ready tr_done tr_ready mm_prod mm_ready lt_ready "
        "dg_ready x_done x_ready z_done z_ready t_done t_ready aw_done aw_ready ry_done y0_ready "
        "r2_ready gk_done gk_read gk_ready s_done s_ready yy_done yt_ready mean_done yc_ready ysq_ready var_done "
        "sd_ready post_done mix_free so_ready so_free sp_ready sp_free si_free").split())
    PC0, PC1 = 1 + SEQ, W1

    MODS = (3, 3, 2)
    LEVELS = (5, 5, 2)

    def per_level(i, step, lo):
        return sum(2 * (n - lo) for n in LEVELS) * i + sum(2 * (n - lo) for n in LEVELS[:step])

    def chan_view(kind, x, step):
        if step < 2:
            lo = 1 + 2 * P * step + P * x
            return CHN[:, kind, lo:lo + P]
        return SLT[:, kind, P * x:P * x + P]

    def two_kinds(rows, kind, x, step):
        if step < 2:
            lo = 1 + 2 * P * step + P * x
            return CHN[rows, kind:kind + 2, lo:lo + P]
        return SLT[rows, kind:kind + 2, P * x:P * x + P]

    with nc.Block() as block:
        @block.sync
        def _(sp):
            for k in range(3):
                sp.dma_start(RING[:, k, :], io["w_in"][8 * k]).then_inc(w_in[k], 16)
            sp.dma_start(WLR[:], io["w_lr"][0]).then_inc(wlr_in, 16)

            def load_ada(n):
                sp.dma_start(RING[:, 3, :], io["w_ada"][n]).then_inc(ada_in, 16)

            def load_pair(i):
                for k in range(3):
                    sp.wait_ge(slot_used, 4 * i + (k - 3))
                    sp.dma_start(RING[:, k, :], io["w_in"][i + 8 * k]).then_inc(w_in[k], 16)
                sp.wait_ge(slot_used, 4 * i)
                sp.dma_start(WLR[:], io["w_lr"][i]).then_inc(wlr_in, 16)

            def load_modulation(i, tiles):
                for t in range(tiles):
                    sp.wait_ge(ada_used, ADA_PAIR * i + (t + 1))
                    load_ada(ADA_PAIR * i + (ADA_H + t + 1))

            load_ada(ADA_H)
            load_pair(1)
            with sp.Fori(0, NPAIR - 2) as i:
                load_pair(i + 2)
                load_modulation(i, ADA_PAIR)
            load_modulation(NPAIR - 2, ADA_PAIR)
            load_modulation(NPAIR - 1, ADA_PAIR - 1)

        BANKS = (6, 2, 4, 6, 2, 4)

        def project(pe, i, which, part=(0, 1)):
            for half in part:
                if half == 0:
                    pe.wait_ge(w_in[which], 16 * i + 16)
                for kt in range(KT):
                    mm = nc.tensor.matmul(PS[:, BANKS[which] + half, 0:TPH], RING[:, which, P * kt:P * kt + P],
                                          HT[:, kt, TPH * half:TPH * half + TPH], start=(kt == 0), stop=(kt == KT - 1))
            if half == 1:
                mm.then_inc(slot_used, 1)
                pe.drain().then_inc(proj_done, 1)

        def project_low(pe, i):
            pe.wait_ge(wlr_in, 16 * i + 16)
            for n, (lhs, rhs) in enumerate(((WLR[0:64, 0, :], LR[0:64, 0, :]), (WLR[64:P, 0, :], LR[64:P, 0, :]),
                                            (WLR[:, 1, :], LR[:, 1, :]))):
                pe.wait_ge(proj_ev, 6 * i + (n + 1))
                for half in range(2):
                    mm = nc.tensor.matmul(PS[:, BANKS[3 + n] + half, 0:TPH], lhs,
                                          rhs[:, 1 + TPH * half:1 + TPH * half + TPH], start=True, stop=True)
                if n == 2:
                    mm.then_inc(slot_used, 1)
                pe.drain().then_inc(proj_done, 1)

        def head_sum(pe, ready, value, done):
            pe.wait_ge(ready, value)
            for half in range(2):
                mm = nc.tensor.matmul(PS[:, half, 0:TPH], BD[:], SQ[:, 1 + TPH * half:1 + TPH * half + TPH],
                                      start=True, stop=True)
            mm.then_inc(done, 1)

        def evacuate(act, i):
            A = nc.scalar.activation
            w0, a0 = (PARAM[:, bass.ds(i + PAR[n], 1)] for n in ("w0", "a0"))
            for which in range(6):
                act.wait_ge(proj_done, 6 * i + (which + 1))
                src = PS[:, BANKS[which]:BANKS[which] + 2, 0:TPH]
                dst = halves((PP[:, which] if which < 3 else (WD, AG, GN)[which - 3])[:, 1:W1])
                if which == 3:
                    A(dst, src, ACT.Sigmoid, bias=w0).then_inc(proj_ev, 1)
                elif which == 4:
                    A(dst, src, ACT.Sigmoid, bias=a0).then_inc(proj_ev, 1)
                else:
                    A(dst, src, ACT.Copy).then_inc(proj_ev, 1)
            act.drain()
            A(WD[:, 1:W1], WD[:, 1:W1], ACT.Exp, scale=-EXP_HALF).then_inc(rows_in, 1)

        def pe_scan(pe, i, step, n):
            pe.wait_ge(s_ready, 18 * i + 9 * step + n + 1)
            nc.tensor.matmul(PS[:, 7, CH_CHUNK * n:CH_CHUNK * n + CH_CHUNK], SB[:, n, :],
                             R2[:, n // 4, 32 * (n % 4):32 * (n % 4) + 32], start=True, stop=True)
            nc.tensor.matmul(PS[:, 7, 256 + P * (n % 2):256 + P * (n % 2) + P], GS[:, n, :], SB[:, n, :],
                             start=True, stop=True).then_inc(s_done, 1)

        def pe_modulation(pe, i, t, lo=0, hi=KT):
            if lo == 0:
                if t in (3, 6):
                    pe.wait_ge(mod_read, 3 * i + t // 3)
                pe.wait_ge(ada_in, 16 * ADA_PAIR * i + 16 * (t + 1))
            for k in range(lo, hi):
                mm = nc.tensor.matmul(PS[0:9, 6, P * (t % 3):P * (t % 3) + P], CS[:, k, :], RING[:, 3, P * k:P * k + P],
                                      start=(k == 0), stop=(k == KT - 1))
            if hi == KT:
                mm.then_inc(ada_used, 1)

        def pe_turn(pe, i, step):
            pe.wait_ge(mr_ready, 3 * i + step + 1)
            for c in range(MODS[step]):
                mm = nc.tensor.matmul(PS[:, 6, 3 * P + 9 * c:3 * P + 9 * c + 9], MR[:, P * c:P * c + P], IDENT[0:9, 0:9],
                                      start=True, stop=True)
            mm.then_inc(turned, 1)

        def pe_step(pe, i, step):
            u = 3 * i + step
            if step:
                pe.wait_ge(y0_ready, 2 * u)
            for x in range(2):
                for c, kind in enumerate((KA_, KBH, KKH, KV_)):
                    mm = nc.tensor.transpose(PS[:, 4 + x, P * c:P * c + P], chan_view(kind, x, step), IDENT[:])
                mm.then_inc(tr_done, 1)
            if step:
                pe.wait_ge(gk_read, u)
            for q in range(4):
                x, h = q // 2, q % 2
                rows = slice(64 * h, 64 * h + 64)
                for c, kind in enumerate((KB_, KK_)):
                    mm = nc.tensor.matmul(PS[:, q, 256 * c:256 * c + 256], chan_view(kind, x, step)[rows],
                                          two_kinds(rows, KA_, x, step), start=True, stop=True)
                mm.then_inc(mm_prod, 1)
            if step:
                pe_turn(pe, i, step - 1)
            for x in range(2):
                pe.wait_ge(mm_ready, 4 * u + (2 * x + 2))
                pe.wait_ge(tr_ready, 2 * u + (x + 1))
                for h in range(2):
                    mm = nc.tensor.matmul(PS[:, 4 + x, 64 * h:64 * h + 64], MM[:, 2, 2 * x + h, :],
                                          TK[:, x, 2, 64 * h:64 * h + 64], start=True, stop=True)
                mm.then_inc(x_done, 1)
            if step:
                pe.wait_ge(gk_ready, u)
            n0, n1 = per_level(i, step, 0), per_level(i, step, 1)
            last = LEVELS[step] - 1
            for lv in range(last + 1):
                for x in range(2):
                    pe.wait_ge(lt_ready, n0 + (2 * lv + x + 1))
                    if lv:
                        pe.wait_ge(t_ready, n0 + (2 * lv + x - 1))
                    for h in range(2):
                        q = 2 * x + h
                        if lv == 0:
                            mm = nc.tensor.transpose(PS[:, 2 * x, P * h:P * h + P], LT[:, 0, q, :], IDENT[:])
                        else:
                            mm = nc.tensor.matmul(PS[:, 2 * x, P * h:P * h + P], LT[:, lv % 2, q, :], TB[:, 0, q, :],
                                                  start=True, stop=True)
                    mm.then_inc(z_done, 1)
                if lv == 0:
                    continue
                if step:
                    pe_scan(pe, i, step - 1, 2 * lv - 2)
                if step == 2:
                    pe_modulation(pe, i, 6, 0, 5)
                    pe_scan(pe, i, 1, 1)
                    pe_modulation(pe, i, 6, 5, 10)
                    pe_scan(pe, i, 1, 2)
                    pe_modulation(pe, i, 6, 10)
                elif lv in (1, 3):
                    pe_modulation(pe, i, 3 * step + lv // 2)
                for x in range(2):
                    pe.wait_ge(z_ready, n1 + (2 * lv + x - 1))
                    for h in range(2):
                        q = 2 * x + h
                        if lv < last:
                            nc.tensor.matmul(PS[:, 2 * x + 1, P * h:P * h + P], TB[:, 1, q, :], ZS[:, q, :],
                                             start=True, stop=True)
                        mm = nc.tensor.matmul(PS[:, 2 * x + 1, 256 + P * h:256 + P * h + P], ZS[:, q, :], TB[:, 1, q, :],
                                              start=True, stop=True)
                    mm.then_inc(t_done, 1)
                if step:
                    pe_scan(pe, i, step - 1, 3 if step == 2 else 2 * lv - 1)
            if step < 2:
                pe_modulation(pe, i, 3 * step + 2)
            for x in range(2):
                pe.wait_ge(x_ready, 2 * u + (x + 1))
                pe.wait_ge(t_ready, n0 + (2 * last + x + 1))
                for h in range(2):
                    mm = nc.tensor.matmul(PS[:, 4 + x, P * h:P * h + P], TB[:, 1, 2 * x + h, :], AXX[:, 2 * x + h, :, :],
                                          start=True, stop=True)
                mm.then_inc(aw_done, 1)
            for x in range(2):
                pe.wait_ge(aw_ready, 2 * u + (x + 1))
                for h in range(2):
                    q = 2 * x + h
                    rows = slice(64 * h, 64 * h + 64)
                    nc.tensor.matmul(PS[rows, 4 + x, 256:384], AW[:, x, 0, h, :], MM[:, 1, q, :], start=True, stop=True)
                    y0 = PS[rows, 4 + x, 384:512]
                    nc.tensor.matmul(y0, AW[:, x, 1, h, :], MM[:, 1, q, :], start=True, stop=False)
                    mm = nc.tensor.matmul(y0, TK[:, x, 2, 64 * h:64 * h + 64], MM[:, 3, q, :], start=False, stop=True)
                mm.then_inc(ry_done, 1)
            if step == 2:
                for n in range(4):
                    pe_modulation(pe, i, 7, 4 * n, 4 * n + 4)
                    pe_scan(pe, i, 1, 4 + n)
            for x in range(2):
                for c in range(4):
                    rows = slice(32 * c, 32 * c + 32)
                    at = 256 * x
                    nc.tensor.matmul(PS[:, c, at:at + P], AW[rows, x, 0, :, :], TK[rows, x, 0, :], start=True, stop=True)
                    nc.tensor.matmul(PS[:, c, at + P:at + 2 * P], TK[rows, x, 0, :], AW[rows, x, 1, :, :],
                                     start=True, stop=False)
                    mm = nc.tensor.matmul(PS[:, c, at + P:at + 2 * P], TK[rows, x, 1, :], TK[rows, x, 2, :],
                                          start=False, stop=True)
                if step == 2 and x == 0:
                    pe_turn(pe, i, 2)
            mm.then_inc(gk_done, 1)

        def pe_samples(pe, i, ahead2):
            u = 3 * i + 2
            if ahead2:
                pe.wait_ge(mod_read, 3 * i + 3)
                project(pe, i + 2, 0, (0,))
            pe.wait_ge(gk_ready, u + 1)
            pe.wait_ge(y0_ready, 2 * u + 2)
            pe.wait_ge(si_in, 32 * i + 32)
            for n in range(8):
                nc.tensor.matmul(PS[:, 4 + n // 4, P * (n % 4):P * (n % 4) + P], GS[:, n, :], SI[:, n, :],
                                 start=True, stop=True)
                mm = nc.tensor.matmul(PS[:, 7, CH_CHUNK * n:CH_CHUNK * n + CH_CHUNK], SI[:, n, :],
                                      R2[:, n // 4, 32 * (n % 4):32 * (n % 4) + 32], start=True, stop=True)
            mm.then_inc(yy_done, 1)

        def pe_post(pe, i, ahead2):
            pe.wait_ge(yt_ready, 3 * i + 3)
            for half in range(2):
                mm = nc.tensor.matmul(PS[:, 0 + half, 0:TH], BDM[:], YT[:, TH * half:TH * half + TH], start=True, stop=True)
            mm.then_inc(mean_done, 1)
            if ahead2:
                project(pe, i + 2, 0, (1,))
            pe.wait_ge(so_ready, i + 1)
            pe.wait_ge(ysq_ready, i + 1)
            for half in range(2):
                mm = nc.tensor.matmul(PS[:, 4 + half, 0:TH], BDM[:], SQ[:, TH * half:TH * half + TH], start=True, stop=True)
            mm.then_inc(var_done, 1)

        @block.tensor
        def _(pe):
            pe.wait_ge(cleared, 1)
            for which in range(3):
                project(pe, 0, which)
            project_low(pe, 0)
            pe.wait_ge(rows_in, 1)
            project(pe, 1, 0)

            def pair(i, ahead, ahead2):
                if ahead:
                    project(pe, i + 1, 1)
                pe.wait_ge(banks_idle, i + 1)
                head_sum(pe, sq_ready, i + 1, ss_done)
                if ahead:
                    project(pe, i + 1, 2)
                head_sum(pe, rk_ready, i + 1, bo_done)
                if ahead:
                    project_low(pe, i + 1)
                    pe.wait_ge(rows_in, i + 2)
                pe.wait_ge(prep_ready, i + 1)
                for step in range(3):
                    pe_step(pe, i, step)
                pe_samples(pe, i, ahead2)
                pe_post(pe, i, ahead2)

            with pe.Fori(0, NPAIR - 2) as i:
                pair(i, True, True)
            pair(NPAIR - 2, True, False)
            pair(NPAIR - 1, False, False)

        def act_step(act, i, step):
            u = 3 * i + step
            A = nc.scalar.activation
            for x in range(2):
                act.wait_ge(tr_done, 2 * u + (x + 1))
                A(AXX[:, 2 * x:2 * x + 2, 0, :], PS[:, 4 + x, 0:P].rearrange("p (h c) -> p h c", h=2), ACT.Copy)
                A(TK[:, x].rearrange("p k c -> p (k c)"), PS[:, 4 + x, P:4 * P], ACT.Copy)
                act.drain().then_inc(tr_ready, 1)
            for x in range(2):
                act.wait_ge(x_done, 2 * u + (x + 1))
                A(AXX[:, 2 * x:2 * x + 2, 1, :], PS[:, 4 + x, 0:P].rearrange("p (h c) -> p h c", h=2),
                  ACT.Copy).then_inc(x_ready, 1)
            for lv in range(1, LEVELS[step]):
                for x in range(2):
                    act.wait_ge(z_done, per_level(i, step, 0) + (2 * lv + x + 1))
                    A(ZS[:, 2 * x:2 * x + 2], PS[:, 2 * x, 0:256].rearrange("p (h c) -> p h c", h=2),
                      ACT.Copy).then_inc(z_ready, 1)
            for x in range(2):
                act.wait_ge(aw_done, 2 * u + (x + 1))
                A(AW[:, x].rearrange("p k h c -> p h k c"),
                  PS[:, 4 + x, 0:256].rearrange("p (h k c) -> p h k c", h=2, k=2), ACT.Copy).then_inc(aw_ready, 1)
            act.wait_ge(ada_used, ADA_PAIR * i + (3 * step + MODS[step]))
            A(MR[:, 0:P * MODS[step]], PS[0:9, 6, 0:P * MODS[step]], ACT.Copy).then_inc(mr_ready, 1)
            if step:
                act.wait_ge(yt_ready, u)
            for x in range(2):
                act.wait_ge(r2_ready, 2 * u + (x + 1))
                A(Y0[:, x], PS[:, 4 + x, 384:512], ACT.Copy).then_inc(y0_ready, 1)

        @block.scalar
        def _(act):
            A = nc.scalar.activation
            act.wait_ge(cleared, 1)
            evacuate(act, 0)

            def pair(i, ahead):
                act.wait_ge(act_rows, i + 1)
                A(SQ[:, 1:W1], KX[:, 1:W1], ACT.Square, scale=PARAM[:, bass.ds(i + PAR["k_k"], 1)]).then_inc(sq_ready, 1)
                act.wait_ge(ss_ready, i + 1)
                A(NR[:, 1:W1], NR[:, 1:W1], ACT.Sqrt).then_inc(nr_ready, 1)
                act.wait_ge(g2_free, i + 1)
                A(G2[:, 1:W1], GN[:, 1:W1], ACT.Copy)
                if ahead:
                    act.wait_ge(rows_used, i + 1)
                    evacuate(act, i + 1)
                for step in range(3):
                    act_step(act, i, step)
                act.wait_ge(yc_ready, i + 1)
                A(SQ[:, 0:T], YC[:], ACT.Square).then_inc(ysq_ready, 1)
                act.wait_ge(var_done, i + 1)
                A(NR[:, 0:T].rearrange("p (h n) -> p h n", h=2), PS[:, 4:6, 0:TH], ACT.Sqrt,
                  bias=EPSG[:, 0:1]).then_inc(sd_ready, 1)

            with act.Fori(0, NPAIR - 1) as i:
                pair(i, True)
            pair(NPAIR - 1, False)

        @block.gpsimd
        def _(pool):
            G = nc.gpsimd
            pool.wait_ge(cleared, 1)

            def load_states(i):
                for h in range(2):
                    rows = slice(64 * h, 64 * h + 64)
                    pool.dma_start(SI[rows, :, rows], io["wkv0"][i][rows]).then_inc(si_in, 16)

            load_states(0)

            def pair(i, ahead):
                for step in range(3):
                    u = 3 * i + step
                    pool.wait_ge(prep_ready, i + 1)
                    ident = bcast(IDENT[:], 1, 4)
                    pool.wait_ge(gk_free, u + 1)
                    for x in range(2):
                        if step < 2:
                            lo = 1 + 2 * P * step + P * x + CH_CHUNK - 1
                            pc = PI[:, lo:lo + 3 * CH_CHUNK + 1:CH_CHUNK]
                        else:
                            lo = PC0 + 4 * (NS + 1) * x + NS
                            pc = PI[:, lo:lo + 3 * (NS + 1) + 1:NS + 1]
                        G.tensor_tensor(DG[:, 4 * x:4 * x + 4, :], ident, bcast(pc, 2, P), ALU.mult)
                    pool.drain().then_inc(dg_ready, 1)
                    pool.wait_ge(mm_ready, 4 * u + 4)
                    for lv in range(LEVELS[step]):
                        for x in range(2):
                            if lv >= 2:
                                pool.wait_ge(t_ready, per_level(i, step, 0) + (2 * lv + x - 3))
                            G.tensor_tensor(LT[:, lv % 2, 2 * x:2 * x + 2], MM[:, 0, 2 * x:2 * x + 2, :],
                                            bcast(LM[:, lv, :], 1, 2), ALU.mult)
                            pool.drain().then_inc(lt_ready, 1)
                    if step == 2:
                        pool.wait_ge(sp_ready, i + 1)
                        for h in range(2):
                            rows = slice(64 * h, 64 * h + 64)
                            pool.dma_start(io["wkv_p"][i][rows], SB[rows, 8, rows]).then_inc(sp_out, 16)
                        pool.wait_ge(sp_out, 32 * i + 32)
                        pool.sem_inc(sp_free, 1)
                pool.wait_ge(so_ready, i + 1)
                for h in range(2):
                    rows = slice(64 * h, 64 * h + 64)
                    pool.dma_start(io["wkv_s"][i][rows], SO[rows, :, rows]).then_inc(so_out, 16)
                if ahead:
                    load_states(i + 1)
                pool.wait_ge(so_out, 32 * i + 32)
                pool.sem_inc(so_free, 1)
                pool.wait_ge(post_done, i + 1)
                pool.dma_start(io["mix"][i], YT[:]).then_inc(y_out, 16)
                pool.wait_ge(y_out, 16 * i + 16)
                pool.sem_inc(mix_free, 1)

            with pool.Fori(0, NPAIR - 1) as i:
                pair(i, True)
            pair(NPAIR - 1, False)

        def prep(dve, i):
            V = nc.vector
            body = slice(1, W1)
            dve.wait_ge(rows_in, i + 1)
            for which, (kt, dst) in enumerate(((0, RR[:, body]), (8, KX[:, body]), (16, CHN[:, KV_, body]))):
                V.tensor_tensor(DT[:, body], PP[:, which, 0:W1 - 1], PP[:, which, 1:W1], ALU.subtract)
                dve.drain()
                V.scalar_tensor_tensor(dst, DT[:, body], PARAM[:, bass.ds(i + (PAR["mu"] + kt), 1)], PP[:, which, 1:W1],
                                       ALU.mult, ALU.add)
                dve.drain()
                if which == 1:
                    dve.sem_inc(act_rows, 1)
            V.tensor_tensor_scan(PX[:, body], WD[:, 0:W1 - 1], SM[:, body], 1.0, ALU.mult, ALU.max)
            V.tensor_scalar(DT[:, body], AG[:, body], PARAM[:, bass.ds(i + PAR["k_a"], 1)], OMK[:, bass.ds(i, 1)],
                            ALU.mult, ALU.add)
            dve.drain()
            V.tensor_tensor(PI[:, body], PX[:, body], WD[:, body], ALU.mult)
            V.tensor_tensor(DT[:, body], DT[:, body], KX[:, body], ALU.mult)
            dve.wait_ge(ss_done, i + 1)
            V.tensor_scalar(halves(NR[:, body]), PS[:, 0:2, 0:TPH], 1e-24, None, ALU.max)
            dve.drain().then_inc(ss_ready, 1)
            V.scalar_tensor_tensor(SQ[:, body], RR[:, body], PARAM[:, bass.ds(i + PAR["r_k"], 1)], DT[:, body],
                                   ALU.mult, ALU.mult)
            dve.drain().then_inc(rk_ready, 1)
            V.reciprocal(RPI[:, body], PI[:, body])
            V.tensor_tensor(CHN[:, KR_, body], RR[:, body], PI[:, body], ALU.mult)
            dve.drain()
            V.tensor_tensor(CHN[:, KK_, body], DT[:, body], RPI[:, body], ALU.mult)
            dve.wait_ge(nr_ready, i + 1)
            V.reciprocal(NR[:, body], NR[:, body])
            dve.drain()
            V.scalar_tensor_tensor(NR[:, body], KX[:, body], PARAM[:, bass.ds(i + PAR["k_k"], 1)], NR[:, body],
                                   ALU.mult, ALU.mult)
            dve.drain()
            V.scalar_tensor_tensor(CHN[:, KA_, body], NR[:, body], -1.0, PX[:, body], ALU.mult, ALU.mult)
            V.tensor_tensor(DT[:, body], NR[:, body], AG[:, body], ALU.mult)
            dve.drain()
            V.tensor_tensor(CHN[:, KB_, body], DT[:, body], RPI[:, body], ALU.mult)
            dve.drain()
            V.tensor_tensor(CHN[:, KBH:KKH + 1, 1:1 + SEQ].rearrange("p k (c s) -> p k c s", s=CH_CHUNK),
                            CHN[:, KB_:KK_ + 1, 1:1 + SEQ].rearrange("p k (c s) -> p k c s", s=CH_CHUNK),
                            bcast(bcast(PI[:, CH_CHUNK:1 + SEQ:CH_CHUNK], 2, CH_CHUNK), 1, 2), ALU.mult)
            s5 = lambda lo, hi: CHN[:, lo:hi, PC0:PC1].rearrange("p k (b s) -> p k b s", s=NS + 1)[:, :, :, 1:]
            s32 = lambda lo, hi: SLT[:, lo:hi, :].rearrange("p k (b s) -> p k b s", s=CH_CHUNK)[:, :, :, 0:NS]
            V.tensor_copy(s32(KA_, KK_ + 1), s5(KA_, KK_ + 1))
            V.tensor_copy(s32(KV_, KV_ + 1), s5(KV_, KV_ + 1))
            V.tensor_tensor(s32(KBH, KKH + 1), s5(KB_, KK_ + 1),
                            bcast(bcast(PI[:, PC0 + NS:PC1:NS + 1], 2, NS), 1, 2), ALU.mult)
            dve.wait_ge(bo_done, i + 1)
            V.tensor_tensor(BO[:, 0:TPH], CHN[:, KV_, 1:1 + TPH], PS[:, 0, 0:TPH], ALU.mult)
            V.tensor_tensor(BO[:, TPH:SEQ], CHN[:, KV_, 1 + TPH:1 + SEQ], PS[:, 1, 0:PB], ALU.mult)
            V.tensor_tensor(samples4(BO[:, SEQ:T]), samples5(CHN[:, KV_, PC0:PC1]), samples5(PS[:, 1, PB:TPH]),
                            ALU.mult)
            dve.drain().then_inc(rows_used, 1)
            dve.sem_inc(prep_ready, 1)

        def dve_step(dve, i, step):
            V = nc.vector
            u = 3 * i + step
            y0 = Y0[:].rearrange("p x t -> p (x t)")
            for q in range(4):
                dve.wait_ge(mm_prod, 4 * u + (q + 1))
                V.tensor_tensor(MM[:, :, q, :], PS[:, q, :].rearrange("p (k t) -> p k t", k=4), MASK[:],
                                ALU.mult).then_inc(mm_ready, 1)
            if step:
                dve_modulation(dve, i, step - 1)
                if step == 1:
                    dve.wait_ge(sp_free, i + 1)
                    V.memset(SB[:, 0, :], 0.0).then_inc(s_ready, 1)
                else:
                    V.tensor_copy(SB[:, 0, :], SB[:, 8, :])
                    dve.drain().then_inc(s_ready, 1)
            n0, n1 = per_level(i, step, 0), per_level(i, step, 1)
            last = LEVELS[step] - 1
            for lv in range(last + 1):
                if lv and step:
                    for n in (0, 1, 2) if step == 2 else (2 * lv - 2,):
                        dve_scan(dve, i, step - 1, n)
                for x in range(2):
                    tb, tbk = TB[:, :, 2 * x:2 * x + 2, :], slice(2 * x, 2 * x + 2)
                    if lv == 0:
                        dve.wait_ge(lt_ready, n0 + (x + 1))
                        V.tensor_tensor(TB[:, 1, tbk], LT[:, 0, tbk], bcast(IDENT[:], 1, 2), ALU.add)
                        dve.wait_ge(z_done, n0 + (x + 1))
                        V.tensor_tensor(TB[:, 0, tbk], PS[:, 2 * x, 0:256].rearrange("p (h t) -> p h t", h=2),
                                        bcast(IDENT[:], 1, 2), ALU.add)
                        dve.drain().then_inc(t_ready, 1)
                        continue
                    dve.wait_ge(t_done, n1 + (2 * lv + x - 1))
                    if lv < last:
                        V.tensor_tensor(tb, tb, PS[:, 2 * x + 1, :].rearrange("p (k h t) -> p k h t", k=2, h=2), ALU.add)
                    else:
                        V.tensor_tensor(TB[:, 1, tbk], TB[:, 1, tbk],
                                        PS[:, 2 * x + 1, 256:512].rearrange("p (h t) -> p h t", h=2), ALU.add)
                    dve.drain().then_inc(t_ready, 1)
                if lv and step:
                    dve_scan(dve, i, step - 1, 3 if step == 2 else 2 * lv - 1)
            if step == 2:
                for n in range(4, 8):
                    dve_scan(dve, i, 1, n)
            if step:
                if step == 2:
                    dve.drain().then_inc(sp_ready, 1)
                if step == 1:
                    dve.wait_ge(mix_free, i + 1)
                V.tensor_tensor(YT[:, 256 * step - 256:256 * step], y0, PS[:, 7, 0:256], ALU.add)
                dve.drain().then_inc(yt_ready, 1)
            for x in range(2):
                dve.wait_ge(ry_done, 2 * u + (x + 1))
                V.tensor_tensor(R2[:, x, :], chan_view(KR_, x, step), PS[:, 4 + x, 256:384], ALU.add)
                dve.drain().then_inc(r2_ready, 1)
            if step == 2:
                dve_modulation(dve, i, 2)
            dve.wait_ge(gk_done, u + 1)
            bd = bcast(bcast(BD[:], 1, 4), 1, 2)
            by_chunk = lambda ap: ap.rearrange("p (x c) t -> p x c t", x=2)
            prod = PS[:, 0:4, :].rearrange("p c (x k t) -> p k x c t", x=2, k=2)
            V.tensor_tensor(by_chunk(GS[:]), prod[:, 0], bd, ALU.mult)
            V.tensor_tensor(by_chunk(K0[:]), prod[:, 1], bd, ALU.mult)
            dve.drain().then_inc(gk_read, 1)
            dve.wait_ge(dg_ready, u + 1)
            V.tensor_tensor(GS[:], GS[:], DG[:], ALU.add)
            dve.drain().then_inc(gk_ready, 1)
            dve.sem_inc(gk_free, 1)

        def dve_scan(dve, i, step, n):
            dve.wait_ge(s_done, 16 * i + 8 * step + (n + 1))
            nc.vector.tensor_tensor(SB[:, n + 1, :], K0[:, n, :], PS[:, 7, 256 + P * (n % 2):256 + P * (n % 2) + P],
                                    ALU.add).then_inc(s_ready, 1)

        def dve_modulation(dve, i, step):
            dve.wait_ge(turned, 3 * i + step + 1)
            n = MODS[step]
            at = bass.ds(ADA_PAIR * i + (ADA_H + 3 * step), n)
            nc.vector.tensor_tensor(MOD[:, at, :], PS[:, 6, 3 * P:3 * P + 9 * n].rearrange("p (c b) -> p c b", b=9),
                                    bcast(BADA[:, at], 2, 9), ALU.add).then_inc(mod_read, 1)

        def dve_samples(dve, i):
            V = nc.vector
            u = 3 * i + 2
            dve.wait_ge(yy_done, i + 1)
            dve.wait_ge(y0_ready, 2 * u + 2)
            sl = lambda ap: ap.rearrange("p (b s) -> p b s", s=CH_CHUNK)[:, :, 0:NS]
            V.tensor_tensor(samples4(YT[:, SEQ:T]), sl(Y0[:].rearrange("p x t -> p (x t)")), sl(PS[:, 7, 0:256]), ALU.add)
            dve.drain().then_inc(yt_ready, 1)
            dve.wait_ge(so_free, i + 1)
            V.tensor_tensor(SO[:].rearrange("p (x c) t -> p x c t", x=2), K0[:].rearrange("p (x c) t -> p x c t", x=2),
                            PS[:, 4:6, :].rearrange("p x (c t) -> p x c t", c=4), ALU.add)
            dve.drain().then_inc(so_ready, 1)

        def post(dve, i):
            V = nc.vector
            dve.wait_ge(mean_done, i + 1)
            V.tensor_tensor(halves(YC[:]), halves(YT[:]), PS[:, 0:2, 0:TH], ALU.subtract)
            dve.drain().then_inc(yc_ready, 1)
            dve.wait_ge(sd_ready, i + 1)
            V.reciprocal(NR[:, 0:T], NR[:, 0:T])
            dve.sem_inc(banks_idle, 1)
            dve.drain()
            V.tensor_tensor(YC[:], YC[:], NR[:, 0:T], ALU.mult)
            dve.drain()
            V.tensor_scalar(YC[:], YC[:], PARAM[:, bass.ds(i + PAR["lnx_w"], 1)], PARAM[:, bass.ds(i + PAR["lnx_b"], 1)],
                            ALU.mult, ALU.add)
            dve.drain()
            V.tensor_tensor(YC[:], YC[:], BO[:], ALU.add)
            dve.drain()
            V.tensor_tensor(YT[:, 0:SEQ], YC[:, 0:SEQ], G2[:, 1:1 + SEQ], ALU.mult)
            V.tensor_tensor(samples4(YT[:, SEQ:T]), samples4(YC[:, SEQ:T]), samples5(G2[:, PC0:PC1]), ALU.mult)
            dve.drain().then_inc(post_done, 1)
            dve.sem_inc(g2_free, 1)

        @block.vector
        def _(dve):
            V = nc.vector
            for buf in (PP, WD, SLT, SI, SB, CHN, NR):
                V.memset(buf[:], 0.0)
            V.tensor_scalar(OMK[:], PARAM[:, PAR["k_a"]:PAR["k_a"] + 8], -1.0, 1.0, ALU.mult, ALU.add)
            V.tensor_scalar(BDM[:], BD[:], 1.0 / 64, None, ALU.mult)
            dve.drain().then_inc(cleared, 1)
            dve.sem_inc(mix_free, 1)
            dve.sem_inc(so_free, 1)
            dve.sem_inc(sp_free, 1)
            dve.sem_inc(gk_free, 1)
            dve.sem_inc(g2_free, 1)
            dve.sem_inc(banks_idle, 1)
            with dve.Fori(0, NPAIR) as i:
                prep(dve, i)
                for step in range(3):
                    dve_step(dve, i, step)
                dve_samples(dve, i)
                post(dve, i)
            for lo, hi in ((2, 3), (4, 6)):
                V.tensor_scalar(MOD[:, KT * lo:KT * hi, :], MOD[:, KT * lo:KT * hi, :], 1.0, None, ALU.add)


class Norm:

    def __init__(self, nc, m, g, X, wname, bname):
        self.nc, self.g, self.X, self.wname, self.bname = nc, g, X, wname, bname
        self.SQ = m.sb("nSQ", [P, 2, T])
        self.MN = m.sb("nMN", [P, 2, T])
        self.ONES = m.sb("nONES", [P, P])
        self.ones_ready, self.mean_done, self.xc_ready, self.sq_ready, self.sq_used, self.sd_ready = (
            m.sem("n_" + x) for x in ("ones_ready", "mean_done", "xc_ready", "sq_ready", "sq_used", "sd_ready"))

    def start(self, dve):
        self.nc.vector.memset(self.ONES[:], 1.0 / D)
        dve.drain().then_inc(self.ones_ready, 1)

    def tensor(self, pe, x_ready, per_tile):
        PS = self.g["PS"]
        pe.wait_ge(self.ones_ready, 1)
        for kt in range(KT):
            pe.wait_ge(x_ready, per_tile * (kt + 1))
            for half in range(2):
                mm = self.nc.tensor.matmul(PS[:, 4 + half, 0:TH], self.ONES[:], self.X[:, kt, TH * half:TH * half + TH],
                                           start=(kt == 0), stop=(kt == KT - 1))
        mm.then_inc(self.mean_done, 1)
        for kt in range(KT):
            pe.wait_ge(self.sq_ready, kt + 1)
            for half in range(2):
                mm = self.nc.tensor.matmul(PS[:, 6 + half, 0:TH], self.ONES[:],
                                           self.SQ[:, kt % 2, TH * half:TH * half + TH],
                                           start=(kt == 0), stop=(kt == KT - 1))
            mm.then_inc(self.sq_used, 1)

    def scalar(self, act):
        for kt in range(KT):
            act.wait_ge(self.xc_ready, kt + 1)
            if kt >= 2:
                act.wait_ge(self.sq_used, kt - 1)
            self.nc.scalar.activation(self.SQ[:, kt % 2, :], self.X[:, kt, :], ACT.Square).then_inc(self.sq_ready, 1)
        act.wait_ge(self.sq_used, KT)
        self.nc.scalar.activation(self.MN[:, 1].rearrange("p (h n) -> p h n", h=2), self.g["PS"][:, 6:8, 0:TH], ACT.Sqrt,
                                  bias=self.g["EPSG"][:, 1:2]).then_inc(self.sd_ready, 1)

    def vector(self, dve, per_tile):
        V, PARAM = self.nc.vector, self.g["PARAM"]
        dve.wait_ge(self.mean_done, 1)
        V.tensor_copy(self.MN[:, 0].rearrange("p (h n) -> p h n", h=2), self.g["PS"][:, 4:6, 0:TH])
        dve.drain()
        for kt in range(KT):
            V.tensor_tensor(self.X[:, kt, :], self.X[:, kt, :], self.MN[:, 0], ALU.subtract).then_inc(self.xc_ready, 1)
        dve.wait_ge(self.sd_ready, 1)
        V.reciprocal(self.MN[:, 1], self.MN[:, 1])
        dve.drain()
        for kt in range(KT):
            V.tensor_tensor(self.X[:, kt, :], self.X[:, kt, :], self.MN[:, 1], ALU.mult)
        dve.drain()
        for kt in range(KT):
            w, b = (PARAM[:, PAR[n] + kt:PAR[n] + kt + 1] for n in (self.wname, self.bname))
            V.tensor_scalar(self.X[:, kt, :], self.X[:, kt, :], w, b, ALU.mult, ALU.add)
            if per_tile:
                per_tile(kt)


def phase_out(nc, io, g, stack):
    m = Mem(nc, stack, "out")
    PS, RING, MOD, XT, H2 = g["PS"], g["RING"], g["MOD"], g["XT"], g["HT"]
    MIX = m.sb("MIX", [P, KT, T])
    TMP = m.sb("TMP", [P, 2, T])
    norm = Norm(nc, m, g, XT, "ln1_w", "ln1_b")
    w_in = m.sems("w_in", 4)
    mix_in, x_in, tile_done, x_ready, bank_free = (
        m.sem(x) for x in ("mix_in", "x_in", "tile_done", "x_ready", "bank_free"))

    with nc.Block() as block:
        @block.sync
        def _(sp):
            sp.dma_start(MIX[:], io["mix"].rearrange("k p t -> p k t")).then_inc(mix_in, 16)
            for k in range(4):
                sp.dma_start(RING[:, k, :], io["w_out"][k]).then_inc(w_in[k], 16)
            sp.dma_start(XT[:], io["xT"]).then_inc(x_in, 16)
            with sp.Fori(0, 3) as i:
                for k in range(4):
                    sp.wait_ge(tile_done, 4 * i + k + 1)
                    sp.dma_start(RING[:, k, :], io["w_out"][4 * i + (k + 4)]).then_inc(w_in[k], 16)

        @block.tensor
        def _(pe):
            pe.wait_ge(mix_in, 16)
            with pe.Fori(0, 4) as i:
                for k in range(4):
                    pe.wait_ge(bank_free, 4 * i + k + 1)
                    pe.wait_ge(w_in[k], 16 * i + 16)
                    for half in range(2):
                        for kt in range(KT):
                            mm = nc.tensor.matmul(PS[:, 2 * (k % 2) + half, 0:TH], RING[:, k, P * kt:P * kt + P],
                                                  MIX[:, kt, TH * half:TH * half + TH], start=(kt == 0), stop=(kt == KT - 1))
                    mm.then_inc(tile_done, 1)
            norm.tensor(pe, x_ready, 1)

        @block.scalar
        def _(act):
            norm.scalar(act)

        @block.vector
        def _(dve):
            V = nc.vector
            dve.sem_inc(bank_free, 2)
            norm.start(dve)
            dve.wait_ge(x_in, 16)
            with dve.Fori(0, 4) as i:
                for k in range(4):
                    ct = 4 * i + k
                    tmp = TMP[:, k % 2]
                    ps = PS[:, 2 * (k % 2):2 * (k % 2) + 2, 0:TH]
                    dve.wait_ge(tile_done, 4 * i + k + 1)
                    V.tensor_scalar(tmp[:, 0:TH], ps[:, 0], MOD[:, bass.ds(ct + 2 * KT, 1), 0:1].rearrange("p c b -> p (c b)"),
                                    None, ALU.mult)
                    V.tensor_scalar(tmp[:, TH:SEQ], ps[:, 1, 0:SEQ - TH],
                                    MOD[:, bass.ds(ct + 2 * KT, 1), 0:1].rearrange("p c b -> p (c b)"), None, ALU.mult)
                    V.tensor_tensor(samples4(tmp[:, SEQ:T]), samples4(ps[:, 1, SEQ - TH:TH]),
                                    bcast(MOD[:, bass.ds(ct + 2 * KT, 1), 1:9].rearrange("p c b -> p (c b)"), 2, NS), ALU.mult)
                    dve.drain().then_inc(bank_free, 1)
                    x = XT[:, bass.ds(ct, 1), :].rearrange("p c t -> p (c t)")
                    V.scalar_tensor_tensor(x, x, ALPHA, tmp, ALU.mult, ALU.add).then_inc(x_ready, 1)
            dve.drain()
            norm.vector(dve, None)
            dve.drain()
            for kt in range(KT):
                V.tensor_scalar(H2[:, kt, 0:SEQ], XT[:, kt, 0:SEQ], MOD[:, 4 * KT + kt, 0:1], MOD[:, 3 * KT + kt, 0:1],
                                ALU.mult, ALU.add)
            xs = XT[:, :, SEQ:T].rearrange("p k (b s) -> p k b s", s=NS)
            hs = H2[:, :, SEQ:T].rearrange("p k (b s) -> p k b s", s=NS)
            V.tensor_tensor(hs, xs, bcast(MOD[:, 4 * KT:5 * KT, 1:9], 3, NS), ALU.mult)
            dve.drain()
            V.tensor_tensor(hs, hs, bcast(MOD[:, 3 * KT:4 * KT, 1:9], 3, NS), ALU.add)


NT = 5


def phase_route(nc, io, g, stack):
    m = Mem(nc, stack, "rt")
    RT = m.sb("RT", [P, 3, NT * P])
    g["RT"] = RT
    run(route_scores, nc, io, g)
    run(gate_tables, nc, io, g)


def route_scores(nc, io, g, stack):
    m = Mem(nc, stack, "sc")
    PS, RING, H2, IDENT, RT = g["PS"], g["RING"], g["HT"], g["IDENT"], g["RT"]
    KEYS = m.sb("KEYS", [P, 2, NK])
    QT = m.sb("QT", [P, 2, NT * P])
    SC = m.sb("SC", [P, 2, 2, NT, NK])
    VV = m.sb("VV", [P, 2, NT, TOPK])
    II = m.sb("II", [P, 2, NT, TOPK], U32)
    IF = m.sb("IF", [P, 2, NT, TOPK])
    CA = m.sb("CA", [P, NT, TOPK, TOPK])
    EQ = m.sb("EQ", [P, NT, TOPK, TOPK])
    SV = m.sb("SV", [P, NT, HEADS, TOPK])
    SH = m.sb("SH", [P, NT, TOPK])
    SI = m.sb("SI", [P, NT, TOPK], U32)
    HL = m.sb("HL", [P, 2, NT, TOPK], U32)
    HF = m.sb("HF", [P, 2, NT, TOPK])
    EG = m.sb("EG", [P, NT, 3, P])
    SM1 = m.sb("SM1", [P, NT, HEADS])
    IO16 = m.sb("IO16", [P, TOPK])
    w_in = m.sems("w_in", 4)
    (keys_in, tile_done, bank_free, q_ready, sc_done, sc_free, sc_ready, iota_ready,
     ex_in, ex_ready, eg_ready, rt_ready, cleared, begun) = (m.sem(x) for x in (
        "keys_in tile_done bank_free q_ready sc_done sc_free sc_ready iota_ready "
        "ex_in ex_ready eg_ready rt_ready cleared begun").split())

    with nc.Block() as block:
        @block.sync
        def _(sp):
            for k in range(4):
                sp.dma_start(RING[:, k, :], io["w_q"][k]).then_inc(w_in[k], 16)
            sp.dma_start(KEYS[:], io["keys"]).then_inc(keys_in, 16)
            with sp.Fori(0, 3) as i:
                for k in range(4):
                    sp.wait_ge(tile_done, 4 * i + k + 1)
                    sp.dma_start(RING[:, k, :], io["w_q"][4 * i + (k + 4)]).then_inc(w_in[k], 16)

        @block.tensor
        def _(pe):
            def query(i, k):
                slot = k % 4
                pe.wait_ge(bank_free, 4 * i + (k + 1))
                pe.wait_ge(w_in[slot], 16 * i + 16 * (k // 4) + 16)
                for half in range(2):
                    for kt in range(KT):
                        mm = nc.tensor.matmul(PS[:, 2 * (k % 2) + half, 0:TH], RING[:, slot, P * kt:P * kt + P],
                                              H2[:, kt, TH * half:TH * half + TH], start=(kt == 0), stop=(kt == KT - 1))
                mm.then_inc(tile_done, 1)

            def scores(i, k):
                n = 4 * i + k
                pe.wait_ge(q_ready, n + 1)
                pe.wait_ge(sc_ready, n + 1)
                for t in range(NT):
                    mm = nc.tensor.matmul(PS[:, 4 + 2 * (k % 2) + t // 4, P * (t % 4):P * (t % 4) + P],
                                          QT[:, k % 2, P * t:P * t + P], KEYS[:, k % 2, :], start=True, stop=True)
                mm.then_inc(sc_done, 1)

            pe.wait_ge(keys_in, 16)
            query(0, 0)
            with pe.Fori(0, 3) as i:
                for k in range(4):
                    query(i, k + 1)
                    scores(i, k)
            for k in range(3):
                query(3, k + 1)
                scores(3, k)
            scores(3, 3)
            for t in range(NT):
                pe.wait_ge(eg_ready, 1)
                for j in range(3):
                    mm = nc.tensor.transpose(PS[:, t, P * j:P * j + P], EG[:, t, j, :], IDENT[:])
                mm.then_inc(rt_ready, 1)

        @block.scalar
        def _(act):
            A = nc.scalar.activation
            act.sem_inc(bank_free, 2)
            act.sem_inc(sc_ready, 1)
            act.wait_ge(cleared, 1)

            def query(k):
                A(QT[:, k % 2, 0:T].rearrange("p (h n) -> p h n", h=2), PS[:, 2 * (k % 2):2 * (k % 2) + 2, 0:TH],
                  ACT.Copy).then_inc(q_ready, 1)
                act.drain().then_inc(bank_free, 1)

            def scores(i, k):
                n = 4 * i + k
                head, half = k // 2, k % 2
                act.wait_ge(sc_done, n + 1)
                if half == 0:
                    act.wait_ge(sc_free, 2 * i + head + 1)
                A(SC[:, head % 2, half, 0:4, :].rearrange("p t k -> p (t k)"), PS[:, 4 + 2 * half, :], ACT.Copy)
                A(SC[:, head % 2, half, 4, :], PS[:, 5 + 2 * half, 0:P], ACT.Copy)
                act.drain().then_inc(sc_ready, 1)

            act.wait_ge(tile_done, 1)
            query(0)
            with act.Fori(0, 3) as i:
                for k in range(4):
                    act.wait_ge(tile_done, 4 * i + (k + 2))
                    query(k + 1)
                    scores(i, k)
            for k in range(3):
                act.wait_ge(tile_done, 12 + k + 2)
                query(k + 1)
                scores(3, k)
            scores(3, 3)
            act.wait_ge(ex_in, 1)
            A(SV[:], SV[:], ACT.Exp).then_inc(ex_ready, 1)
            for t in range(NT):
                act.wait_ge(rt_ready, t + 1)
                A(RT[:, :, P * t:P * t + P], PS[:, t, 0:3 * P].rearrange("p (j t) -> p j t", j=3), ACT.Copy)

        @block.gpsimd
        def _(pool):
            nc.gpsimd.iota(IO16[:], [[1, TOPK]], base=0, channel_multiplier=0,
                           allow_small_or_imprecise_dtypes=True).then_inc(iota_ready, 1)

        @block.vector
        def _(dve):
            V = nc.vector
            V.memset(QT[:], 0.0)
            dve.drain().then_inc(cleared, 1)
            dve.sem_inc(sc_free, 2)
            dve.wait_ge(iota_ready, 1)

            def best16(values, indices, data):
                for r in range(2):
                    at = slice(8 * r, 8 * r + 8)
                    for t in range(NT):
                        V.max(values[t][:, at], data[t])
                    dve.drain()
                    for t in range(NT):
                        V.max_index(indices[t][:, at], values[t][:, at], data[t])
                    if r == 0:
                        for t in range(NT):
                            V.match_replace(data[t], values[t][:, at], data[t], NEG)
                        dve.drain()

            def head(h, par):
                for half in range(2):
                    dve.wait_ge(sc_ready, 2 * h + (half + 2))
                    dve.sem_inc(begun, 1)
                    best16([VV[:, half, t] for t in range(NT)], [II[:, half, t] for t in range(NT)],
                           [SC[:, par, half, t, :] for t in range(NT)])
                dve.drain().then_inc(sc_free, 1)
                V.tensor_tensor(CA[:], bcast(VV[:, 0], 3, TOPK), bcast(VV[:, 1], 2, TOPK), ALU.add)
                V.tensor_copy(IF[:], II[:])
                dve.drain()
                best16([SH[:, t] for t in range(NT)], [SI[:, t] for t in range(NT)], [CA[:, t].rearrange("p a b -> p (a b)") for t in range(NT)])
                dve.drain()
                V.tensor_copy(SV[:, :, bass.ds(h, 1), :].rearrange("p t h k -> p t (h k)"), SH[:])
                V.tensor_scalar(HL[:, 0], SI[:], 4, None, ALU.logical_shift_right)
                V.tensor_scalar(HL[:, 1], SI[:], 15, None, ALU.bitwise_and)
                dve.drain()
                V.tensor_copy(HF[:], HL[:])
                dve.drain()
                for j in range(2):
                    V.tensor_tensor(EQ[:], bcast(HF[:, j], 3, TOPK), bcast(bcast(IO16[:], 1, TOPK), 1, NT), ALU.is_equal)
                    dve.drain()
                    V.tensor_tensor(EQ[:], EQ[:], bcast(IF[:, j], 2, TOPK), ALU.mult)
                    dve.drain()
                    V.tensor_reduce(EG[:, :, j, bass.ds(h * TOPK, TOPK)], EQ[:], AX.X, ALU.add)
                    dve.drain()

            with dve.Fori(0, HEADS // 2) as i:
                for par in range(2):
                    head(2 * i + par, par)
            V.tensor_copy(SM1[:], SV[:, :, :, 0])
            dve.drain()
            V.tensor_tensor(SV[:], SV[:], bcast(SM1[:], 3, TOPK), ALU.subtract)
            dve.drain().then_inc(ex_in, 1)
            dve.wait_ge(ex_ready, 1)
            V.tensor_reduce(SM1[:], SV[:], AX.X, ALU.add)
            dve.drain()
            V.reciprocal(SM1[:], SM1[:])
            dve.drain()
            V.tensor_tensor(EG[:, :, 2, :].rearrange("p t (h k) -> p t h k", h=HEADS), SV[:], bcast(SM1[:], 3, TOPK),
                            ALU.mult)
            dve.drain().then_inc(eg_ready, 1)


def gate_tables(nc, io, g, stack):
    m = Mem(nc, stack, "gt")
    PS, RT = g["PS"], g["RT"]
    IOTA = m.sb("IOTA", [P, NK])
    BATCH = 4
    NBUF = 4
    OH = m.sb("OH", [P, NBUF, 2, BATCH, NK])
    STG = m.sb("STG", [P, 2, NG, 16, JG])
    (iota_ready, oh_ready, oh_free, tab_done, bank_free, stg_ready) = (m.sem(x) for x in (
        "iota_ready oh_ready oh_free tab_done bank_free stg_ready").split())
    stored = m.sems("stored", 2)

    with nc.Block() as block:
        @block.gpsimd
        def _(pool):
            nc.gpsimd.iota(IOTA[:], [[1, NK]], base=0, channel_multiplier=0,
                           allow_small_or_imprecise_dtypes=True).then_inc(iota_ready, 1)

        @block.vector
        def _(dve):
            V = nc.vector
            dve.sem_inc(oh_free, NBUF)
            dve.wait_ge(iota_ready, 1)
            with dve.Fori(0, T // (NBUF * BATCH)) as i:
                for b in range(NBUF):
                    dve.wait_ge(oh_free, NBUF * i + b + 1)
                    for q in range(BATCH):
                        at = bass.ds(NBUF * BATCH * i + (BATCH * b + q), 1)
                        V.tensor_scalar(OH[:, b, 0, q, :], IOTA[:], RT[:, 0, at], RT[:, 2, at], ALU.is_equal, ALU.mult)
                        last = V.tensor_scalar(OH[:, b, 1, q, :], IOTA[:], RT[:, 1, at], None, ALU.is_equal)
                    last.then_inc(oh_ready, 1)

        @block.tensor
        def _(pe):
            with pe.Fori(0, T // (NBUF * BATCH)) as i:
                for b in range(NBUF):
                    pe.wait_ge(bank_free, NBUF * i + b + 1)
                    pe.wait_ge(oh_ready, NBUF * i + b + 1)
                    for q in range(BATCH):
                        mm = nc.tensor.matmul(PS[:, b, NK * q:NK * q + NK], OH[:, b, 0, q, :], OH[:, b, 1, q, :],
                                              start=True, stop=True)
                    mm.then_inc(tab_done, 1)

        @block.scalar
        def _(act):
            A = nc.scalar.activation
            act.sem_inc(bank_free, NBUF)

            def sixteen(i, half, first=False):
                if not first:
                    act.wait_ge(stored[half], 16 * i)
                for b in range(4):
                    act.wait_ge(tab_done, 8 * i + (4 * half + b + 1))
                    A(STG[:, half].rearrange("p g t j -> p t g j")[:, BATCH * b:BATCH * b + BATCH],
                      PS[:, b, :].rearrange("p (t g j) -> p t g j", t=BATCH, g=NG), ACT.Copy).then_inc(bank_free, 1)
                    act.sem_inc(oh_free, 1)
                act.drain().then_inc(stg_ready, 1)

            for half in range(2):
                sixteen(0, half, first=True)
            with act.Fori(1, T // 32) as i:
                for half in range(2):
                    sixteen(i, half)

        @block.sync
        def _(sp):
            gd = io["gd"].rearrange("g p t j -> p g t j")
            with sp.Fori(0, T // 32) as i:
                for half in range(2):
                    sp.wait_ge(stg_ready, 2 * i + half + 1)
                    sp.dma_start(gd[:, :, bass.ds(32 * i + 16 * half, 16), :].rearrange("p g t j -> p g (t j)"),
                                 STG[:, half].rearrange("p g t j -> p g (t j)")).then_inc(stored[half], 16)
            for half in range(2):
                sp.wait_ge(stored[half], 16 * (T // 32))


def phase_experts(nc, io, g, stack):
    m = Mem(nc, stack, "ex")
    PS, RING, H2, YA = g["PS"], g["RING"], g["HT"], g["YA"]
    GG = m.sb("GG", [P, 2, T, JG])
    HB = m.sb("HB", [P, JG, T])
    GE = m.sb("GE", [P, 2, T])
    w_in = m.sems("w_in", 4)
    g_in = m.sems("g_in", 2)
    (u_done, ge_ready, ge_free, ge_used, hb_ready, v_done, ya_ready, gg_free, bank_free) = (m.sem(x) for x in (
        "u_done ge_ready ge_free ge_used hb_ready v_done ya_ready gg_free bank_free").split())
    PER = 16

    with nc.Block() as block:
        @block.sync
        def _(sp):
            def load(slot, src):
                sp.dma_start(RING[:, slot, :], src).then_inc(w_in[slot], 16)

            def group(gi, par, last=False):
                for n in range(4, PER + 4):
                    if n < 12:
                        sp.wait_ge(u_done, 8 * gi + (n - 3))
                    else:
                        sp.wait_ge(v_done, 8 * gi + (n - 11))
                    if n < 8:
                        load(n % 4, io["peer_u"][8 * gi + n])
                    elif n < PER:
                        load(n % 4, io["peer_v"][gi, n - 8])
                    elif not last:
                        load(n % 4, io["peer_u"][8 * gi + (8 + n - PER)])
                    if n == 8 and not last:
                        sp.wait_ge(gg_free, gi + 1)
                        sp.dma_start(GG[:, 1 - par], io["gd"][gi + 1]).then_inc(g_in[1 - par], 16)

            for k in range(4):
                load(k, io["peer_u"][k])
            sp.dma_start(GG[:, 0], io["gd"][0]).then_inc(g_in[0], 16)
            with sp.Fori(0, NG // 2 - 1) as i:
                for par in range(2):
                    group(2 * i + par, par)
            group(NG - 2, 0)
            group(NG - 1, 1, last=True)

        @block.tensor
        def _(pe):
            with pe.Fori(0, NG) as gi:
                for j in range(JG):
                    pe.wait_ge(ge_free, 8 * gi + (j + 1))
                    pe.wait_ge(w_in[j % 4], 64 * gi + (16 * (j // 4) + 16))
                    for half in range(2):
                        for kt in range(KT):
                            mm = nc.tensor.matmul(PS[:, 2 * (j % 2) + half, 0:TH], RING[:, j % 4, P * kt:P * kt + P],
                                                  H2[:, kt, TH * half:TH * half + TH], start=(kt == 0), stop=(kt == KT - 1))
                    mm.then_inc(u_done, 1)
                for dp in range(8):
                    pe.wait_ge(w_in[dp % 4], 64 * gi + (16 * (dp // 4) + 48))
                    for dd in range(2):
                        ct = 2 * dp + dd
                        pe.wait_ge(bank_free, 16 * gi + (ct + 1))
                        for half in range(2):
                            for j in range(JG):
                                if ct == 0 and half == 0:
                                    pe.wait_ge(hb_ready, 8 * gi + (j + 1))
                                mm = nc.tensor.matmul(PS[:, 4 + 2 * (ct % 2) + half, 0:TH],
                                                      RING[:, dp % 4, 256 * j + P * dd:256 * j + P * dd + P],
                                                      HB[:, j, TH * half:TH * half + TH], start=(j == 0), stop=(j == JG - 1))
                        if dd == 0:
                            mm.then_inc(ya_ready, 1)
                    mm.then_inc(v_done, 1)

        @block.scalar
        def _(act):
            act.sem_inc(ge_free, 2)
            with act.Fori(0, NG) as gi:
                for j in range(JG):
                    act.wait_ge(u_done, 8 * gi + (j + 1))
                    act.wait_ge(ge_used, 8 * gi + (j + 1))
                    nc.scalar.activation(GE[:, j % 2].rearrange("p (h n) -> p h n", h=2),
                                         PS[:, 2 * (j % 2):2 * (j % 2) + 2, 0:TH], ACT.Gelu_apprx_tanh).then_inc(ge_ready, 1)
                    act.drain().then_inc(ge_free, 1)

        @block.vector
        def _(dve):
            V = nc.vector
            V.memset(YA[:], 0.0)
            dve.sem_inc(bank_free, 2)
            dve.sem_inc(ge_used, 2)
            dve.sem_inc(gg_free, 1)
            dve.drain()
            with dve.Fori(0, NG // 2) as i:
                for par in range(2):
                    dve.wait_ge(g_in[par], 16 * i + 16)
                    for j in range(JG):
                        dve.wait_ge(ge_ready, 16 * i + (8 * par + j + 1))
                        V.tensor_tensor(HB[:, j, :], GE[:, j % 2], GG[:, par, :, j], ALU.mult).then_inc(hb_ready, 1)
                        dve.drain().then_inc(ge_used, 1)
                    dve.sem_inc(gg_free, 1)
                    for ct in range(KT):
                        if ct % 2 == 0:
                            dve.wait_ge(ya_ready, 16 * i + (8 * par + ct // 2 + 1))
                        else:
                            dve.wait_ge(v_done, 16 * i + (8 * par + ct // 2 + 1))
                        V.tensor_tensor(YA[:, ct, :].rearrange("p (h n) -> p h n", h=2),
                                        YA[:, ct, :].rearrange("p (h n) -> p h n", h=2),
                                        PS[:, 4 + 2 * (ct % 2):6 + 2 * (ct % 2), 0:TH], ALU.add).then_inc(bank_free, 1)


def phase_final(nc, io, g, stack):
    m = Mem(nc, stack, "fin")
    MOD, XT, YA = g["MOD"], g["XT"], g["YA"]
    norm = Norm(nc, m, g, XT, "ln2_w", "ln2_b")
    x_ready, y_ready, y_out = m.sem("x_ready"), m.sem("y_ready"), m.sem("y_out")

    with nc.Block() as block:
        @block.tensor
        def _(pe):
            norm.tensor(pe, x_ready, 1)

        @block.scalar
        def _(act):
            norm.scalar(act)

        @block.vector
        def _(dve):
            V = nc.vector
            norm.start(dve)
            for kt in range(KT):
                V.tensor_scalar(YA[:, kt, 0:SEQ], YA[:, kt, 0:SEQ], MOD[:, 5 * KT + kt, 0:1], None, ALU.mult)
            ys = YA[:, :, SEQ:T].rearrange("p k (b s) -> p k b s", s=NS)
            V.tensor_tensor(ys, ys, bcast(MOD[:, 5 * KT:6 * KT, 1:9], 3, NS), ALU.mult)
            dve.drain()
            for kt in range(KT):
                V.scalar_tensor_tensor(XT[:, kt, :], XT[:, kt, :], ALPHA, YA[:, kt, :], ALU.mult, ALU.add)\
                    .then_inc(x_ready, 1)
            dve.drain()
            norm.vector(dve, lambda kt: dve.drain().then_inc(y_ready, 1) if kt % 4 == 3 else None)

        @block.sync
        def _(sp):
            for q in range(4):
                sp.wait_ge(y_ready, q + 1)
                sp.dma_start(io["y"][:, 4 * q:4 * q + 4, :], XT[:, 4 * q:4 * q + 4, :]).then_inc(y_out, 16)
            sp.wait_ge(y_out, 64)


def phase_rest(nc, io, g):
    with ExitStack() as tail:
        m = Mem(nc, tail, "tail")
        g["XT"] = m.sb("XT", [P, KT, T])
        run(phase_out, nc, io, g)
        run(phase_route, nc, io, g)
        g["YA"] = m.sb("YA", [P, KT, T])
        run(phase_experts, nc, io, g)
        run(phase_final, nc, io, g)


def program(nc, io):
    with ExitStack() as top:
        m = Mem(nc, top, "all")
        g = {
            "PS": top.enter_context(nc.psum_tensor("PS", [P, 8, 512], F32)),
            "RING": m.sb("RING", [P, 4, D]),
            "HT": m.sb("HT", [P, KT, TP]),
            "MOD": m.sb("MOD", [P, ADA, 9]),
            "PARAM": m.sb("PARAM", [P, NPAR]),
            "IDENT": m.sb("IDENT", [P, P]),
            "EPSG": m.sb("EPSG", [P, 2]),
        }
        with ExitStack() as mixer:
            mx = Mem(nc, mixer, "mix")
            g.update({
                "CS": mx.sb("CS", [P, KT, 9]), "BADA": mx.sb("BADA", [P, ADA]),
                "LR": mx.sb("LR", [P, 2, W1]), "BD": mx.sb("BD", [P, P]), "MASK": mx.sb("MASK", [P, 4, P]),
                "LM": mx.sb("LM", [P, 5, P]), "SM": mx.sb("SM", [P, W1]), "SP8": mx.sb("SP8", [P, 2, 8]),
            })
            run(phase_ada, nc, io, g)
            run(phase_lru, nc, io, g)
            run(phase_rwkv, nc, io, g)
        phase_rest(nc, io, g)


INPUTS = {
    "xT": (P, KT, T), "cT": (P, KT, 9), "shiftT": (P, KT, NB), "w_ada": (ADA, P, D), "b_ada": (P, ADA),
    "par": (P, NPAR), "w_in": (42, P, D), "w_gate": (8, P, 2, 64), "lru0": (P, 8, 8), "conv0": (P, 8, 24),
    "w_lr": (8, P, 2, P), "wkv0": (8, P, NB, 64), "w_out": (KT, P, D), "w_q": (KT, P, D), "keys": (P, 2, NK),
    "peer_u": (NK, P, D), "peer_v": (NG, 8, P, D),
}
OUTPUTS = {
    "y": (P, KT, T), "shift_out": (P, KT, 9), "wkv_p": (8, P, 64), "wkv_s": (8, P, NB, 64), "lru_out": (P, 8, 9),
    "conv_out": (P, 8, 27),
}
SCRATCH = {"mix": (KT, P, T), "gd": (NG, P, T, JG)}


def laid_out(i):
    import numpy as np

    def cols(v):
        return v.reshape(-1, P).T

    def tiles(w):
        k, c = w.shape
        return w.reshape(k // P, P, c // P, P).transpose(2, 1, 0, 3).reshape(c // P, P, -1)

    def chan(x):
        return x.T.reshape(-1, P, x.shape[0]).transpose(1, 0, 2)

    x = np.concatenate([i["x_prompt"][0], i["x_sample"].reshape(NB * NS, D)])
    c = np.concatenate([i["c_prompt"], i["c_sample"]])
    par = np.concatenate([cols(i[n][0].reshape(-1)) for n in (
        "mu_shift", "w0", "a0", "k_k", "k_a", "r_k", "lnx_w", "lnx_b", "conv_w", "conv_b", "b_gate_a", "b_gate_i",
        "lru_lambda", "ln1_w", "ln1_b", "ln2_w", "ln2_b")], axis=1)
    out = {
        "xT": chan(x), "cT": chan(c), "shiftT": chan(i["state_shift"][0]), "w_ada": tiles(i["w_ada"][0]),
        "b_ada": cols(i["b_ada"][0]), "par": par, "w_in": tiles(i["w_in"][0]),
        "w_gate": np.stack([i["w_gate_a"][0].reshape(8, P, 64), i["w_gate_i"][0].reshape(8, P, 64)], axis=2),
        "lru0": chan(i["state_lru"][0]),
        "conv0": chan(i["state_conv"][0].reshape(NB * 3, DA)),
        "w_lr": np.stack([np.concatenate([i["w_w2"][0], i["w_a2"][0]]).reshape(P, 8, P),
                          i["w_g2"][0].reshape(P, 8, P)], axis=2).transpose(1, 0, 2, 3),
        "wkv0": i["state_wkv"][0].transpose(1, 3, 0, 2).reshape(8, P, NB, 64),
        "w_out": tiles(i["w_out"][0]), "w_q": tiles(i["w_q"][0]),
        "keys": i["sub_keys"][0].transpose(2, 0, 1),
        "peer_u": i["peer_u"][0].reshape(P, NK, KT, P).transpose(1, 3, 2, 0).reshape(NK, P, D),
        "peer_v": i["peer_v"][0].reshape(P, NG, JG, 8, 256).transpose(1, 3, 0, 2, 4).reshape(NG, 8, P, D),
    }
    return {k: np.ascontiguousarray(v) for k, v in out.items()}


def gathered(o):
    def rows(x):
        return x.transpose(2, 1, 0).reshape(x.shape[2], -1)

    y, sh = rows(o["y"]), rows(o["shift_out"])
    lru, conv = rows(o["lru_out"]), rows(o["conv_out"]).reshape(9, 3, DA)
    wp = o["wkv_p"].reshape(16, 64, 64).transpose(0, 2, 1)
    ws = o["wkv_s"].reshape(16, 64, NB, 64).transpose(2, 0, 3, 1)
    return (y[None, :SEQ], y[SEQ:].reshape(NB, NS, D), sh[None, :1], wp[None, None], lru[None, :1], conv[None, :1],
            sh[None, 1:], ws[None], lru[None, 1:], conv[None, 1:])


def kernel(**inputs):
    import numpy as np
    import concourse.bacc as bacc
    from concourse.bass_utils import run_bass_kernel_spmd

    arrays = {f"in_{k}": v for k, v in laid_out({k: np.asarray(v) for k, v in inputs.items()}).items()}
    nc = bacc.Bacc("TRN2", target_bir_lowering=False, num_devices=1)
    io = {k: nc.dram_tensor(f"in_{k}", s, F32, kind="ExternalInput").ap() for k, s in INPUTS.items()}
    io.update({k: nc.dram_tensor(f"out_{k}", s, F32, kind="ExternalOutput").ap() for k, s in OUTPUTS.items()})
    io.update({k: nc.dram_tensor(f"tmp_{k}", s, F32).ap() for k, s in SCRATCH.items()})
    program(nc, io)
    r = run_bass_kernel_spmd(nc, [arrays], core_ids=[0]).results[0]
    return tuple(np.ascontiguousarray(x) for x in gathered({k: np.asarray(r[f"out_{k}"]) for k in OUTPUTS}))
```

```python
import concourse.bass as bass
from concourse import mybir
from concourse.alu_op_type import AluOpType as ALU
from contextlib import ExitStack

F32 = mybir.dt.float32
F32R = mybir.dt.float32r
U32 = mybir.dt.uint32
I32 = mybir.dt.int32
ACT = mybir.ActivationFunctionType
AX = mybir.AxisListType

P = 128
D = 2048
KT = D // P
SEQ = 512
NB, NS = 8, 4
T = SEQ + NB * NS
TH = T // 2
TP = SEQ + NB * (NS + 1)
SP5 = NB * (NS + 1)
TPH = TP // 2
PB = SEQ - TPH
W1 = TP + 1
DA = 1024
NPAIR = DA // P
ADA = 6 * KT
ADA_H = 2 * KT
ADA_PAIR = 8
CH_CHUNK = 32
NK = 128
HEADS, TOPK = 8, 16
JG = 8
HG = JG // 2
NG = NK // JG
ALPHA = 2.0 ** 0.25
LN_EPS, GN_EPS = 1e-5, 64e-5
EXP_HALF = 0.6065306597126334
C_LRU = 8.0
NEG = -3.0e38

PAR_SIZES = [("mu", 26), ("w0", 8), ("a0", 8), ("k_k", 8), ("k_a", 8), ("r_k", 8), ("lnx_w", 8), ("lnx_b", 8),
             ("conv_w", 32), ("conv_b", 8), ("b_ga", 8), ("b_gi", 8), ("lam", 8),
             ("ln1_w", 16), ("ln1_b", 16), ("ln2_w", 16), ("ln2_b", 16)]
PAR = {}
_at = 0
for _n, _s in PAR_SIZES:
    PAR[_n] = _at
    _at += _s
NPAR = _at


def samples5(ap, lo=1):
    return ap.rearrange("p (b s) -> p b s", s=NS + 1)[:, :, lo:NS + 1]


def halves(ap):
    return ap.rearrange("p (h n) -> p h n", h=2)


def samples4(ap):
    return ap.rearrange("p (b s) -> p b s", s=NS)


def r32(ap):
    return ap.bitcast(F32R)


def product(nc, out, wh, wl, xh, xl, first, last):
    nc.tensor.matmul(out, r32(wh), r32(xh), start=first, stop=False)
    nc.tensor.matmul(out, r32(wh), r32(xl), start=False, stop=False)
    return nc.tensor.matmul(out, r32(wl), r32(xh), start=False, stop=last)


def bcast(ap, axis, n):
    v = ap.unsqueeze(axis)
    shape = list(v.shape)
    shape[axis] = n
    return v.broadcast_to(shape)


class Mem:

    used = []

    def __init__(self, nc, stack, tag):
        self.nc, self.stack, self.tag = nc, stack, tag

    def sb(self, name, shape, dt=F32):
        return self.stack.enter_context(self.nc.sbuf_tensor(f"{self.tag}_{name}", shape, dt))

    def sem(self, name):
        s = self.stack.enter_context(self.nc.semaphore(f"{self.tag}_{name}"))
        Mem.used.append(s)
        return s

    def sems(self, name, n):
        return [self.sem(f"{name}{i}") for i in range(n)]


def run(phase, nc, io, g):
    with ExitStack() as stack:
        Mem.used = []
        phase(nc, io, g, stack)
        with nc.Block() as block:
            @block.sync
            def _(sp):
                for s in Mem.used:
                    sp.sem_clear(s)


def phase_ada(nc, io, g, stack):
    m = Mem(nc, stack, "ada")
    PS, RING, HT, MOD, PARAM, CS, BADA = (g[x] for x in ("PS", "RING", "HT", "MOD", "PARAM", "CS", "BADA"))
    IDENT = g["IDENT"]
    XT = m.sb("XT", [P, KT, T])
    MR = m.sb("MR", [9, 2, 4 * P])
    CT = m.sb("CT", [P, KT, 9])
    SHT = m.sb("SHT", [P, KT, NB])
    SHO = m.sb("SHO", [P, KT, 9])
    c_in, x_in, b_in, out_sem = m.sem("c_in"), m.sem("x_in"), m.sem("b_in"), m.sem("out")
    w_in = m.sems("w_in", 4)
    (tile_done, sig_ready, cs_ready, bank_free, rows_ready, turned, turned_free, ident_ready, h_ready) = (m.sem(x) for x in (
        "tile_done sig_ready cs_ready bank_free rows_ready turned turned_free ident_ready h_ready").split())

    with nc.Block() as block:
        @block.sync
        def _(sp):
            sp.dma_start(CT[:], io["cT"]).then_inc(c_in, 16)
            for k in range(4):
                sp.dma_start(RING[:, k, :], io["w_ada"][k]).then_inc(w_in[k], 16)
            sp.dma_start(BADA[:], io["b_ada"]).then_inc(b_in, 16)
            sp.dma_start(XT[:], io["xT"]).then_inc(x_in, 16)
            sp.dma_start(SHT[:], io["shiftT"]).then_inc(x_in, 16)
            sp.dma_start(PARAM[:], io["par"]).then_inc(x_in, 16)
            with sp.Fori(0, ADA_H // 4 - 1) as i:
                for k in range(4):
                    sp.wait_ge(tile_done, 4 * i + k + 1)
                    sp.dma_start(RING[:, k, :], io["w_ada"][4 * i + (4 + k)]).then_inc(w_in[k], 16)
            sp.wait_ge(h_ready, 1)
            sp.dma_start(io["shift_out"], SHO[:]).then_inc(out_sem, 16)
            sp.wait_ge(out_sem, 16)

        @block.scalar
        def _(act):
            act.wait_ge(c_in, 16)
            nc.scalar.activation(CS[:], CT[:], ACT.Sigmoid).then_inc(sig_ready, 1)
            act.sem_inc(bank_free, 2)
            with act.Fori(0, ADA_H // 8) as i:
                for b in range(2):
                    act.wait_ge(tile_done, 8 * i + 4 * b + 4)
                    nc.scalar.activation(MR[:, b, :], PS[0:9, b, :], ACT.Copy).then_inc(rows_ready, 1)
                    act.drain().then_inc(bank_free, 1)

        @block.gpsimd
        def _(pool):
            nc.gpsimd.memset(IDENT[:], 0.0)
            pool.drain()
            nc.gpsimd.affine_select(out=IDENT[:], in_=IDENT[:], compare_op=ALU.not_equal, fill=1.0, base=0,
                                    pattern=[[-1, P]], channel_multiplier=1)
            pool.drain().then_inc(ident_ready, 1)

        @block.tensor
        def _(pe):
            def group(i, b):
                pe.wait_ge(bank_free, 2 * i + b + 1)
                for c in range(4):
                    pe.wait_ge(w_in[c], 32 * i + (16 * b + 16))
                    for k in range(KT):
                        mm = nc.tensor.matmul(PS[0:9, b, P * c:P * c + P], CS[:, k, :], RING[:, c, P * k:P * k + P],
                                              start=(k == 0), stop=(k == KT - 1))
                    mm.then_inc(tile_done, 1)

            def turn(i, b):
                pe.wait_ge(rows_ready, 2 * i + b + 1)
                pe.wait_ge(turned_free, 2 * i + b + 1)
                for c in range(4):
                    mm = nc.tensor.matmul(PS[:, 2 + b, 9 * c:9 * c + 9], MR[:, b, P * c:P * c + P], IDENT[0:9, 0:9],
                                          start=True, stop=True)
                mm.then_inc(turned, 1)

            pe.wait_ge(cs_ready, 1)
            pe.wait_ge(ident_ready, 1)
            group(0, 0)
            with pe.Fori(0, ADA_H // 8 - 1) as i:
                group(i, 1)
                turn(i, 0)
                group(i + 1, 0)
                turn(i, 1)
            group(ADA_H // 8 - 1, 1)
            for b in range(2):
                turn(ADA_H // 8 - 1, b)

        @block.vector
        def _(dve):
            dve.sem_inc(turned_free, 2)
            dve.wait_ge(sig_ready, 1)
            nc.vector.tensor_tensor(CS[:], CS[:], CT[:], ALU.mult).then_inc(cs_ready, 1)
            dve.wait_ge(b_in, 16)
            dve.wait_ge(x_in, 48)
            nc.vector.tensor_copy(HT[:, :, SEQ:TP].rearrange("p k (b s) -> p k b s", s=NS + 1)[:, :, :, 0], SHT[:])
            with dve.Fori(0, ADA_H // 8) as i:
                for b in range(2):
                    dve.wait_ge(turned, 2 * i + b + 1)
                    at = bass.ds(8 * i + 4 * b, 4)
                    nc.vector.tensor_tensor(MOD[:, at, :], PS[:, 2 + b, 0:36].rearrange("p (c b) -> p c b", b=9),
                                            bcast(BADA[:, at], 2, 9), ALU.add).then_inc(turned_free, 1)
            dve.drain()
            nc.vector.tensor_scalar(MOD[:, KT:2 * KT, :], MOD[:, KT:2 * KT, :], 1.0, None, ALU.add)
            dve.drain()
            for k in range(KT):
                nc.vector.tensor_scalar(HT[:, k, 0:SEQ], XT[:, k, 0:SEQ], MOD[:, KT + k, 0:1], MOD[:, k, 0:1],
                                        ALU.mult, ALU.add)
            hs = HT[:, :, SEQ:TP].rearrange("p k (b s) -> p k b s", s=NS + 1)[:, :, :, 1:NS + 1]
            xs = XT[:, :, SEQ:T].rearrange("p k (b s) -> p k b s", s=NS)
            nc.vector.tensor_tensor(hs, xs, bcast(MOD[:, KT:2 * KT, 1:9], 3, NS), ALU.mult)
            dve.drain()
            nc.vector.tensor_tensor(hs, hs, bcast(MOD[:, 0:KT, 1:9], 3, NS), ALU.add)
            dve.drain()
            nc.vector.tensor_copy(SHO[:, :, 0:1], HT[:, :, SEQ - 1:SEQ])
            nc.vector.tensor_copy(SHO[:, :, 1:9],
                                  HT[:, :, SEQ:TP].rearrange("p k (b s) -> p k b s", s=NS + 1)[:, :, :, NS]).then_inc(h_ready, 1)


def phase_lru(nc, io, g, stack):
    m = Mem(nc, stack, "lru")
    PS, RING, HT, PARAM, LR = g["PS"], g["RING"], g["HT"], g["PARAM"], g["LR"]
    IDENT, BD, MASK, LM, SM, EPSG = (g[x] for x in ("IDENT", "BD", "MASK", "LM", "SM", "EPSG"))
    WG = m.sb("WG", [P, 2, 2, P])
    XP = m.sb("XP", [P, 2, 3 + SEQ + NB * 7])
    XC = m.sb("XC", [P, T])
    RG, IG, AA, TT, QQ, HS, GE = (m.sb(x, [P, T]) for x in ("RG", "IG", "AA", "TT", "QQ", "HS", "GE"))
    YB = m.sb("YB", [P, T])
    LRU0 = m.sb("LRU0", [P, 8, 8])
    CONV0 = m.sb("CONV0", [P, 8, 24])
    LRUO = m.sb("LRUO", [P, 8, 9])
    CVO = m.sb("CVO", [P, 8, 27])
    SPL = m.sb("SPL", [P, 4, 8])
    PT = m.sb("PT", [P, 2, W1])
    DT = m.sb("DT", [P, W1])
    IA = m.sb("IA", [P, 2, P], I32)
    IB = m.sb("IB", [P, 2, P], I32)
    BK = m.sb("BK", [P, 6, P])
    TMPS = m.sb("TMPS", [P, NB])
    st_in, out_sem, y_out = m.sem("st_in"), m.sem("out"), m.sem("y_out")
    w_in = m.sems("w_in", 4)
    wg_in = m.sems("wg_in", 2)
    names = ("slot_used", "wg_used", "lr_mm", "lr_ev", "lr_shift", "px_done", "pg_done", "px_free", "pg_free",
             "xp_ready", "xc_ready", "gates_done", "gates_free", "sig_ready", "a_ready", "q_ready", "s_ready",
             "ge_ready", "tile_done", "y_ready", "iota_ready", "sp_a", "sp_b", "sp_c")
    (slot_used, wg_used, lr_mm, lr_ev, lr_shift, px_done, pg_done, px_free, pg_free, xp_ready, xc_ready,
     gates_done, gates_free, sig_ready, a_ready, q_ready, s_ready, ge_ready, tile_done, y_ready, iota_ready,
     sp_a, sp_b, sp_c) = (m.sem(x) for x in names)
    y_free, cleared = m.sem("y_free"), m.sem("cleared")
    N0 = 24

    with nc.Block() as block:
        def load_gates(sp, i, slot):
            for blk in range(2):
                rows = slice(64 * blk, 64 * blk + 64)
                sp.dma_start(WG[rows, slot, :, rows], io["w_gate"][i][rows]).then_inc(wg_in[slot], 16)

        @block.sync
        def _(sp):
            for k in range(2):
                sp.dma_start(RING[:, k, :], io["w_in"][N0 + k]).then_inc(w_in[k], 16)
            sp.dma_start(LRU0[:], io["lru0"]).then_inc(st_in, 16)
            sp.dma_start(CONV0[:], io["conv0"]).then_inc(st_in, 16)
            for k in range(2):
                sp.dma_start(RING[:, 2 + k, :], io["w_in"][26 + 8 * k]).then_inc(w_in[2 + k], 16)
            sp.wait_ge(cleared, 1)
            load_gates(sp, 0, 0)
            for k in range(2):
                sp.wait_ge(slot_used, k + 1)
                sp.dma_start(RING[:, k, :], io["w_in"][27 + 8 * k]).then_inc(w_in[k], 16)
            load_gates(sp, 1, 1)
            with sp.Fori(0, 3) as j:
                for odd in range(2):
                    for k in range(2):
                        slot = 2 * (1 - odd) + k
                        sp.wait_ge(slot_used, 4 * j + (2 * odd + k + 3))
                        sp.dma_start(RING[:, slot, :], io["w_in"][2 * j + (28 + odd + 8 * k)]).then_inc(w_in[slot], 16)
                    sp.wait_ge(wg_used, 2 * j + odd + 1)
                    load_gates(sp, 2 * j + 2 + odd, odd)
            sp.wait_ge(tile_done, 9)
            sp.dma_start(io["lru_out"], LRUO[:]).then_inc(out_sem, 16)
            sp.dma_start(io["conv_out"], CVO[:]).then_inc(out_sem, 16)
            sp.wait_ge(out_sem, 32)

        def lr_project(pe, k):
            pe.wait_ge(w_in[k], 16)
            for half in range(2):
                for kt in range(KT):
                    mm = nc.tensor.matmul(PS[:, 2 * k + half, 0:TPH], RING[:, k, P * kt:P * kt + P],
                                          HT[:, kt, TPH * half:TPH * half + TPH], start=(kt == 0), stop=(kt == KT - 1))
            mm.then_inc(slot_used, 1)
            pe.drain().then_inc(lr_mm, 1)

        @block.tensor
        def _(pe):
            for k in range(2):
                lr_project(pe, k)

            def project(j, odd, k):
                free, done = ((px_free, px_done), (pg_free, pg_done))[k]
                slot = 2 * (1 - odd) + k
                pe.wait_ge(free, 2 * j + odd + 1)
                pe.wait_ge(w_in[slot], 16 * j + (32 if odd else 16))
                for half in range(2):
                    for kt in range(KT):
                        mm = nc.tensor.matmul(PS[:, 2 * k + half, 0:TPH], RING[:, slot, P * kt:P * kt + P],
                                              HT[:, kt, TPH * half:TPH * half + TPH], start=(kt == 0), stop=(kt == KT - 1))
                mm.then_inc(slot_used, 1)
                pe.drain().then_inc(done, 1)

            def gates(j, odd):
                pe.wait_ge(xc_ready, 2 * j + odd + 1)
                pe.wait_ge(wg_in[odd], 32 * j + 32)
                pe.wait_ge(gates_free, 2 * j + odd + 1)
                for gate in range(2):
                    for half in range(2):
                        mm = nc.tensor.matmul(PS[:, 4 + 2 * gate + half, 0:TH], WG[:, odd, gate, :],
                                              XC[:, TH * half:TH * half + TH], start=True, stop=True)
                mm.then_inc(wg_used, 1)
                pe.drain().then_inc(gates_done, 1)

            project(0, 0, 0)
            project(0, 0, 1)
            with pe.Fori(0, 3) as j:
                project(j, 1, 0)
                gates(j, 0)
                project(j, 1, 1)
                project(j + 1, 0, 0)
                gates(j, 1)
                project(j + 1, 0, 1)
            project(3, 1, 0)
            gates(3, 0)
            project(3, 1, 1)
            gates(3, 1)

        @block.scalar
        def _(act):
            act.wait_ge(cleared, 1)
            for k in range(2):
                act.wait_ge(lr_mm, k + 1)
                nc.scalar.activation(halves(PT[:, k, 1:W1]), PS[:, 2 * k:2 * k + 2, 0:TPH], ACT.Copy).then_inc(lr_ev, 1)
            act.drain().then_inc(px_free, 1)
            act.sem_inc(pg_free, 1)
            act.sem_inc(gates_free, 1)
            act.wait_ge(lr_shift, 2)
            nc.scalar.activation(LR[0:64, 0, 1:W1], LR[0:64, 0, 1:W1], ACT.Tanh)
            nc.scalar.activation(LR[:, 1, 1:W1], LR[:, 1, 1:W1], ACT.Sigmoid)
            act.wait_ge(sp_a, 1)
            nc.scalar.activation(SPL[:, 1], SPL[:, 0], ACT.Exp, scale=-1.0).then_inc(sp_b, 1)
            act.wait_ge(sp_a, 2)
            nc.scalar.activation(SPL[:, 3], SPL[:, 2], ACT.Ln).then_inc(sp_b, 1)

            def x_branch(i, par):
                act.wait_ge(px_done, i + 1)
                nc.scalar.activation(XP[:, par, 3:3 + TPH], PS[:, 0, 0:TPH], ACT.Copy)
                nc.scalar.activation(XP[:, par, 3 + TPH:3 + SEQ], PS[:, 1, 0:PB], ACT.Copy)
                nc.scalar.activation(XP[:, par, 3 + SEQ:].rearrange("p (b s) -> p b s", s=7)[:, :, 3:7],
                                     samples5(PS[:, 1, PB:TPH]), ACT.Copy).then_inc(xp_ready, 1)
                act.drain().then_inc(px_free, 1)

            def gate_branch(i):
                act.wait_ge(pg_done, i + 1)
                act.wait_ge(tile_done, i + 1)
                nc.scalar.activation(GE[:, 0:TPH], PS[:, 2, 0:TPH], ACT.Gelu_apprx_tanh)
                nc.scalar.activation(GE[:, TPH:SEQ], PS[:, 3, 0:PB], ACT.Gelu_apprx_tanh)
                nc.scalar.activation(samples4(GE[:, SEQ:T]), samples5(PS[:, 3, PB:TPH]),
                                     ACT.Gelu_apprx_tanh).then_inc(ge_ready, 1)
                act.drain().then_inc(pg_free, 1)

            def tile(i, par, last=False):
                act.wait_ge(gates_done, i + 1)
                nc.scalar.activation(RG[:].rearrange("p (h n) -> p h n", h=2), PS[:, 4:6, 0:TH], ACT.Sigmoid,
                                     bias=PARAM[:, bass.ds(i + PAR["b_ga"], 1)])
                nc.scalar.activation(IG[:].rearrange("p (h n) -> p h n", h=2), PS[:, 6:8, 0:TH], ACT.Sigmoid,
                                     bias=PARAM[:, bass.ds(i + PAR["b_gi"], 1)]).then_inc(sig_ready, 1)
                act.drain().then_inc(gates_free, 1)
                act.wait_ge(sp_c, 1)
                nc.scalar.activation(TT[:], RG[:], ACT.Tanh, scale=g["SP8"][:, 0, bass.ds(i, 1)]).then_inc(a_ready, 1)
                nc.scalar.activation(AA[:], RG[:], ACT.Exp, scale=g["SP8"][:, 1, bass.ds(i, 1)]).then_inc(a_ready, 1)
                if not last:
                    x_branch(i + 1, 1 - par)
                act.wait_ge(q_ready, i + 1)
                nc.scalar.activation(QQ[:], QQ[:], ACT.Sqrt).then_inc(s_ready, 1)
                if not last:
                    gate_branch(i + 1)

            x_branch(0, 0)
            gate_branch(0)
            with act.Fori(0, 3) as j:
                for odd in range(2):
                    tile(2 * j + odd, odd)
            tile(6, 0)
            tile(7, 1, last=True)

        @block.gpsimd
        def _(pool):
            nc.gpsimd.iota(IA[:, 0, :], [[0, P]], base=0, channel_multiplier=1)
            nc.gpsimd.iota(IA[:, 1, :], [[1, P]], base=0, channel_multiplier=0)
            pool.drain().then_inc(iota_ready, 1)
            pool.sem_inc(y_free, 1)
            with pool.Fori(0, 8) as i:
                pool.wait_ge(y_ready, i + 1)
                pool.dma_start(io["mix"][8 + i], YB[:]).then_inc(y_out, 16)
                pool.wait_ge(y_out, 16 * i + 16)
                pool.sem_inc(y_free, 1)

        @block.vector
        def _(dve):
            V = nc.vector
            V.memset(EPSG[:, 0:1], GN_EPS)
            V.memset(EPSG[:, 1:2], LN_EPS)
            V.memset(BD[:], 0.0)
            V.memset(SM[:], 0.0)
            V.memset(LR[:], 0.0)
            V.memset(PT[:], 0.0)
            V.memset(XP[:], 0.0)
            V.memset(WG[:], 0.0)
            dve.drain().then_inc(cleared, 1)
            V.memset(BD[0:64, 0:64], 1.0)
            V.memset(BD[64:128, 64:128], 1.0)
            V.memset(SM[:, 1:1 + SEQ].rearrange("p (c s) -> p c s", s=CH_CHUNK)[:, :, 0], 1.0)
            V.memset(SM[:, 1 + SEQ:W1].rearrange("p (b s) -> p b s", s=NS + 1)[:, :, 1], 1.0)
            dve.wait_ge(iota_ready, 1)
            for n in range(6):
                V.tensor_scalar(IB[:], IA[:], n, None, ALU.logical_shift_right)
                dve.drain()
                V.tensor_tensor(BK[:, n, :], IB[:, 0, :], IB[:, 1, :], ALU.is_equal)
                dve.drain()
            V.tensor_tensor(MASK[:, 0, :], IA[:, 0, :], IA[:, 1, :], ALU.is_lt)
            V.tensor_tensor(MASK[:, 1, :], IA[:, 0, :], IA[:, 1, :], ALU.is_le)
            dve.drain()
            for lv in range(5):
                V.tensor_tensor(LM[:, lv, :], BK[:, lv + 1, :], BK[:, lv, :], ALU.subtract)
            dve.drain()
            for lv in range(5):
                V.tensor_tensor(LM[:, lv, :], LM[:, lv, :], MASK[:, 0, :], ALU.mult)
            dve.drain()
            for k in range(2):
                V.tensor_tensor(MASK[:, k, :], MASK[:, k, :], BK[:, 5, :], ALU.mult)
            dve.drain()
            V.tensor_copy(MASK[:, 2:4, :], MASK[:, 0:2, :])
            for k in range(2):
                dve.wait_ge(lr_ev, k + 1)
                V.tensor_tensor(DT[:, 1:W1], PT[:, k, 0:W1 - 1], PT[:, k, 1:W1], ALU.subtract)
                dve.drain()
                c = PAR["mu"] + N0 + k
                V.scalar_tensor_tensor(LR[:, k, 1:W1], DT[:, 1:W1], PARAM[:, c:c + 1], PT[:, k, 1:W1], ALU.mult, ALU.add)
                dve.drain().then_inc(lr_shift, 1)
            lam = PARAM[:, PAR["lam"]:PAR["lam"] + 8]
            SP8 = g["SP8"]
            V.tensor_scalar(SPL[:, 0], lam, -1.0, None, ALU.mult)
            dve.drain()
            V.tensor_tensor(SPL[:, 0], SPL[:, 0], lam, ALU.max)
            dve.drain().then_inc(sp_a, 1)
            dve.wait_ge(sp_b, 1)
            V.tensor_scalar(SPL[:, 2], SPL[:, 1], 1.0, None, ALU.add)
            dve.drain().then_inc(sp_a, 1)
            dve.wait_ge(sp_b, 2)
            V.tensor_scalar(SPL[:, 2], SPL[:, 2], -1.0, None, ALU.add)
            dve.drain()
            V.tensor_scalar(SPL[:, 0], SPL[:, 2], 0.0, None, ALU.is_equal)
            dve.drain()
            V.tensor_tensor(SPL[:, 2:4], SPL[:, 2:4], bcast(SPL[:, 0], 1, 2), ALU.add)
            dve.drain()
            V.reciprocal(SPL[:, 2], SPL[:, 2])
            V.tensor_tensor(SPL[:, 1], SPL[:, 1], SPL[:, 3], ALU.mult)
            V.tensor_scalar(SPL[:, 0], lam, -1.0, 0.0, ALU.mult, ALU.max)
            dve.drain()
            V.tensor_tensor(SPL[:, 1], SPL[:, 1], SPL[:, 2], ALU.mult)
            dve.drain()
            V.tensor_tensor(SPL[:, 1], SPL[:, 1], SPL[:, 0], ALU.add)
            dve.drain()
            V.tensor_scalar(SP8[:, 0], SPL[:, 1], C_LRU, None, ALU.mult)
            V.tensor_scalar(SP8[:, 1], SPL[:, 1], -C_LRU, None, ALU.mult)
            dve.drain().then_inc(sp_c, 1)
            dve.wait_ge(st_in, 32)
            dve.sem_inc(tile_done, 1)

            def tile(i, par):
                xp = XP[:, par]
                xps = xp[:, 3 + SEQ:].rearrange("p (b s) -> p b s", s=7)
                V.tensor_copy(xps[:, :, 0:3], CONV0[:, bass.ds(i, 1), :].rearrange("p i (b s) -> p (i b) s", s=3))
                dve.drain()
                dve.wait_ge(xp_ready, i + 1)
                cw = [PARAM[:, bass.ds(i + (PAR["conv_w"] + 8 * j), 1)] for j in range(4)]
                cb = PARAM[:, bass.ds(i + PAR["conv_b"], 1)]
                xcs = samples4(XC[:, SEQ:T])
                V.tensor_scalar(XC[:, 0:SEQ], xp[:, 0:SEQ], cw[0], cb, ALU.mult, ALU.add)
                V.tensor_scalar(xcs, xps[:, :, 0:4], cw[0], cb, ALU.mult, ALU.add)
                for j in range(1, 4):
                    dve.drain()
                    V.scalar_tensor_tensor(XC[:, 0:SEQ], xp[:, j:j + SEQ], cw[j], XC[:, 0:SEQ], ALU.mult, ALU.add)
                    V.scalar_tensor_tensor(xcs, xps[:, :, j:j + 4], cw[j], xcs, ALU.mult, ALU.add)
                dve.drain().then_inc(xc_ready, 1)
                cvo = CVO[:, bass.ds(i, 1), :].rearrange("p i (b s) -> p (i b) s", s=3)
                V.tensor_copy(cvo[:, 0:1, :], xp[:, SEQ:SEQ + 3].unsqueeze(1))
                V.tensor_copy(cvo[:, 1:9, :], xps[:, :, 4:7])
                dve.wait_ge(a_ready, 2 * i + 1)
                V.tensor_scalar(HS[:], TT[:], 1.0, None, ALU.add)
                V.tensor_scalar(QQ[:], TT[:], 2.0, 1e-30, ALU.mult, ALU.max)
                dve.drain()
                V.reciprocal(HS[:], HS[:])
                dve.drain()
                V.tensor_tensor(QQ[:], QQ[:], HS[:], ALU.mult)
                dve.drain().then_inc(q_ready, 1)
                V.tensor_tensor(IG[:], IG[:], XC[:], ALU.mult)
                dve.drain()
                dve.wait_ge(s_ready, i + 1)
                V.tensor_tensor(QQ[:], QQ[:], IG[:], ALU.mult)
                dve.wait_ge(a_ready, 2 * i + 2)
                a0 = samples4(AA[:, SEQ:T])[:, :, 0]
                g0 = samples4(QQ[:, SEQ:T])[:, :, 0]
                V.tensor_tensor(TMPS[:], a0, LRU0[:, bass.ds(i, 1), :].rearrange("p i b -> p (i b)"), ALU.mult)
                dve.drain()
                V.tensor_tensor(g0, g0, TMPS[:], ALU.add)
                V.memset(a0, 0.0)
                dve.drain()
                V.tensor_tensor_scan(HS[:], AA[:], QQ[:], 0.0, ALU.mult, ALU.add)
                dve.drain()
                lo = LRUO[:, bass.ds(i, 1), :].rearrange("p i b -> p (i b)")
                V.tensor_copy(lo[:, 0:1], HS[:, SEQ - 1:SEQ])
                V.tensor_copy(lo[:, 1:9], samples4(HS[:, SEQ:T])[:, :, NS - 1])
                dve.wait_ge(ge_ready, i + 1)
                dve.wait_ge(y_free, i + 1)
                V.tensor_tensor(YB[:], HS[:], GE[:], ALU.mult)
                dve.drain().then_inc(y_ready, 1)
                dve.sem_inc(tile_done, 1)

            with dve.Fori(0, 4) as j:
                for odd in range(2):
                    tile(2 * j + odd, odd)


KA_, KR_, KB_, KK_, KBH, KKH, KV_ = range(7)


def phase_rwkv(nc, io, g, stack):
    m = Mem(nc, stack, "rw")
    PS, RING, HT, PARAM, LR = g["PS"], g["RING"], g["HT"], g["PARAM"], g["LR"]
    IDENT, BD, MASK, LM, SM, EPSG = (g[x] for x in ("IDENT", "BD", "MASK", "LM", "SM", "EPSG"))
    MOD, CS, BADA = g["MOD"], g["CS"], g["BADA"]
    WLR = m.sb("WLR", [P, 2, P])
    PP = m.sb("PP", [P, 3, W1])
    RR, KX, WD, AG, GN, G2, DT, PX, PI, RPI, SQ, NR = (m.sb(x, [P, W1]) for x in (
        "RR", "KX", "WD", "AG", "GN", "G2", "DT", "PX", "PI", "RPI", "SQ", "NR"))
    BO, YT, YC = (m.sb(x, [P, T]) for x in ("BO", "YT", "YC"))
    OMK = m.sb("OMK", [P, 8])
    BDM = m.sb("BDM", [P, P])
    CHN = m.sb("CHN", [P, 7, W1])
    SLT = m.sb("SLT", [P, 7, 2 * P])
    MM = m.sb("MM", [P, 4, 4, P])
    LT = m.sb("LT", [P, 2, 4, P])
    TB = m.sb("TB", [P, 2, 4, P])
    ZS = m.sb("ZS", [P, 4, P])
    TK = m.sb("TK", [P, 2, 3, P])
    AXX = m.sb("AXX", [P, 4, 2, 64])
    AW = m.sb("AW", [P, 2, 2, 2, 64])
    R2 = m.sb("R2", [P, 2, P])
    Y0 = m.sb("Y0", [P, 2, P])
    GS = m.sb("GS", [P, 8, P])
    K0 = m.sb("K0", [P, 8, P])
    DG = m.sb("DG", [P, 8, P])
    SB = m.sb("SB", [P, 9, P])
    SI = m.sb("SI", [P, 8, P])
    SO = m.sb("SO", [P, 8, P])
    w_in = m.sems("w_in", 3)
    wlr_in, si_in, so_out, sp_out, y_out = (m.sem(x) for x in ("wlr_in", "si_in", "so_out", "sp_out", "y_out"))
    MR = m.sb("MR", [9, 3 * P])
    ada_in, ada_used, mr_ready, turned, mod_read = (m.sem(x) for x in "ada_in ada_used mr_ready turned mod_read".split())
    (cleared, slot_used, proj_done, proj_ev, gk_free, banks_idle, act_rows, rows_used, sq_ready, ss_done, ss_ready,
     nr_ready, rk_ready, bo_done, rows_in, g2_free, prep_ready, tr_done, tr_ready, mm_prod, mm_ready, lt_ready,
     dg_ready, x_done, x_ready, z_done, z_ready, t_done, t_ready, aw_done, aw_ready, ry_done, y0_ready,
     r2_ready, gk_done, gk_read, gk_ready, s_done, s_ready, yy_done, yt_ready, mean_done, yc_ready, ysq_ready, var_done,
     sd_ready, post_done, mix_free, so_ready, so_free, sp_ready, sp_free) = (m.sem(x) for x in (
        "cleared slot_used proj_done proj_ev gk_free banks_idle act_rows rows_used sq_ready ss_done ss_ready "
        "nr_ready rk_ready bo_done rows_in g2_free prep_ready tr_done tr_ready mm_prod mm_ready lt_ready "
        "dg_ready x_done x_ready z_done z_ready t_done t_ready aw_done aw_ready ry_done y0_ready "
        "r2_ready gk_done gk_read gk_ready s_done s_ready yy_done yt_ready mean_done yc_ready ysq_ready var_done "
        "sd_ready post_done mix_free so_ready so_free sp_ready sp_free").split())
    PC0, PC1 = 1 + SEQ, W1

    MODS = (3, 3, 2)
    LEVELS = (5, 5, 2)

    def per_level(i, step, lo):
        return sum(2 * (n - lo) for n in LEVELS) * i + sum(2 * (n - lo) for n in LEVELS[:step])

    def chan_view(kind, x, step):
        if step < 2:
            lo = 1 + 2 * P * step + P * x
            return CHN[:, kind, lo:lo + P]
        return SLT[:, kind, P * x:P * x + P]

    def two_kinds(rows, kind, x, step):
        if step < 2:
            lo = 1 + 2 * P * step + P * x
            return CHN[rows, kind:kind + 2, lo:lo + P]
        return SLT[rows, kind:kind + 2, P * x:P * x + P]

    with nc.Block() as block:
        @block.sync
        def _(sp):
            for k in range(3):
                sp.dma_start(RING[:, k, :], io["w_in"][8 * k]).then_inc(w_in[k], 16)
            sp.dma_start(WLR[:], io["w_lr"][0]).then_inc(wlr_in, 16)

            def load_ada(n):
                sp.dma_start(RING[:, 3, :], io["w_ada"][n]).then_inc(ada_in, 16)

            def load_pair(i):
                for k in range(3):
                    sp.wait_ge(slot_used, 4 * i + (k - 3))
                    sp.dma_start(RING[:, k, :], io["w_in"][i + 8 * k]).then_inc(w_in[k], 16)
                sp.wait_ge(slot_used, 4 * i)
                sp.dma_start(WLR[:], io["w_lr"][i]).then_inc(wlr_in, 16)

            def load_modulation(i, tiles):
                for t in range(tiles):
                    sp.wait_ge(ada_used, ADA_PAIR * i + (t + 1))
                    load_ada(ADA_PAIR * i + (ADA_H + t + 1))

            load_ada(ADA_H)
            load_pair(1)
            with sp.Fori(0, NPAIR - 2) as i:
                load_pair(i + 2)
                load_modulation(i, ADA_PAIR)
            load_modulation(NPAIR - 2, ADA_PAIR)
            load_modulation(NPAIR - 1, ADA_PAIR - 1)

        BANKS = (6, 2, 4, 6, 2, 4)

        def project(pe, i, which, part=(0, 1)):
            for half in part:
                if half == 0:
                    pe.wait_ge(w_in[which], 16 * i + 16)
                for kt in range(KT):
                    mm = nc.tensor.matmul(PS[:, BANKS[which] + half, 0:TPH], RING[:, which, P * kt:P * kt + P],
                                          HT[:, kt, TPH * half:TPH * half + TPH], start=(kt == 0), stop=(kt == KT - 1))
            if half == 1:
                mm.then_inc(slot_used, 1)
                pe.drain().then_inc(proj_done, 1)

        def project_low(pe, i):
            pe.wait_ge(wlr_in, 16 * i + 16)
            for n, (lhs, rhs) in enumerate(((WLR[0:64, 0, :], LR[0:64, 0, :]), (WLR[64:P, 0, :], LR[64:P, 0, :]),
                                            (WLR[:, 1, :], LR[:, 1, :]))):
                pe.wait_ge(proj_ev, 6 * i + (n + 1))
                for half in range(2):
                    mm = nc.tensor.matmul(PS[:, BANKS[3 + n] + half, 0:TPH], lhs,
                                          rhs[:, 1 + TPH * half:1 + TPH * half + TPH], start=True, stop=True)
                if n == 2:
                    mm.then_inc(slot_used, 1)
                pe.drain().then_inc(proj_done, 1)

        def head_sum(pe, ready, value, done):
            pe.wait_ge(ready, value)
            for half in range(2):
                mm = nc.tensor.matmul(PS[:, half, 0:TPH], BD[:], SQ[:, 1 + TPH * half:1 + TPH * half + TPH],
                                      start=True, stop=True)
            mm.then_inc(done, 1)

        def evacuate(act, i):
            A = nc.scalar.activation
            w0, a0 = (PARAM[:, bass.ds(i + PAR[n], 1)] for n in ("w0", "a0"))
            for which in range(6):
                act.wait_ge(proj_done, 6 * i + (which + 1))
                src = PS[:, BANKS[which]:BANKS[which] + 2, 0:TPH]
                dst = halves((PP[:, which] if which < 3 else (WD, AG, GN)[which - 3])[:, 1:W1])
                if which == 3:
                    A(dst, src, ACT.Sigmoid, bias=w0).then_inc(proj_ev, 1)
                elif which == 4:
                    A(dst, src, ACT.Sigmoid, bias=a0).then_inc(proj_ev, 1)
                else:
                    A(dst, src, ACT.Copy).then_inc(proj_ev, 1)
            act.drain()
            A(WD[:, 1:W1], WD[:, 1:W1], ACT.Exp, scale=-EXP_HALF).then_inc(rows_in, 1)

        def pe_scan(pe, i, step, n):
            pe.wait_ge(s_ready, 18 * i + 9 * step + n + 1)
            nc.tensor.matmul(PS[:, 7, CH_CHUNK * n:CH_CHUNK * n + CH_CHUNK], SB[:, n, :],
                             R2[:, n // 4, 32 * (n % 4):32 * (n % 4) + 32], start=True, stop=True)
            nc.tensor.matmul(PS[:, 7, 256 + P * (n % 2):256 + P * (n % 2) + P], GS[:, n, :], SB[:, n, :],
                             start=True, stop=True).then_inc(s_done, 1)

        def pe_modulation(pe, i, t, lo=0, hi=KT):
            if lo == 0:
                if t in (3, 6):
                    pe.wait_ge(mod_read, 3 * i + t // 3)
                pe.wait_ge(ada_in, 16 * ADA_PAIR * i + 16 * (t + 1))
            for k in range(lo, hi):
                mm = nc.tensor.matmul(PS[0:9, 6, P * (t % 3):P * (t % 3) + P], CS[:, k, :], RING[:, 3, P * k:P * k + P],
                                      start=(k == 0), stop=(k == KT - 1))
            if hi == KT:
                mm.then_inc(ada_used, 1)

        def pe_turn(pe, i, step):
            pe.wait_ge(mr_ready, 3 * i + step + 1)
            for c in range(MODS[step]):
                mm = nc.tensor.matmul(PS[:, 6, 3 * P + 9 * c:3 * P + 9 * c + 9], MR[:, P * c:P * c + P], IDENT[0:9, 0:9],
                                      start=True, stop=True)
            mm.then_inc(turned, 1)

        def pe_step(pe, i, step):
            u = 3 * i + step
            if step:
                pe.wait_ge(y0_ready, 2 * u)
            for x in range(2):
                for c, kind in enumerate((KA_, KBH, KKH, KV_)):
                    mm = nc.tensor.transpose(PS[:, 4 + x, P * c:P * c + P], chan_view(kind, x, step), IDENT[:])
                mm.then_inc(tr_done, 1)
            if step:
                pe.wait_ge(gk_read, u)
            for q in range(4):
                x, h = q // 2, q % 2
                rows = slice(64 * h, 64 * h + 64)
                for c, kind in enumerate((KB_, KK_)):
                    mm = nc.tensor.matmul(PS[:, q, 256 * c:256 * c + 256], chan_view(kind, x, step)[rows],
                                          two_kinds(rows, KA_, x, step), start=True, stop=True)
                mm.then_inc(mm_prod, 1)
            if step:
                pe_turn(pe, i, step - 1)
            for x in range(2):
                pe.wait_ge(mm_ready, 4 * u + (2 * x + 2))
                pe.wait_ge(tr_ready, 2 * u + (x + 1))
                for h in range(2):
                    mm = nc.tensor.matmul(PS[:, 4 + x, 64 * h:64 * h + 64], MM[:, 2, 2 * x + h, :],
                                          TK[:, x, 2, 64 * h:64 * h + 64], start=True, stop=True)
                mm.then_inc(x_done, 1)
            if step:
                pe.wait_ge(gk_ready, u)
            n0, n1 = per_level(i, step, 0), per_level(i, step, 1)
            last = LEVELS[step] - 1
            for lv in range(last + 1):
                for x in range(2):
                    pe.wait_ge(lt_ready, n0 + (2 * lv + x + 1))
                    if lv:
                        pe.wait_ge(t_ready, n0 + (2 * lv + x - 1))
                    for h in range(2):
                        q = 2 * x + h
                        if lv == 0:
                            mm = nc.tensor.transpose(PS[:, 2 * x, P * h:P * h + P], LT[:, 0, q, :], IDENT[:])
                        else:
                            mm = nc.tensor.matmul(PS[:, 2 * x, P * h:P * h + P], LT[:, lv % 2, q, :], TB[:, 0, q, :],
                                                  start=True, stop=True)
                    mm.then_inc(z_done, 1)
                if lv == 0:
                    continue
                if step:
                    pe_scan(pe, i, step - 1, 2 * lv - 2)
                if step == 2:
                    pe_modulation(pe, i, 6, 0, 5)
                    pe_scan(pe, i, 1, 1)
                    pe_modulation(pe, i, 6, 5, 10)
                    pe_scan(pe, i, 1, 2)
                    pe_modulation(pe, i, 6, 10)
                elif lv in (1, 3):
                    pe_modulation(pe, i, 3 * step + lv // 2)
                for x in range(2):
                    pe.wait_ge(z_ready, n1 + (2 * lv + x - 1))
                    for h in range(2):
                        q = 2 * x + h
                        if lv < last:
                            nc.tensor.matmul(PS[:, 2 * x + 1, P * h:P * h + P], TB[:, 1, q, :], ZS[:, q, :],
                                             start=True, stop=True)
                        mm = nc.tensor.matmul(PS[:, 2 * x + 1, 256 + P * h:256 + P * h + P], ZS[:, q, :], TB[:, 1, q, :],
                                              start=True, stop=True)
                    mm.then_inc(t_done, 1)
                if step:
                    pe_scan(pe, i, step - 1, 3 if step == 2 else 2 * lv - 1)
            if step < 2:
                pe_modulation(pe, i, 3 * step + 2)
            for x in range(2):
                pe.wait_ge(x_ready, 2 * u + (x + 1))
                pe.wait_ge(t_ready, n0 + (2 * last + x + 1))
                for h in range(2):
                    mm = nc.tensor.matmul(PS[:, 4 + x, P * h:P * h + P], TB[:, 1, 2 * x + h, :], AXX[:, 2 * x + h, :, :],
                                          start=True, stop=True)
                mm.then_inc(aw_done, 1)
            for x in range(2):
                pe.wait_ge(aw_ready, 2 * u + (x + 1))
                for h in range(2):
                    q = 2 * x + h
                    rows = slice(64 * h, 64 * h + 64)
                    nc.tensor.matmul(PS[rows, 4 + x, 256:384], AW[:, x, 0, h, :], MM[:, 1, q, :], start=True, stop=True)
                    y0 = PS[rows, 4 + x, 384:512]
                    nc.tensor.matmul(y0, AW[:, x, 1, h, :], MM[:, 1, q, :], start=True, stop=False)
                    mm = nc.tensor.matmul(y0, TK[:, x, 2, 64 * h:64 * h + 64], MM[:, 3, q, :], start=False, stop=True)
                mm.then_inc(ry_done, 1)
            if step == 2:
                for n in range(4):
                    pe_modulation(pe, i, 7, 4 * n, 4 * n + 4)
                    pe_scan(pe, i, 1, 4 + n)
            for x in range(2):
                for c in range(4):
                    rows = slice(32 * c, 32 * c + 32)
                    at = 256 * x
                    nc.tensor.matmul(PS[:, c, at:at + P], AW[rows, x, 0, :, :], TK[rows, x, 0, :], start=True, stop=True)
                    nc.tensor.matmul(PS[:, c, at + P:at + 2 * P], TK[rows, x, 0, :], AW[rows, x, 1, :, :],
                                     start=True, stop=False)
                    mm = nc.tensor.matmul(PS[:, c, at + P:at + 2 * P], TK[rows, x, 1, :], TK[rows, x, 2, :],
                                          start=False, stop=True)
                if step == 2 and x == 0:
                    pe_turn(pe, i, 2)
            mm.then_inc(gk_done, 1)

        def pe_samples(pe, i, ahead2):
            u = 3 * i + 2
            if ahead2:
                pe.wait_ge(mod_read, 3 * i + 3)
                project(pe, i + 2, 0, (0,))
            pe.wait_ge(gk_ready, u + 1)
            pe.wait_ge(y0_ready, 2 * u + 2)
            pe.wait_ge(si_in, 32 * i + 32)
            for n in range(8):
                nc.tensor.matmul(PS[:, 4 + n // 4, P * (n % 4):P * (n % 4) + P], GS[:, n, :], SI[:, n, :],
                                 start=True, stop=True)
                mm = nc.tensor.matmul(PS[:, 7, CH_CHUNK * n:CH_CHUNK * n + CH_CHUNK], SI[:, n, :],
                                      R2[:, n // 4, 32 * (n % 4):32 * (n % 4) + 32], start=True, stop=True)
            mm.then_inc(yy_done, 1)

        def pe_post(pe, i, ahead2):
            pe.wait_ge(yt_ready, 3 * i + 3)
            for half in range(2):
                mm = nc.tensor.matmul(PS[:, 0 + half, 0:TH], BDM[:], YT[:, TH * half:TH * half + TH], start=True, stop=True)
            mm.then_inc(mean_done, 1)
            if ahead2:
                project(pe, i + 2, 0, (1,))
            pe.wait_ge(so_ready, i + 1)
            pe.wait_ge(ysq_ready, i + 1)
            for half in range(2):
                mm = nc.tensor.matmul(PS[:, 4 + half, 0:TH], BDM[:], SQ[:, TH * half:TH * half + TH], start=True, stop=True)
            mm.then_inc(var_done, 1)

        @block.tensor
        def _(pe):
            for which in range(3):
                project(pe, 0, which)
            project_low(pe, 0)
            pe.wait_ge(rows_in, 1)
            project(pe, 1, 0)

            def pair(i, ahead, ahead2):
                if ahead:
                    project(pe, i + 1, 1)
                pe.wait_ge(banks_idle, i + 1)
                head_sum(pe, sq_ready, i + 1, ss_done)
                if ahead:
                    project(pe, i + 1, 2)
                head_sum(pe, rk_ready, i + 1, bo_done)
                if ahead:
                    project_low(pe, i + 1)
                    pe.wait_ge(rows_in, i + 2)
                pe.wait_ge(prep_ready, i + 1)
                for step in range(3):
                    pe_step(pe, i, step)
                pe_samples(pe, i, ahead2)
                pe_post(pe, i, ahead2)

            with pe.Fori(0, NPAIR - 2) as i:
                pair(i, True, True)
            pair(NPAIR - 2, True, False)
            pair(NPAIR - 1, False, False)

        def act_step(act, i, step):
            u = 3 * i + step
            A = nc.scalar.activation
            for x in range(2):
                act.wait_ge(tr_done, 2 * u + (x + 1))
                A(AXX[:, 2 * x:2 * x + 2, 0, :], PS[:, 4 + x, 0:P].rearrange("p (h c) -> p h c", h=2), ACT.Copy)
                A(TK[:, x].rearrange("p k c -> p (k c)"), PS[:, 4 + x, P:4 * P], ACT.Copy)
                act.drain().then_inc(tr_ready, 1)
            for x in range(2):
                act.wait_ge(x_done, 2 * u + (x + 1))
                A(AXX[:, 2 * x:2 * x + 2, 1, :], PS[:, 4 + x, 0:P].rearrange("p (h c) -> p h c", h=2),
                  ACT.Copy).then_inc(x_ready, 1)
            for lv in range(1, LEVELS[step]):
                for x in range(2):
                    act.wait_ge(z_done, per_level(i, step, 0) + (2 * lv + x + 1))
                    A(ZS[:, 2 * x:2 * x + 2], PS[:, 2 * x, 0:256].rearrange("p (h c) -> p h c", h=2),
                      ACT.Copy).then_inc(z_ready, 1)
            for x in range(2):
                act.wait_ge(aw_done, 2 * u + (x + 1))
                A(AW[:, x].rearrange("p k h c -> p h k c"),
                  PS[:, 4 + x, 0:256].rearrange("p (h k c) -> p h k c", h=2, k=2), ACT.Copy).then_inc(aw_ready, 1)
            act.wait_ge(ada_used, ADA_PAIR * i + (3 * step + MODS[step]))
            A(MR[:, 0:P * MODS[step]], PS[0:9, 6, 0:P * MODS[step]], ACT.Copy).then_inc(mr_ready, 1)
            if step:
                act.wait_ge(yt_ready, u)
            for x in range(2):
                act.wait_ge(r2_ready, 2 * u + (x + 1))
                A(Y0[:, x], PS[:, 4 + x, 384:512], ACT.Copy).then_inc(y0_ready, 1)

        @block.scalar
        def _(act):
            A = nc.scalar.activation
            act.wait_ge(cleared, 1)
            evacuate(act, 0)

            def pair(i, ahead):
                act.wait_ge(act_rows, i + 1)
                A(SQ[:, 1:W1], KX[:, 1:W1], ACT.Square, scale=PARAM[:, bass.ds(i + PAR["k_k"], 1)]).then_inc(sq_ready, 1)
                act.wait_ge(ss_ready, i + 1)
                A(NR[:, 1:W1], NR[:, 1:W1], ACT.Sqrt).then_inc(nr_ready, 1)
                act.wait_ge(g2_free, i + 1)
                A(G2[:, 1:W1], GN[:, 1:W1], ACT.Copy)
                if ahead:
                    act.wait_ge(rows_used, i + 1)
                    evacuate(act, i + 1)
                for step in range(3):
                    act_step(act, i, step)
                act.wait_ge(yc_ready, i + 1)
                A(SQ[:, 0:T], YC[:], ACT.Square).then_inc(ysq_ready, 1)
                act.wait_ge(var_done, i + 1)
                A(NR[:, 0:T].rearrange("p (h n) -> p h n", h=2), PS[:, 4:6, 0:TH], ACT.Sqrt,
                  bias=EPSG[:, 0:1]).then_inc(sd_ready, 1)

            with act.Fori(0, NPAIR - 1) as i:
                pair(i, True)
            pair(NPAIR - 1, False)

        @block.gpsimd
        def _(pool):
            G = nc.gpsimd
            pool.wait_ge(cleared, 1)

            def load_states(i):
                for h in range(2):
                    rows = slice(64 * h, 64 * h + 64)
                    pool.dma_start(SI[rows, :, rows], io["wkv0"][i][rows]).then_inc(si_in, 16)

            load_states(0)

            def pair(i, ahead):
                for step in range(3):
                    u = 3 * i + step
                    pool.wait_ge(prep_ready, i + 1)
                    ident = bcast(IDENT[:], 1, 4)
                    pool.wait_ge(gk_free, u + 1)
                    for x in range(2):
                        if step < 2:
                            lo = 1 + 2 * P * step + P * x + CH_CHUNK - 1
                            pc = PI[:, lo:lo + 3 * CH_CHUNK + 1:CH_CHUNK]
                        else:
                            lo = PC0 + 4 * (NS + 1) * x + NS
                            pc = PI[:, lo:lo + 3 * (NS + 1) + 1:NS + 1]
                        G.tensor_tensor(DG[:, 4 * x:4 * x + 4, :], ident, bcast(pc, 2, P), ALU.mult)
                    pool.drain().then_inc(dg_ready, 1)
                    pool.wait_ge(mm_ready, 4 * u + 4)
                    for lv in range(LEVELS[step]):
                        for x in range(2):
                            if lv >= 2:
                                pool.wait_ge(t_ready, per_level(i, step, 0) + (2 * lv + x - 3))
                            G.tensor_tensor(LT[:, lv % 2, 2 * x:2 * x + 2], MM[:, 0, 2 * x:2 * x + 2, :],
                                            bcast(LM[:, lv, :], 1, 2), ALU.mult)
                            pool.drain().then_inc(lt_ready, 1)
                    if step == 2:
                        pool.wait_ge(sp_ready, i + 1)
                        for h in range(2):
                            rows = slice(64 * h, 64 * h + 64)
                            pool.dma_start(io["wkv_p"][i][rows], SB[rows, 8, rows]).then_inc(sp_out, 16)
                        pool.wait_ge(sp_out, 32 * i + 32)
                        pool.sem_inc(sp_free, 1)
                pool.wait_ge(so_ready, i + 1)
                for h in range(2):
                    rows = slice(64 * h, 64 * h + 64)
                    pool.dma_start(io["wkv_s"][i][rows], SO[rows, :, rows]).then_inc(so_out, 16)
                if ahead:
                    load_states(i + 1)
                pool.wait_ge(so_out, 32 * i + 32)
                pool.sem_inc(so_free, 1)
                pool.wait_ge(post_done, i + 1)
                pool.dma_start(io["mix"][i], YT[:]).then_inc(y_out, 16)
                pool.wait_ge(y_out, 16 * i + 16)
                pool.sem_inc(mix_free, 1)

            with pool.Fori(0, NPAIR - 1) as i:
                pair(i, True)
            pair(NPAIR - 1, False)

        def prep(dve, i):
            V = nc.vector
            body = slice(1, W1)
            dve.wait_ge(rows_in, i + 1)
            for which, (kt, dst) in enumerate(((0, RR[:, body]), (8, KX[:, body]), (16, CHN[:, KV_, body]))):
                V.tensor_tensor(DT[:, body], PP[:, which, 0:W1 - 1], PP[:, which, 1:W1], ALU.subtract)
                dve.drain()
                V.scalar_tensor_tensor(dst, DT[:, body], PARAM[:, bass.ds(i + (PAR["mu"] + kt), 1)], PP[:, which, 1:W1],
                                       ALU.mult, ALU.add)
                dve.drain()
                if which == 1:
                    dve.sem_inc(act_rows, 1)
            V.tensor_tensor_scan(PX[:, body], WD[:, 0:W1 - 1], SM[:, body], 1.0, ALU.mult, ALU.max)
            V.tensor_scalar(DT[:, body], AG[:, body], PARAM[:, bass.ds(i + PAR["k_a"], 1)], OMK[:, bass.ds(i, 1)],
                            ALU.mult, ALU.add)
            dve.drain()
            V.tensor_tensor(PI[:, body], PX[:, body], WD[:, body], ALU.mult)
            V.tensor_tensor(DT[:, body], DT[:, body], KX[:, body], ALU.mult)
            dve.wait_ge(ss_done, i + 1)
            V.tensor_scalar(halves(NR[:, body]), PS[:, 0:2, 0:TPH], 1e-24, None, ALU.max)
            dve.drain().then_inc(ss_ready, 1)
            V.scalar_tensor_tensor(SQ[:, body], RR[:, body], PARAM[:, bass.ds(i + PAR["r_k"], 1)], DT[:, body],
                                   ALU.mult, ALU.mult)
            dve.drain().then_inc(rk_ready, 1)
            V.reciprocal(RPI[:, body], PI[:, body])
            V.tensor_tensor(CHN[:, KR_, body], RR[:, body], PI[:, body], ALU.mult)
            dve.drain()
            V.tensor_tensor(CHN[:, KK_, body], DT[:, body], RPI[:, body], ALU.mult)
            dve.wait_ge(nr_ready, i + 1)
            V.reciprocal(NR[:, body], NR[:, body])
            dve.drain()
            V.scalar_tensor_tensor(NR[:, body], KX[:, body], PARAM[:, bass.ds(i + PAR["k_k"], 1)], NR[:, body],
                                   ALU.mult, ALU.mult)
            dve.drain()
            V.scalar_tensor_tensor(CHN[:, KA_, body], NR[:, body], -1.0, PX[:, body], ALU.mult, ALU.mult)
            V.tensor_tensor(DT[:, body], NR[:, body], AG[:, body], ALU.mult)
            dve.drain()
            V.tensor_tensor(CHN[:, KB_, body], DT[:, body], RPI[:, body], ALU.mult)
            dve.drain()
            V.tensor_tensor(CHN[:, KBH:KKH + 1, 1:1 + SEQ].rearrange("p k (c s) -> p k c s", s=CH_CHUNK),
                            CHN[:, KB_:KK_ + 1, 1:1 + SEQ].rearrange("p k (c s) -> p k c s", s=CH_CHUNK),
                            bcast(bcast(PI[:, CH_CHUNK:1 + SEQ:CH_CHUNK], 2, CH_CHUNK), 1, 2), ALU.mult)
            s5 = lambda lo, hi: CHN[:, lo:hi, PC0:PC1].rearrange("p k (b s) -> p k b s", s=NS + 1)[:, :, :, 1:]
            s32 = lambda lo, hi: SLT[:, lo:hi, :].rearrange("p k (b s) -> p k b s", s=CH_CHUNK)[:, :, :, 0:NS]
            V.tensor_copy(s32(KA_, KK_ + 1), s5(KA_, KK_ + 1))
            V.tensor_copy(s32(KV_, KV_ + 1), s5(KV_, KV_ + 1))
            V.tensor_tensor(s32(KBH, KKH + 1), s5(KB_, KK_ + 1),
                            bcast(bcast(PI[:, PC0 + NS:PC1:NS + 1], 2, NS), 1, 2), ALU.mult)
            dve.wait_ge(bo_done, i + 1)
            V.tensor_tensor(BO[:, 0:TPH], CHN[:, KV_, 1:1 + TPH], PS[:, 0, 0:TPH], ALU.mult)
            V.tensor_tensor(BO[:, TPH:SEQ], CHN[:, KV_, 1 + TPH:1 + SEQ], PS[:, 1, 0:PB], ALU.mult)
            V.tensor_tensor(samples4(BO[:, SEQ:T]), samples5(CHN[:, KV_, PC0:PC1]), samples5(PS[:, 1, PB:TPH]),
                            ALU.mult)
            dve.drain().then_inc(rows_used, 1)
            dve.sem_inc(prep_ready, 1)

        def dve_step(dve, i, step):
            V = nc.vector
            u = 3 * i + step
            y0 = Y0[:].rearrange("p x t -> p (x t)")
            for q in range(4):
                dve.wait_ge(mm_prod, 4 * u + (q + 1))
                V.tensor_tensor(MM[:, :, q, :], PS[:, q, :].rearrange("p (k t) -> p k t", k=4), MASK[:],
                                ALU.mult).then_inc(mm_ready, 1)
            if step:
                dve_modulation(dve, i, step - 1)
                if step == 1:
                    dve.wait_ge(sp_free, i + 1)
                    V.memset(SB[:, 0, :], 0.0).then_inc(s_ready, 1)
                else:
                    V.tensor_copy(SB[:, 0, :], SB[:, 8, :])
                    dve.drain().then_inc(s_ready, 1)
            n0, n1 = per_level(i, step, 0), per_level(i, step, 1)
            last = LEVELS[step] - 1
            for lv in range(last + 1):
                if lv and step:
                    for n in (0, 1, 2) if step == 2 else (2 * lv - 2,):
                        dve_scan(dve, i, step - 1, n)
                for x in range(2):
                    tb, tbk = TB[:, :, 2 * x:2 * x + 2, :], slice(2 * x, 2 * x + 2)
                    if lv == 0:
                        dve.wait_ge(lt_ready, n0 + (x + 1))
                        V.tensor_tensor(TB[:, 1, tbk], LT[:, 0, tbk], bcast(IDENT[:], 1, 2), ALU.add)
                        dve.wait_ge(z_done, n0 + (x + 1))
                        V.tensor_tensor(TB[:, 0, tbk], PS[:, 2 * x, 0:256].rearrange("p (h t) -> p h t", h=2),
                                        bcast(IDENT[:], 1, 2), ALU.add)
                        dve.drain().then_inc(t_ready, 1)
                        continue
                    dve.wait_ge(t_done, n1 + (2 * lv + x - 1))
                    if lv < last:
                        V.tensor_tensor(tb, tb, PS[:, 2 * x + 1, :].rearrange("p (k h t) -> p k h t", k=2, h=2), ALU.add)
                    else:
                        V.tensor_tensor(TB[:, 1, tbk], TB[:, 1, tbk],
                                        PS[:, 2 * x + 1, 256:512].rearrange("p (h t) -> p h t", h=2), ALU.add)
                    dve.drain().then_inc(t_ready, 1)
                if lv and step:
                    dve_scan(dve, i, step - 1, 3 if step == 2 else 2 * lv - 1)
            if step == 2:
                for n in range(4, 8):
                    dve_scan(dve, i, 1, n)
            if step:
                if step == 2:
                    dve.drain().then_inc(sp_ready, 1)
                if step == 1:
                    dve.wait_ge(mix_free, i + 1)
                V.tensor_tensor(YT[:, 256 * step - 256:256 * step], y0, PS[:, 7, 0:256], ALU.add)
                dve.drain().then_inc(yt_ready, 1)
            for x in range(2):
                dve.wait_ge(ry_done, 2 * u + (x + 1))
                V.tensor_tensor(R2[:, x, :], chan_view(KR_, x, step), PS[:, 4 + x, 256:384], ALU.add)
                dve.drain().then_inc(r2_ready, 1)
            if step == 2:
                dve_modulation(dve, i, 2)
            dve.wait_ge(gk_done, u + 1)
            bd = bcast(bcast(BD[:], 1, 4), 1, 2)
            by_chunk = lambda ap: ap.rearrange("p (x c) t -> p x c t", x=2)
            prod = PS[:, 0:4, :].rearrange("p c (x k t) -> p k x c t", x=2, k=2)
            V.tensor_tensor(by_chunk(GS[:]), prod[:, 0], bd, ALU.mult)
            V.tensor_tensor(by_chunk(K0[:]), prod[:, 1], bd, ALU.mult)
            dve.drain().then_inc(gk_read, 1)
            dve.wait_ge(dg_ready, u + 1)
            V.tensor_tensor(GS[:], GS[:], DG[:], ALU.add)
            dve.drain().then_inc(gk_ready, 1)
            dve.sem_inc(gk_free, 1)

        def dve_scan(dve, i, step, n):
            dve.wait_ge(s_done, 16 * i + 8 * step + (n + 1))
            nc.vector.tensor_tensor(SB[:, n + 1, :], K0[:, n, :], PS[:, 7, 256 + P * (n % 2):256 + P * (n % 2) + P],
                                    ALU.add).then_inc(s_ready, 1)

        def dve_modulation(dve, i, step):
            dve.wait_ge(turned, 3 * i + step + 1)
            n = MODS[step]
            at = bass.ds(ADA_PAIR * i + (ADA_H + 3 * step), n)
            nc.vector.tensor_tensor(MOD[:, at, :], PS[:, 6, 3 * P:3 * P + 9 * n].rearrange("p (c b) -> p c b", b=9),
                                    bcast(BADA[:, at], 2, 9), ALU.add).then_inc(mod_read, 1)

        def dve_samples(dve, i):
            V = nc.vector
            u = 3 * i + 2
            dve.wait_ge(yy_done, i + 1)
            dve.wait_ge(y0_ready, 2 * u + 2)
            sl = lambda ap: ap.rearrange("p (b s) -> p b s", s=CH_CHUNK)[:, :, 0:NS]
            V.tensor_tensor(samples4(YT[:, SEQ:T]), sl(Y0[:].rearrange("p x t -> p (x t)")), sl(PS[:, 7, 0:256]), ALU.add)
            dve.drain().then_inc(yt_ready, 1)
            dve.wait_ge(so_free, i + 1)
            V.tensor_tensor(SO[:].rearrange("p (x c) t -> p x c t", x=2), K0[:].rearrange("p (x c) t -> p x c t", x=2),
                            PS[:, 4:6, :].rearrange("p x (c t) -> p x c t", c=4), ALU.add)
            dve.drain().then_inc(so_ready, 1)

        def post(dve, i):
            V = nc.vector
            dve.wait_ge(mean_done, i + 1)
            V.tensor_tensor(halves(YC[:]), halves(YT[:]), PS[:, 0:2, 0:TH], ALU.subtract)
            dve.drain().then_inc(yc_ready, 1)
            dve.wait_ge(sd_ready, i + 1)
            V.reciprocal(NR[:, 0:T], NR[:, 0:T])
            dve.sem_inc(banks_idle, 1)
            dve.drain()
            V.tensor_tensor(YC[:], YC[:], NR[:, 0:T], ALU.mult)
            dve.drain()
            V.tensor_scalar(YC[:], YC[:], PARAM[:, bass.ds(i + PAR["lnx_w"], 1)], PARAM[:, bass.ds(i + PAR["lnx_b"], 1)],
                            ALU.mult, ALU.add)
            dve.drain()
            V.tensor_tensor(YC[:], YC[:], BO[:], ALU.add)
            dve.drain()
            V.tensor_tensor(YT[:, 0:SEQ], YC[:, 0:SEQ], G2[:, 1:1 + SEQ], ALU.mult)
            V.tensor_tensor(samples4(YT[:, SEQ:T]), samples4(YC[:, SEQ:T]), samples5(G2[:, PC0:PC1]), ALU.mult)
            dve.drain().then_inc(post_done, 1)
            dve.sem_inc(g2_free, 1)

        @block.vector
        def _(dve):
            V = nc.vector
            for buf in (PP, WD, SLT, SI, SB, CHN, NR):
                V.memset(buf[:], 0.0)
            V.tensor_scalar(OMK[:], PARAM[:, PAR["k_a"]:PAR["k_a"] + 8], -1.0, 1.0, ALU.mult, ALU.add)
            V.tensor_scalar(BDM[:], BD[:], 1.0 / 64, None, ALU.mult)
            dve.drain().then_inc(cleared, 1)
            dve.sem_inc(mix_free, 1)
            dve.sem_inc(so_free, 1)
            dve.sem_inc(sp_free, 1)
            dve.sem_inc(gk_free, 1)
            dve.sem_inc(g2_free, 1)
            dve.sem_inc(banks_idle, 1)
            with dve.Fori(0, NPAIR) as i:
                prep(dve, i)
                for step in range(3):
                    dve_step(dve, i, step)
                dve_samples(dve, i)
                post(dve, i)
            for lo, hi in ((2, 3), (4, 6)):
                V.tensor_scalar(MOD[:, KT * lo:KT * hi, :], MOD[:, KT * lo:KT * hi, :], 1.0, None, ALU.add)


class Norm:

    def __init__(self, nc, m, g, X, wname, bname):
        self.nc, self.g, self.X, self.wname, self.bname = nc, g, X, wname, bname
        self.SQ = m.sb("nSQ", [P, 2, T])
        self.MN = m.sb("nMN", [P, 2, T])
        self.ONES = m.sb("nONES", [P, P])
        (self.ones_ready, self.mean_done, self.xc_ready, self.sq_ready, self.sq_used, self.sd_ready, self.scaled,
         self.normed) = (m.sem("n_" + x) for x in (
            "ones_ready mean_done xc_ready sq_ready sq_used sd_ready scaled normed").split())

    def start(self, dve):
        self.nc.vector.memset(self.ONES[:], 1.0 / D)
        dve.drain().then_inc(self.ones_ready, 1)

    def mean(self, pe, x_ready, kt, first, last):
        pe.wait_ge(x_ready, kt + 1)
        for half in range(2):
            mm = self.nc.tensor.matmul(self.g["PS"][:, 4 + half, 0:TH], self.ONES[:],
                                       self.X[:, bass.ds(kt, 1), TH * half:TH * half + TH].rearrange("p k t -> p (k t)"),
                                       start=first, stop=last)
        if last:
            mm.then_inc(self.mean_done, 1)

    def variance(self, pe):
        for kt in range(KT):
            pe.wait_ge(self.sq_ready, kt + 1)
            for half in range(2):
                mm = self.nc.tensor.matmul(self.g["PS"][:, 6 + half, 0:TH], self.ONES[:],
                                           self.SQ[:, kt % 2, TH * half:TH * half + TH],
                                           start=(kt == 0), stop=(kt == KT - 1))
            mm.then_inc(self.sq_used, 1)

    def scalar(self, act):
        A = self.nc.scalar.activation
        for kt in range(KT):
            act.wait_ge(self.xc_ready, kt + 1)
            if kt >= 2:
                act.wait_ge(self.sq_used, kt - 1)
            A(self.SQ[:, kt % 2, :], self.X[:, kt, :], ACT.Square).then_inc(self.sq_ready, 1)
        act.wait_ge(self.sq_used, KT)
        A(self.MN[:, 1].rearrange("p (h n) -> p h n", h=2), self.g["PS"][:, 6:8, 0:TH], ACT.Sqrt,
          bias=self.g["EPSG"][:, 1:2]).then_inc(self.sd_ready, 1)
        for kt in range(KT):
            at = PAR[self.bname] + kt
            act.wait_ge(self.scaled, kt + 1)
            A(self.X[:, kt, :], self.X[:, kt, :], ACT.Identity, bias=self.g["PARAM"][:, at:at + 1]).then_inc(self.normed, 1)

    def vector(self, dve):
        V, PARAM = self.nc.vector, self.g["PARAM"]
        dve.wait_ge(self.mean_done, 1)
        V.tensor_copy(self.MN[:, 0].rearrange("p (h n) -> p h n", h=2), self.g["PS"][:, 4:6, 0:TH])
        dve.drain()
        for kt in range(KT):
            V.tensor_tensor(self.X[:, kt, :], self.X[:, kt, :], self.MN[:, 0], ALU.subtract).then_inc(self.xc_ready, 1)
        dve.wait_ge(self.sd_ready, 1)
        V.reciprocal(self.MN[:, 1], self.MN[:, 1])
        dve.drain()
        for kt in range(KT):
            at = PAR[self.wname] + kt
            V.scalar_tensor_tensor(self.X[:, kt, :], self.X[:, kt, :], PARAM[:, at:at + 1], self.MN[:, 1],
                                   ALU.mult, ALU.mult).then_inc(self.scaled, 1)


def phase_out(nc, io, g, stack):
    m = Mem(nc, stack, "out")
    PS, MOD, XT = g["PS"], g["MOD"], g["XT"]
    WR, WH, WL = g["WR"], g["WH"], g["WL"]
    MH, ML = g["HH"], g["HL"]
    MIX = m.sb("MIX", [P, 2, 4, T])
    TMP = m.sb("TMP", [P, 4, T])
    norm = Norm(nc, m, g, XT, "ln1_w", "ln1_b")
    w_in, mix_in = g["W_IN"], m.sems("mix_in", 4)
    x_in, tile_done, x_ready, bank_free, mh_ready, ml_ready, hi_ready, lo_ready, h2_ready, h2_high, h2_low = (
        m.sem(x) for x in "x_in tile_done x_ready bank_free mh_ready ml_ready hi_ready lo_ready h2_ready h2_high h2_low".split())

    with nc.Block() as block:
        @block.sync
        def _(sp):
            mix = io["mix"].rearrange("k p t -> p k t")

            def quarter(q):
                if q >= 2:
                    sp.wait_ge(ml_ready, q - 1)
                sp.dma_start(MIX[:, q % 2], mix[:, 4 * q:4 * q + 4, :]).then_inc(mix_in[q], 16)

            sp.dma_start(WR[:, 0, :], io["w_out"][0]).then_inc(w_in[0], 16)
            for q in range(4):
                quarter(q)
            sp.dma_start(WR[:, 1, :], io["w_out"][1]).then_inc(w_in[1], 16)
            sp.dma_start(XT[:], io["xT"]).then_inc(x_in, 16)
            with sp.Fori(0, 7) as i:
                for k in range(2):
                    sp.wait_ge(lo_ready, 2 * i + k + 1)
                    sp.dma_start(WR[:, k, :], io["w_out"][2 * i + (k + 2)]).then_inc(w_in[k], 16)
            for k in range(2):
                sp.wait_ge(lo_ready, KT - 1 + k)
                sp.dma_start(WR[:, k, :], io["w_q"][k]).then_inc(w_in[k], 16)

        @block.tensor
        def _(pe):
            def tile(i, k, first=False):
                pe.wait_ge(bank_free, 4 * i + k + 1)
                pe.wait_ge(lo_ready, 4 * i + k + 1)
                for half in range(2):
                    cols = slice(TH * half, TH * half + TH)
                    for kt in range(KT):
                        at = slice(P * kt, P * kt + P)
                        if first and half == 0 and kt % 4 == 0:
                            pe.wait_ge(ml_ready, kt // 4 + 1)
                        mm = product(nc, PS[:, 2 * (k % 2) + half, 0:TH], WH[:, k % 2, at], WL[:, k % 2, at],
                                     MH[:, kt, cols], ML[:, kt, cols], kt == 0, kt == KT - 1)
                mm.then_inc(tile_done, 1)

            pe.wait_ge(norm.ones_ready, 1)
            tile(0, 0, first=True)
            for k in range(1, 4):
                tile(0, k)
                norm.mean(pe, x_ready, k - 1, first=(k == 1), last=False)
            with pe.Fori(1, 4) as i:
                for k in range(4):
                    tile(i, k)
                    norm.mean(pe, x_ready, 4 * i + (k - 1), first=False, last=False)
            norm.mean(pe, x_ready, KT - 1, first=False, last=True)
            norm.variance(pe)

        @block.scalar
        def _(act):
            A = nc.scalar.activation

            def high(k):
                A(r32(WH[:, k % 2]), WR[:, k % 2], ACT.Copy).then_inc(hi_ready, 1)

            act.wait_ge(w_in[0], 16)
            high(0)
            for q in range(4):
                act.wait_ge(mix_in[q], 16)
                A(r32(MH[:, 4 * q:4 * q + 4]), MIX[:, q % 2], ACT.Copy).then_inc(mh_ready, 1)
            act.wait_ge(w_in[1], 16)
            high(1)
            with act.Fori(0, 7) as i:
                for k in range(2):
                    act.wait_ge(w_in[k], 16 * i + 32)
                    act.wait_ge(tile_done, 2 * i + k + 1)
                    high(k)
            norm.scalar(act)
            for kt in range(KT):
                act.wait_ge(h2_ready, kt + 1)
                A(r32(MH[:, kt]), TMP[:, kt % 4], ACT.Copy).then_inc(h2_high, 1)

        @block.gpsimd
        def _(pool):
            for kt in range(KT):
                pool.wait_ge(h2_high, kt + 1)
                nc.gpsimd.tensor_tensor(r32(ML[:, kt]), TMP[:, kt % 4], MH[:, kt], ALU.subtract).then_inc(h2_low, 1)

        @block.vector
        def _(dve):
            V = nc.vector
            dve.sem_inc(bank_free, 2)
            norm.start(dve)

            def low(i, k):
                dve.wait_ge(hi_ready, 4 * i + k + 1)
                V.tensor_tensor(r32(WL[:, k % 2]), WR[:, k % 2], WH[:, k % 2], ALU.subtract).then_inc(lo_ready, 1)

            low(0, 0)
            for q in range(4):
                dve.wait_ge(mh_ready, q + 1)
                V.tensor_tensor(r32(ML[:, 4 * q:4 * q + 4]), MIX[:, q % 2], MH[:, 4 * q:4 * q + 4],
                                ALU.subtract).then_inc(ml_ready, 1)
            low(0, 1)
            dve.wait_ge(x_in, 16)

            def group(i, last):
                for k in range(4):
                    ct = 4 * i + k
                    tmp = TMP[:, k % 2]
                    ps = PS[:, 2 * (k % 2):2 * (k % 2) + 2, 0:TH]
                    dve.wait_ge(tile_done, 4 * i + k + 1)
                    V.tensor_scalar(tmp[:, 0:TH], ps[:, 0], MOD[:, bass.ds(ct + 2 * KT, 1), 0:1].rearrange("p c b -> p (c b)"),
                                    None, ALU.mult)
                    V.tensor_scalar(tmp[:, TH:SEQ], ps[:, 1, 0:SEQ - TH],
                                    MOD[:, bass.ds(ct + 2 * KT, 1), 0:1].rearrange("p c b -> p (c b)"), None, ALU.mult)
                    V.tensor_tensor(samples4(tmp[:, SEQ:T]), samples4(ps[:, 1, SEQ - TH:TH]),
                                    bcast(MOD[:, bass.ds(ct + 2 * KT, 1), 1:9].rearrange("p c b -> p (c b)"), 2, NS), ALU.mult)
                    dve.drain().then_inc(bank_free, 1)
                    x = XT[:, bass.ds(ct, 1), :].rearrange("p c t -> p (c t)")
                    V.scalar_tensor_tensor(x, x, ALPHA, tmp, ALU.mult, ALU.add).then_inc(x_ready, 1)
                    if not (last and k >= 2):
                        low(i, k + 2)

            with dve.Fori(0, 3) as i:
                group(i, False)
            group(3, True)
            dve.drain()
            norm.vector(dve)
            for kt in range(KT):
                tmp = TMP[:, kt % 4]
                if kt >= 4:
                    dve.wait_ge(h2_low, kt - 3)
                scale, shift = MOD[:, 4 * KT + kt], MOD[:, 3 * KT + kt]
                dve.wait_ge(norm.normed, kt + 1)
                V.tensor_scalar(tmp[:, 0:SEQ], XT[:, kt, 0:SEQ], scale[:, 0:1], shift[:, 0:1], ALU.mult, ALU.add)
                V.tensor_tensor(samples4(tmp[:, SEQ:T]), samples4(XT[:, kt, SEQ:T]), bcast(scale[:, 1:9], 2, NS), ALU.mult)
                dve.drain()
                V.tensor_tensor(samples4(tmp[:, SEQ:T]), samples4(tmp[:, SEQ:T]), bcast(shift[:, 1:9], 2, NS), ALU.add)
                dve.drain().then_inc(h2_ready, 1)


NT = 5


def phase_route(nc, io, g, stack):
    m = Mem(nc, stack, "rt")
    RT = m.sb("RT", [P, 3, NT * P])
    g["RT"] = RT
    run(route_scores, nc, io, g)
    run(gate_tables, nc, io, g)


def route_scores(nc, io, g, stack):
    m = Mem(nc, stack, "sc")
    PS, IDENT, RT = g["PS"], g["IDENT"], g["RT"]
    WR, WH, WL, HH, HL = (g[x] for x in ("WR", "WH", "WL", "HH", "HL"))
    KEYS = m.sb("KEYS", [P, 2, NK])
    QT = m.sb("QT", [P, 2, NT * P])
    SC = m.sb("SC", [P, 2, 2, NT, NK])
    VV = m.sb("VV", [P, 2, NT, TOPK])
    II = m.sb("II", [P, 2, NT, TOPK], U32)
    IF = m.sb("IF", [P, 2, NT, TOPK])
    CA = m.sb("CA", [P, NT, TOPK, TOPK])
    EQ = m.sb("EQ", [P, 2, NT, TOPK, TOPK])
    IH = m.sb("IH", [P, 2, NT, TOPK])
    SV = m.sb("SV", [P, NT, HEADS, TOPK])
    SH = m.sb("SH", [P, NT, TOPK])
    SI = m.sb("SI", [P, NT, TOPK], U32)
    PL = m.sb("PL", [P, 2, NT, TOPK], U32)
    HF = m.sb("HF", [P, 2, NT, TOPK])
    EG = m.sb("EG", [P, NT, 3, P])
    SM1 = m.sb("SM1", [P, NT, HEADS])
    IO16 = m.sb("IO16", [P, TOPK])
    w_in, w_base = g["W_IN"], 8 * KT
    (keys_in, tile_done, bank_free, q_ready, sc_done, sc_free, sc_ready, iota_ready,
     ex_in, ex_ready, eg_ready, rt_ready, cleared, begun, x_out,
     hi_ready, lo_ready, eq_ready, looked_up) = (m.sem(x) for x in (
        "keys_in tile_done bank_free q_ready sc_done sc_free sc_ready iota_ready "
        "ex_in ex_ready eg_ready rt_ready cleared begun x_out hi_ready lo_ready eq_ready looked_up").split())

    with nc.Block() as block:
        @block.sync
        def _(sp):
            sp.dma_start(KEYS[:], io["keys"]).then_inc(keys_in, 16)
            sp.dma_start(io["x1"], g["XT"][:]).then_inc(x_out, 16)
            with sp.Fori(0, 7) as i:
                for k in range(2):
                    sp.wait_ge(lo_ready, 2 * i + k + 1)
                    sp.dma_start(WR[:, k, :], io["w_q"][2 * i + (k + 2)]).then_inc(w_in[k], 16)
            for k in range(2):
                sp.wait_ge(lo_ready, KT - 1 + k)
                sp.dma_start(WR[:, k, :], io["peer_u"][k]).then_inc(w_in[k], 16)
            sp.wait_ge(x_out, 16)

        @block.tensor
        def _(pe):
            def query(i, k):
                pe.wait_ge(bank_free, 4 * i + (k + 1))
                pe.wait_ge(lo_ready, 4 * i + (k + 1))
                for half in range(2):
                    cols = slice(TH * half, TH * half + TH)
                    for kt in range(KT):
                        at = slice(P * kt, P * kt + P)
                        mm = product(nc, PS[:, 2 * (k % 2) + half, 0:TH], WH[:, k % 2, at], WL[:, k % 2, at],
                                     HH[:, kt, cols], HL[:, kt, cols], kt == 0, kt == KT - 1)
                mm.then_inc(tile_done, 1)

            def scores(i, k):
                n = 4 * i + k
                pe.wait_ge(q_ready, n + 1)
                pe.wait_ge(sc_ready, n + 1)
                for t in range(NT):
                    mm = nc.tensor.matmul(PS[:, 4 + 2 * (k % 2) + t // 4, P * (t % 4):P * (t % 4) + P],
                                          QT[:, k % 2, P * t:P * t + P], KEYS[:, k % 2, :], start=True, stop=True)
                mm.then_inc(sc_done, 1)

            pe.wait_ge(keys_in, 16)
            query(0, 0)
            with pe.Fori(0, 3) as i:
                for k in range(4):
                    query(i, k + 1)
                    scores(i, k)
            for k in range(3):
                query(3, k + 1)
                scores(3, k)
            scores(3, 3)
            for t in range(NT):
                pe.wait_ge(eg_ready, 1)
                for j in range(3):
                    mm = nc.tensor.transpose(PS[:, t, P * j:P * j + P], EG[:, t, j, :], IDENT[:])
                mm.then_inc(rt_ready, 1)

        @block.scalar
        def _(act):
            A = nc.scalar.activation
            act.sem_inc(bank_free, 2)
            act.sem_inc(sc_ready, 1)
            act.wait_ge(cleared, 1)

            def query(k):
                A(QT[:, k % 2, 0:T].rearrange("p (h n) -> p h n", h=2), PS[:, 2 * (k % 2):2 * (k % 2) + 2, 0:TH],
                  ACT.Copy).then_inc(q_ready, 1)
                act.drain().then_inc(bank_free, 1)

            def scores(i, k):
                n = 4 * i + k
                head, half = k // 2, k % 2
                act.wait_ge(sc_done, n + 1)
                if half == 0:
                    act.wait_ge(sc_free, 2 * i + head + 1)
                A(SC[:, head % 2, half, 0:4, :].rearrange("p t k -> p (t k)"), PS[:, 4 + 2 * half, :], ACT.Copy)
                A(SC[:, head % 2, half, 4, :], PS[:, 5 + 2 * half, 0:P], ACT.Copy)
                act.drain().then_inc(sc_ready, 1)

            def high(k):
                A(r32(WH[:, k % 2]), WR[:, k % 2], ACT.Copy).then_inc(hi_ready, 1)

            for k in range(2):
                act.wait_ge(w_in[k], w_base + 16)
                high(k)
            act.wait_ge(tile_done, 1)
            query(0)
            with act.Fori(0, 3) as i:
                for k in range(4):
                    act.wait_ge(w_in[k % 2], 32 * i + (w_base + 16 * (k // 2) + 32))
                    high(k)
                    act.wait_ge(tile_done, 4 * i + (k + 2))
                    query(k + 1)
                    scores(i, k)
            for k in range(3):
                if k < 2:
                    act.wait_ge(w_in[k], w_base + 8 * KT)
                    high(k)
                act.wait_ge(tile_done, 12 + k + 2)
                query(k + 1)
                scores(3, k)
            scores(3, 3)
            act.wait_ge(ex_in, 1)
            A(SV[:], SV[:], ACT.Exp).then_inc(ex_ready, 1)
            for t in range(NT):
                act.wait_ge(rt_ready, t + 1)
                A(RT[:, :, P * t:P * t + P], PS[:, t, 0:3 * P].rearrange("p (j t) -> p j t", j=3), ACT.Copy)

        @block.gpsimd
        def _(pool):
            nc.gpsimd.iota(IO16[:], [[1, TOPK]], base=0, channel_multiplier=0,
                           allow_small_or_imprecise_dtypes=True).then_inc(iota_ready, 1)

            def low(i):
                for k in range(2):
                    pool.wait_ge(hi_ready, 2 * i + k + 1)
                    nc.gpsimd.tensor_tensor(r32(WL[:, k]), WR[:, k], WH[:, k], ALU.subtract).then_inc(lo_ready, 1)

            def lookup(h):
                for j in range(2):
                    pool.wait_ge(eq_ready, 2 * h + j + 1)
                    nc.gpsimd.tensor_tensor(EQ[:, j], EQ[:, j], bcast(IH[:, j], 2, TOPK), ALU.mult).then_inc(looked_up, 1)

            for i in range(3):
                low(i)
            with pool.Fori(0, HEADS - 3) as h:
                lookup(h)
                low(h + 3)
            for h in range(HEADS - 3, HEADS):
                lookup(h)

        @block.vector
        def _(dve):
            V = nc.vector
            V.memset(QT[:], 0.0)
            dve.drain().then_inc(cleared, 1)
            dve.sem_inc(sc_free, 2)
            dve.wait_ge(iota_ready, 1)

            def best16(values, indices, data):
                for r in range(2):
                    at = slice(8 * r, 8 * r + 8)
                    for t in range(NT):
                        V.max(values[t][:, at], data[t])
                    dve.drain()
                    for t in range(NT):
                        V.max_index(indices[t][:, at], values[t][:, at], data[t])
                    if r == 0:
                        for t in range(NT):
                            V.match_replace(data[t], values[t][:, at], data[t], NEG)
                        dve.drain()

            def chosen(h):
                for j in range(2):
                    dve.wait_ge(looked_up, 2 * h + j + 1)
                    V.tensor_reduce(EG[:, :, j, bass.ds(h * TOPK, TOPK)], EQ[:, j], AX.X, ALU.add)
                dve.drain()

            def head(h, par, before=None):
                for half in range(2):
                    dve.wait_ge(sc_ready, 2 * h + (half + 2))
                    dve.sem_inc(begun, 1)
                    best16([VV[:, half, t] for t in range(NT)], [II[:, half, t] for t in range(NT)],
                           [SC[:, par, half, t, :] for t in range(NT)])
                dve.drain().then_inc(sc_free, 1)
                if before is not None:
                    chosen(before)
                V.tensor_tensor(CA[:], bcast(VV[:, 0], 3, TOPK), bcast(VV[:, 1], 2, TOPK), ALU.add)
                V.tensor_copy(IF[:], II[:])
                dve.drain()
                best16([SH[:, t] for t in range(NT)], [SI[:, t] for t in range(NT)], [CA[:, t].rearrange("p a b -> p (a b)") for t in range(NT)])
                dve.drain()
                V.tensor_copy(SV[:, :, bass.ds(h, 1), :].rearrange("p t h k -> p t (h k)"), SH[:])
                V.tensor_scalar(PL[:, 0], SI[:], 4, None, ALU.logical_shift_right)
                V.tensor_scalar(PL[:, 1], SI[:], 15, None, ALU.bitwise_and)
                dve.drain()
                V.tensor_copy(HF[:], PL[:])
                V.tensor_copy(IH[:], IF[:])
                dve.drain()
                for j in range(2):
                    V.tensor_tensor(EQ[:, j], bcast(HF[:, j], 3, TOPK), bcast(bcast(IO16[:], 1, TOPK), 1, NT),
                                    ALU.is_equal).then_inc(eq_ready, 1)

            head(0, 0)
            with dve.Fori(0, HEADS // 2 - 1) as i:
                for par in range(2):
                    head(2 * i + par + 1, 1 - par, before=2 * i + par)
            head(HEADS - 1, 1, before=HEADS - 2)
            chosen(HEADS - 1)
            V.tensor_copy(SM1[:], SV[:, :, :, 0])
            dve.drain()
            V.tensor_tensor(SV[:], SV[:], bcast(SM1[:], 3, TOPK), ALU.subtract)
            dve.drain().then_inc(ex_in, 1)
            dve.wait_ge(ex_ready, 1)
            V.tensor_reduce(SM1[:], SV[:], AX.X, ALU.add)
            dve.drain()
            V.reciprocal(SM1[:], SM1[:])
            dve.drain()
            V.tensor_tensor(EG[:, :, 2, :].rearrange("p t (h k) -> p t h k", h=HEADS), SV[:], bcast(SM1[:], 3, TOPK),
                            ALU.mult)
            dve.drain().then_inc(eg_ready, 1)


def gate_tables(nc, io, g, stack):
    m = Mem(nc, stack, "gt")
    PS, RT = g["PS"], g["RT"]
    IOTA = m.sb("IOTA", [P, NK])
    BATCH = 4
    NBUF = 4
    OH = m.sb("OH", [P, NBUF, 2, BATCH, NK])
    STG = m.sb("STG", [P, 2, NG, 16, JG])
    (iota_ready, first_ready, second_ready, oh_ready, oh_free, tab_done, bank_free, stg_ready) = (m.sem(x) for x in (
        "iota_ready first_ready second_ready oh_ready oh_free tab_done bank_free stg_ready").split())
    stored = m.sems("stored", 2)

    with nc.Block() as block:
        @block.gpsimd
        def _(pool):
            nc.gpsimd.iota(IOTA[:], [[1, NK]], base=0, channel_multiplier=0,
                           allow_small_or_imprecise_dtypes=True).then_inc(iota_ready, 1)
            with pool.Fori(0, T // (NBUF * BATCH)) as i:
                for b in range(NBUF):
                    pool.wait_ge(first_ready, NBUF * i + b + 1)
                    gates = RT[:, 2, bass.ds(NBUF * BATCH * i + BATCH * b, BATCH)]
                    nc.gpsimd.tensor_tensor(OH[:, b, 0], OH[:, b, 0], bcast(gates, 2, NK), ALU.mult).then_inc(oh_ready, 1)

        @block.vector
        def _(dve):
            V = nc.vector
            dve.sem_inc(oh_free, NBUF)
            dve.wait_ge(iota_ready, 1)
            with dve.Fori(0, T // (NBUF * BATCH)) as i:
                for b in range(NBUF):
                    dve.wait_ge(oh_free, NBUF * i + b + 1)
                    at = bass.ds(NBUF * BATCH * i + BATCH * b, BATCH)
                    for key, done in ((0, first_ready), (1, second_ready)):
                        V.tensor_tensor(OH[:, b, key], bcast(IOTA[:], 1, BATCH), bcast(RT[:, key, at], 2, NK),
                                        ALU.is_equal).then_inc(done, 1)

        @block.tensor
        def _(pe):
            with pe.Fori(0, T // (NBUF * BATCH)) as i:
                for b in range(NBUF):
                    pe.wait_ge(bank_free, NBUF * i + b + 1)
                    pe.wait_ge(oh_ready, NBUF * i + b + 1)
                    pe.wait_ge(second_ready, NBUF * i + b + 1)
                    for q in range(BATCH):
                        mm = nc.tensor.matmul(PS[:, b, NK * q:NK * q + NK], OH[:, b, 0, q, :], OH[:, b, 1, q, :],
                                              start=True, stop=True)
                    mm.then_inc(tab_done, 1)

        @block.scalar
        def _(act):
            A = nc.scalar.activation
            act.sem_inc(bank_free, NBUF)

            def sixteen(i, half, first=False):
                if not first:
                    act.wait_ge(stored[half], 16 * i)
                for b in range(4):
                    act.wait_ge(tab_done, 8 * i + (4 * half + b + 1))
                    A(STG[:, half].rearrange("p g t j -> p t g j")[:, BATCH * b:BATCH * b + BATCH],
                      PS[:, b, :].rearrange("p (t g j) -> p t g j", t=BATCH, g=NG), ACT.Copy).then_inc(bank_free, 1)
                    act.sem_inc(oh_free, 1)
                act.drain().then_inc(stg_ready, 1)

            for half in range(2):
                sixteen(0, half, first=True)
            with act.Fori(1, T // 32) as i:
                for half in range(2):
                    sixteen(i, half)

        @block.sync
        def _(sp):
            gd = io["gd"].rearrange("g p t j -> p g t j")
            with sp.Fori(0, T // 32) as i:
                for half in range(2):
                    sp.wait_ge(stg_ready, 2 * i + half + 1)
                    sp.dma_start(gd[:, :, bass.ds(32 * i + 16 * half, 16), :].rearrange("p g t j -> p g (t j)"),
                                 STG[:, half].rearrange("p g t j -> p g (t j)")).then_inc(stored[half], 16)
            for half in range(2):
                sp.wait_ge(stored[half], 16 * (T // 32))


def phase_experts(nc, io, g, stack):
    m = Mem(nc, stack, "ex")
    PS, YA, HH, HL, WR, WH, WL = (g[x] for x in ("PS", "YA", "HH", "HL", "WR", "WH", "WL"))
    GG = m.sb("GG", [P, T, JG])
    BH = m.sb("BH", [P, HG, T])
    BL = m.sb("BL", [P, HG, T])
    GE = m.sb("GE", [P, 2, T])
    w_in, w_base = g["W_IN"], 2 * 8 * KT
    (g_in, hi_ready, lo_ready, used, ge_ready, ge_free, ge_used, hb_ready, ya_ready, gg_free,
     bank_free) = (m.sem(x) for x in (
        "g_in hi_ready lo_ready used ge_ready ge_free ge_used hb_ready ya_ready gg_free "
        "bank_free").split())
    PER = 16
    IS_U = [(n // HG) % 2 == 0 for n in range(PER)]

    def source(gi, n):
        hh, k = n // 8, n % 4
        return io["peer_u"][8 * gi + (4 * hh + k)] if IS_U[n] else io["peer_v"][gi, 4 * hh + k]

    with nc.Block() as block:
        @block.sync
        def _(sp):
            def group(gi, last=False):
                for n in range(PER):
                    if last and n >= PER - 2:
                        break
                    sp.wait_ge(lo_ready, PER * gi + (n + 1))
                    src = source(gi, n + 2) if n < PER - 2 else source(gi + 1, n + 2 - PER)
                    sp.dma_start(WR[:, n % 2, :], src).then_inc(w_in[n % 2], 16)
                    if n == 14 and not last:
                        sp.wait_ge(gg_free, gi + 1)
                        sp.dma_start(GG[:], io["gd"][gi + 1]).then_inc(g_in, 16)

            sp.dma_start(GG[:], io["gd"][0]).then_inc(g_in, 16)
            with sp.Fori(0, NG - 1) as gi:
                group(gi)
            group(NG - 1, last=True)

        @block.tensor
        def _(pe):
            def u_tile(gi, n):
                b = 2 * (n % 2)
                pe.wait_ge(ge_free, 8 * gi + (4 * (n // 8) + n % 4 + 1))
                pe.wait_ge(lo_ready, PER * gi + (n + 1))
                for half in range(2):
                    cols = slice(TH * half, TH * half + TH)
                    for kt in range(KT):
                        at = slice(P * kt, P * kt + P)
                        mm = product(nc, PS[:, b + half, 0:TH], WH[:, n % 2, at], WL[:, n % 2, at],
                                     HH[:, kt, cols], HL[:, kt, cols], kt == 0, kt == KT - 1)
                mm.then_inc(used, 1)

            def v_part(n, ct, js):
                for half in range(2):
                    cols = slice(TH * half, TH * half + TH)
                    for j in js:
                        at = slice(4 * P * j + P * ct, 4 * P * j + P * ct + P)
                        mm = product(nc, PS[:, 4 + 2 * (ct % 2) + half, 0:TH], WH[:, n % 2, at], WL[:, n % 2, at],
                                     BH[:, j, cols], BL[:, j, cols], j == 0, j == HG - 1)
                return mm

            def v_tile(gi, n):
                first = n % 4 == 0
                base = 32 * gi + 16 * (n // 8) + 4 * (n % 4)
                pe.wait_ge(lo_ready, PER * gi + (n + 1))
                for ct in range(4):
                    pe.wait_ge(bank_free, base + ct + 1)
                    if first and ct == 0:
                        pe.wait_ge(hb_ready, 8 * gi + (4 * (n // 8) + HG - 1))
                        v_part(n, 0, range(HG - 1))
                        pe.wait_ge(bank_free, base + 2)
                        v_part(n, 1, range(HG - 1))
                        pe.wait_ge(hb_ready, 8 * gi + (4 * (n // 8) + HG))
                    mm = v_part(n, ct, range(HG - 1, HG) if first and ct < 2 else range(HG))
                    mm.then_inc(ya_ready if ct < 3 else used, 1)

            with pe.Fori(0, NG) as gi:
                for n in range(PER):
                    (u_tile if IS_U[n] else v_tile)(gi, n)

        @block.scalar
        def _(act):
            A = nc.scalar.activation
            act.sem_inc(ge_free, 2)

            def high(gi, n, slot, peeled=False):
                act.wait_ge(w_in[slot % 2], 128 * gi + (w_base + 16 * (n // 2) + 16))
                if not peeled:
                    act.wait_ge(used, PER * gi + (n - 1))
                A(r32(WH[:, slot % 2]), WR[:, slot % 2], ACT.Copy).then_inc(hi_ready, 1)

            def group(gi, last=False):
                for n in range(PER):
                    if IS_U[n]:
                        k = 4 * (n // 8) + n % 4
                        act.wait_ge(used, PER * gi + (n + 1))
                        act.wait_ge(ge_used, 8 * gi + (k + 1))
                        A(GE[:, n % 2].rearrange("p (h n) -> p h n", h=2),
                          PS[:, 2 * (n % 2):2 * (n % 2) + 2, 0:TH], ACT.Gelu_apprx_tanh).then_inc(ge_ready, 1)
                        act.drain().then_inc(ge_free, 1)
                    if not (last and n >= PER - 2):
                        high(gi, n + 2, n + 2)

            high(0, 0, 0, peeled=True)
            high(0, 1, 1, peeled=True)
            with act.Fori(0, NG - 1) as gi:
                group(gi)
            group(NG - 1, last=True)

        @block.vector
        def _(dve):
            V = nc.vector
            dve.sem_inc(bank_free, 2)
            dve.sem_inc(ge_used, 2)
            dve.drain()

            def low(gi, n):
                dve.wait_ge(hi_ready, PER * gi + (n + 1))
                V.tensor_tensor(r32(WL[:, n % 2]), WR[:, n % 2], WH[:, n % 2], ALU.subtract).then_inc(lo_ready, 1)

            def group(gi, last=False):
                for n in range(PER):
                    k = 4 * (n // 8) + n % 4
                    if IS_U[n]:
                        if n == 0:
                            dve.wait_ge(g_in, 16 * gi + 16)
                        ge = GE[:, n % 2]
                        dve.wait_ge(ge_ready, 8 * gi + (k + 1))
                        V.tensor_tensor(ge, ge, GG[:, :, k], ALU.mult)
                        dve.drain()
                        V.tensor_copy(r32(BH[:, n % 4]), ge)
                        dve.drain()
                        V.tensor_tensor(r32(BL[:, n % 4]), ge, BH[:, n % 4], ALU.subtract).then_inc(hb_ready, 1)
                        dve.drain().then_inc(ge_used, 1)
                        if k == 7:
                            dve.sem_inc(gg_free, 1)
                    else:
                        for ct in range(4):
                            if ct < 3:
                                dve.wait_ge(ya_ready, 24 * gi + (12 * (n // 8) + 3 * (n % 4) + ct + 1))
                            else:
                                dve.wait_ge(used, PER * gi + (n + 1))
                            y = YA[:, 4 * (n % 4) + ct, :].rearrange("p (h n) -> p h n", h=2)
                            V.tensor_tensor(y, y, PS[:, 4 + 2 * (ct % 2):6 + 2 * (ct % 2), 0:TH],
                                            ALU.add).then_inc(bank_free, 1)
                    if not (last and n >= PER - 2):
                        low(gi, n + 2)

            low(0, 0)
            low(0, 1)
            V.memset(YA[:], 0.0)
            dve.drain()
            with dve.Fori(0, NG - 1) as gi:
                group(gi)
            group(NG - 1, last=True)


def phase_final(nc, io, g, stack):
    m = Mem(nc, stack, "fin")
    MOD, XT, YA = g["MOD"], g["XT"], g["YA"]
    norm = Norm(nc, m, g, XT, "ln2_w", "ln2_b")
    x_ready, y_out = m.sem("x_ready"), m.sem("y_out")
    x_in = m.sems("x_in", 4)

    with nc.Block() as block:
        @block.tensor
        def _(pe):
            pe.wait_ge(norm.ones_ready, 1)
            for kt in range(KT):
                norm.mean(pe, x_ready, kt, first=(kt == 0), last=(kt == KT - 1))
            norm.variance(pe)

        @block.scalar
        def _(act):
            norm.scalar(act)

        @block.vector
        def _(dve):
            V = nc.vector
            norm.start(dve)
            for kt in range(KT):
                V.tensor_scalar(YA[:, kt, 0:SEQ], YA[:, kt, 0:SEQ], MOD[:, 5 * KT + kt, 0:1], None, ALU.mult)
            ys = YA[:, :, SEQ:T].rearrange("p k (b s) -> p k b s", s=NS)
            V.tensor_tensor(ys, ys, bcast(MOD[:, 5 * KT:6 * KT, 1:9], 3, NS), ALU.mult)
            dve.drain()
            for kt in range(KT):
                if kt % 4 == 0:
                    dve.wait_ge(x_in[kt // 4], 16)
                V.scalar_tensor_tensor(XT[:, kt, :], XT[:, kt, :], ALPHA, YA[:, kt, :], ALU.mult, ALU.add)\
                    .then_inc(x_ready, 1)
            dve.drain()
            norm.vector(dve)

        @block.sync
        def _(sp):
            for q in range(4):
                sp.dma_start(XT[:, 4 * q:4 * q + 4, :], io["x1"][:, 4 * q:4 * q + 4, :]).then_inc(x_in[q], 16)
            for q in range(4):
                sp.wait_ge(norm.normed, 4 * q + 4)
                sp.dma_start(io["y"][:, 4 * q:4 * q + 4, :], XT[:, 4 * q:4 * q + 4, :]).then_inc(y_out, 16)
            sp.wait_ge(y_out, 64)


def phase_rest(nc, io, g):
    with ExitStack() as tail:
        m = Mem(nc, tail, "tail")
        g.update({
            "HH": m.sb("HH", [P, KT, T]), "HL": m.sb("HL", [P, KT, T]),
            "WR": m.sb("WR", [P, 2, D]), "WH": m.sb("WH", [P, 2, D]), "WL": m.sb("WL", [P, 2, D]),
        })
        g["W_IN"] = m.sems("w_in", 2)
        with ExitStack() as first:
            g["XT"] = Mem(nc, first, "first").sb("XT", [P, KT, T])
            run(phase_out, nc, io, g)
            run(phase_route, nc, io, g)
        g["YA"] = Mem(nc, tail, "last").sb("YA", [P, KT, T])
        run(phase_experts, nc, io, g)
        g["XT"] = Mem(nc, tail, "last").sb("XT", [P, KT, T])
        run(phase_final, nc, io, g)


def program(nc, io):
    with ExitStack() as top:
        m = Mem(nc, top, "all")
        g = {
            "PS": top.enter_context(nc.psum_tensor("PS", [P, 8, 512], F32)),
            "MOD": m.sb("MOD", [P, ADA, 9]),
            "PARAM": m.sb("PARAM", [P, NPAR]),
            "IDENT": m.sb("IDENT", [P, P]),
            "EPSG": m.sb("EPSG", [P, 2]),
        }
        with ExitStack() as mixer:
            mx = Mem(nc, mixer, "mix")
            g.update({
                "RING": mx.sb("RING", [P, 4, D]), "HT": mx.sb("HT", [P, KT, TP]),
                "CS": mx.sb("CS", [P, KT, 9]), "BADA": mx.sb("BADA", [P, ADA]),
                "LR": mx.sb("LR", [P, 2, W1]), "BD": mx.sb("BD", [P, P]), "MASK": mx.sb("MASK", [P, 4, P]),
                "LM": mx.sb("LM", [P, 5, P]), "SM": mx.sb("SM", [P, W1]), "SP8": mx.sb("SP8", [P, 2, 8]),
            })
            run(phase_ada, nc, io, g)
            run(phase_lru, nc, io, g)
            run(phase_rwkv, nc, io, g)
        phase_rest(nc, io, g)


INPUTS = {
    "xT": (P, KT, T), "cT": (P, KT, 9), "shiftT": (P, KT, NB), "w_ada": (ADA, P, D), "b_ada": (P, ADA),
    "par": (P, NPAR), "w_in": (42, P, D), "w_gate": (8, P, 2, 64), "lru0": (P, 8, 8), "conv0": (P, 8, 24),
    "w_lr": (8, P, 2, P), "wkv0": (8, P, NB, 64), "w_out": (KT, P, D), "w_q": (KT, P, D), "keys": (P, 2, NK),
    "peer_u": (NK, P, D), "peer_v": (NG, 8, P, D),
}
OUTPUTS = {
    "y": (P, KT, T), "shift_out": (P, KT, 9), "wkv_p": (8, P, 64), "wkv_s": (8, P, NB, 64), "lru_out": (P, 8, 9),
    "conv_out": (P, 8, 27),
}
SCRATCH = {"mix": (KT, P, T), "x1": (P, KT, T), "gd": (NG, P, T, JG)}


def laid_out(i):
    import numpy as np

    def cols(v):
        return v.reshape(-1, P).T

    def tiles(w):
        k, c = w.shape
        return w.reshape(k // P, P, c // P, P).transpose(2, 1, 0, 3).reshape(c // P, P, -1)

    def chan(x):
        return x.T.reshape(-1, P, x.shape[0]).transpose(1, 0, 2)

    x = np.concatenate([i["x_prompt"][0], i["x_sample"].reshape(NB * NS, D)])
    c = np.concatenate([i["c_prompt"], i["c_sample"]])
    par = np.concatenate([cols(i[n][0].reshape(-1)) for n in (
        "mu_shift", "w0", "a0", "k_k", "k_a", "r_k", "lnx_w", "lnx_b", "conv_w", "conv_b", "b_gate_a", "b_gate_i",
        "lru_lambda", "ln1_w", "ln1_b", "ln2_w", "ln2_b")], axis=1)
    out = {
        "xT": chan(x), "cT": chan(c), "shiftT": chan(i["state_shift"][0]), "w_ada": tiles(i["w_ada"][0]),
        "b_ada": cols(i["b_ada"][0]), "par": par, "w_in": tiles(i["w_in"][0]),
        "w_gate": np.stack([i["w_gate_a"][0].reshape(8, P, 64), i["w_gate_i"][0].reshape(8, P, 64)], axis=2),
        "lru0": chan(i["state_lru"][0]),
        "conv0": chan(i["state_conv"][0].reshape(NB * 3, DA)),
        "w_lr": np.stack([np.concatenate([i["w_w2"][0], i["w_a2"][0]]).reshape(P, 8, P),
                          i["w_g2"][0].reshape(P, 8, P)], axis=2).transpose(1, 0, 2, 3),
        "wkv0": i["state_wkv"][0].transpose(1, 3, 0, 2).reshape(8, P, NB, 64),
        "w_out": tiles(i["w_out"][0]), "w_q": tiles(i["w_q"][0]),
        "keys": i["sub_keys"][0].transpose(2, 0, 1),
        "peer_u": i["peer_u"][0].reshape(P, NK, KT, P).transpose(1, 3, 2, 0).reshape(NK, P, D),
        "peer_v": i["peer_v"][0].reshape(P, NG, 2, HG, 4, 4 * P).transpose(1, 2, 4, 0, 3, 5).reshape(NG, 8, P, D),
    }
    return {k: np.ascontiguousarray(v) for k, v in out.items()}


def gathered(o):
    def rows(x):
        return x.transpose(2, 1, 0).reshape(x.shape[2], -1)

    y, sh = rows(o["y"]), rows(o["shift_out"])
    lru, conv = rows(o["lru_out"]), rows(o["conv_out"]).reshape(9, 3, DA)
    wp = o["wkv_p"].reshape(16, 64, 64).transpose(0, 2, 1)
    ws = o["wkv_s"].reshape(16, 64, NB, 64).transpose(2, 0, 3, 1)
    return (y[None, :SEQ], y[SEQ:].reshape(NB, NS, D), sh[None, :1], wp[None, None], lru[None, :1], conv[None, :1],
            sh[None, 1:], ws[None], lru[None, 1:], conv[None, 1:])


def kernel(**inputs):
    import numpy as np
    import concourse.bacc as bacc
    from concourse.bass_utils import run_bass_kernel_spmd

    arrays = {f"in_{k}": v for k, v in laid_out({k: np.asarray(v) for k, v in inputs.items()}).items()}
    nc = bacc.Bacc("TRN2", target_bir_lowering=False, num_devices=1)
    io = {k: nc.dram_tensor(f"in_{k}", s, F32, kind="ExternalInput").ap() for k, s in INPUTS.items()}
    io.update({k: nc.dram_tensor(f"out_{k}", s, F32, kind="ExternalOutput").ap() for k, s in OUTPUTS.items()})
    io.update({k: nc.dram_tensor(f"tmp_{k}", s, F32).ap() for k, s in SCRATCH.items()})
    program(nc, io)
    r = run_bass_kernel_spmd(nc, [arrays], core_ids=[0]).results[0]
    return tuple(np.ascontiguousarray(x) for x in gathered({k: np.asarray(r[f"out_{k}"]) for k in OUTPUTS}))
```
